# Optimizing a Trainium2 kernel written in Bass

```python
import jax, jax.numpy as jnp
from jax import lax
import numpy as np

D_MODEL = 2048
BATCH = 1
SEQ = 256
DEPTH = 2

GRID_W = 64
CTX_LEN = 256

D_MLSTM = D_MODEL // 2
N_MLSTM_HEADS = 4
MLSTM_HEAD_DIM = D_MLSTM // N_MLSTM_HEADS
MLSTM_CHUNK = 64
QK_CONV = 3
N_DIR = 2
D_POOL = D_MODEL - D_MLSTM
POOL_WINDOWS = (2, 4, 8, 16)
N_POOL_GROUPS = len(POOL_WINDOWS)
POOL_GROUP_DIM = D_POOL // N_POOL_GROUPS
N_GATE = 2 * N_DIR * N_MLSTM_HEADS
N_IN_EVEN = 5 * D_MLSTM + N_GATE + 2 * D_POOL
EVEN_SPLITS = (D_MLSTM, 2 * D_MLSTM, 3 * D_MLSTM, 4 * D_MLSTM, 5 * D_MLSTM,
               5 * D_MLSTM + N_GATE, 5 * D_MLSTM + N_GATE + D_POOL)
D_SGU = D_MODEL
N_SGU_HEADS = 8
SGU_HEAD_DIM = D_SGU // N_SGU_HEADS
SGU_CHUNK = 128
N_IN_ODD = 3 * D_SGU

N_EVEN = (DEPTH + 1) // 2
N_ODD = DEPTH // 2
DEEPNORM_ALPHA = (2.0 * DEPTH) ** 0.25
DEEPNORM_BETA = (8.0 * DEPTH) ** -0.25
LN_EPS = 1e-5


def _normalize(x):
    xf = x.astype(jnp.float32)
    mu = xf.mean(-1, keepdims=True)
    var = jnp.square(xf - mu).mean(-1, keepdims=True)
    return (xf - mu) * lax.rsqrt(var + LN_EPS)

def layer_norm(x, g, b):
    return (_normalize(x) * g + b).astype(x.dtype)

def ada_params(cond, w, b):
    mod = jax.nn.silu(cond) @ w + b
    return jnp.split(mod, 3, axis=-1)

def dwconv_centered(x, w):
    k, ch = w.shape
    return lax.conv_general_dilated(x, w[:, None, :].astype(x.dtype), window_strides=(1,),
                                    padding=[(k // 2, k // 2)],
                                    dimension_numbers=('NWC', 'WIO', 'NWC'),
                                    feature_group_count=ch)

def mlstm_scan(q, k, v, log_i, log_f, state):
    bsz, nh, seqlen, dh = q.shape
    nc = seqlen // MLSTM_CHUNK

    def to_chunks(a):
        a = a.astype(jnp.float32).reshape(bsz, nh, nc, MLSTM_CHUNK, *a.shape[3:])
        return jnp.moveaxis(a, 2, 0)

    lower = jnp.tril(jnp.ones((MLSTM_CHUNK, MLSTM_CHUNK), bool))

    def step(carry, inp):
        cmat, nvec, m = carry
        qc, kc, vc, ic, fc = inp
        b = jnp.cumsum(fc, axis=-1)
        d = b[..., :, None] - b[..., None, :] + ic[..., None, :]
        d = jnp.where(lower, d, -jnp.inf)
        inter = b + m[..., None]
        m_t = jnp.maximum(d.max(-1), inter)
        w_intra = jnp.exp(d - m_t[..., None])
        w_inter = jnp.exp(inter - m_t)
        s = jnp.einsum('bhtd,bhsd->bhts', qc, kc) * w_intra
        num = (jnp.einsum('bhts,bhsd->bhtd', s, vc)
               + w_inter[..., None] * jnp.einsum('bhvk,bhtk->bhtv', cmat, qc))
        den = s.sum(-1) + w_inter * jnp.einsum('bhk,bhtk->bht', nvec, qc)
        h = num / jnp.maximum(jnp.abs(den), jnp.exp(-m_t))[..., None]
        b_last = b[..., -1]
        g = b_last[..., None] - b + ic
        m_new = jnp.maximum(b_last + m, g.max(-1))
        w_s = jnp.exp(g - m_new[..., None])
        decay = jnp.exp(b_last + m - m_new)
        c_new = decay[..., None, None] * cmat + jnp.einsum('bhs,bhsv,bhsk->bhvk', w_s, vc, kc)
        n_new = decay[..., None] * nvec + jnp.einsum('bhs,bhsk->bhk', w_s, kc)
        return (c_new, n_new, m_new), h

    xs = tuple(to_chunks(a) for a in (q, k, v, log_i, log_f))
    state, h = lax.scan(step, state, xs)
    h = jnp.moveaxis(h, 0, 2).reshape(bsz, nh, seqlen, dh)
    return h, state

def zero_mlstm_state(bsz):
    return (jnp.zeros((bsz, N_MLSTM_HEADS, MLSTM_HEAD_DIM, MLSTM_HEAD_DIM), jnp.float32),
            jnp.zeros((bsz, N_MLSTM_HEADS, MLSTM_HEAD_DIM), jnp.float32),
            jnp.zeros((bsz, N_MLSTM_HEADS), jnp.float32))

def even_proj(xm, w_in, conv_qk, b_igate, b_fgate):
    bsz, seqlen, _ = xm.shape
    proj = xm @ w_in
    q, k, v, o, z_m, gates, u_p, z_p = jnp.split(proj, EVEN_SPLITS, axis=-1)
    qk = jax.nn.silu(dwconv_centered(jnp.concatenate([q, k], -1), conv_qk))
    q, k = jnp.split(qk, 2, axis=-1)

    def heads(a):
        return a.reshape(bsz, seqlen, N_MLSTM_HEADS, MLSTM_HEAD_DIM).transpose(0, 2, 1, 3)

    q, k, v = heads(q), heads(k) * (MLSTM_HEAD_DIM ** -0.5), heads(v)
    gates = gates.astype(jnp.float32).reshape(bsz, seqlen, 2, N_DIR, N_MLSTM_HEADS)
    log_i = (gates[:, :, 0] + b_igate).transpose(2, 0, 3, 1)
    log_f = jax.nn.log_sigmoid(gates[:, :, 1] + b_fgate).transpose(2, 0, 3, 1)
    return q, k, v, o, z_m, log_i, log_f, u_p, z_p

def multiscale_pool(u, row_len):
    bsz, seqlen, _ = u.shape
    rows = seqlen // row_len
    ug = u.astype(jnp.float32).reshape(bsz, rows, row_len, N_POOL_GROUPS, POOL_GROUP_DIM)
    cs = jnp.pad(jnp.cumsum(ug, axis=2), ((0, 0), (0, 0), (1, 0), (0, 0), (0, 0)))
    pos = jnp.arange(row_len)
    outs = []
    for g, w in enumerate(POOL_WINDOWS):
        lo = jnp.maximum(pos - w // 2, 0)
        hi = jnp.minimum(pos + (w - 1 - w // 2), row_len - 1)
        csg = cs[:, :, :, g, :]
        s = jnp.take(csg, hi + 1, axis=2) - jnp.take(csg, lo, axis=2)
        outs.append(s / (hi - lo + 1).astype(jnp.float32)[:, None])
    pooled = jnp.stack(outs, axis=3)
    return (pooled - ug).reshape(bsz, seqlen, N_POOL_GROUPS, POOL_GROUP_DIM)

def even_out(h, o, z_m, u_p, z_p, row_len, mh_norm_g, pool_w, pool_scale):
    bsz, nh, seqlen, dh = h.shape
    h = jnp.moveaxis(h, 1, 2) * jax.nn.sigmoid(o.astype(jnp.float32)).reshape(bsz, seqlen, nh, dh)
    h = _normalize(h).reshape(bsz, seqlen, D_MLSTM) * mh_norm_g
    y_m = h * jax.nn.silu(z_m.astype(jnp.float32))
    r = multiscale_pool(u_p, row_len)
    y_p = jnp.einsum('blgc,gcd->blgd', r, pool_w.astype(jnp.float32)).reshape(bsz, seqlen, D_POOL)
    y_p = y_p * pool_scale * jax.nn.silu(z_p.astype(jnp.float32))
    return jnp.concatenate([y_m, y_p], axis=-1).astype(u_p.dtype)

def sgu_mixer(xm, w_in, ln_g, ln_b, w_sp, b_sp):
    bsz, seqlen, _ = xm.shape
    u, v, z = jnp.split(xm @ w_in, 3, axis=-1)
    v = layer_norm(v, ln_g, ln_b)
    nc = seqlen // SGU_CHUNK
    vh = v.reshape(bsz, nc, SGU_CHUNK, N_SGU_HEADS, SGU_HEAD_DIM)
    s = jnp.einsum('hts,bnshc->bnthc', w_sp, vh) + b_sp.T[None, None, :, :, None]
    return u * s.reshape(bsz, seqlen, D_SGU) * jax.nn.silu(z)

def first_inputs(seed: int = 0) -> dict:
    key = jax.random.key(seed)
    ks = jax.random.split(key, 24)

    def nrm(k, shape, s):
        return jax.random.normal(k, shape, jnp.float32) * s

    d = D_MODEL
    fgate_base = jnp.linspace(3.0, 6.0, N_MLSTM_HEADS, dtype=jnp.float32)
    return {
        "x": nrm(ks[0], (BATCH, SEQ, d), 1.0),
        "c": nrm(ks[1], (BATCH, d), 1.0),
        "ctx": nrm(ks[2], (BATCH, CTX_LEN, d), 1.0),
        "c_ctx": nrm(ks[3], (d,), 1.0),
        "ada_w": nrm(ks[4], (DEPTH, d, 3 * d), 0.5 * d ** -0.5),
        "ada_b": nrm(ks[5], (DEPTH, 3 * d), 0.02),
        "post_ln_g": 1.0 + nrm(ks[6], (DEPTH, d), 0.05),
        "post_ln_b": nrm(ks[7], (DEPTH, d), 0.02),
        "w_in_even": nrm(ks[8], (N_EVEN, d, N_IN_EVEN), d ** -0.5),
        "conv_qk": nrm(ks[9], (N_EVEN, QK_CONV, 2 * D_MLSTM), QK_CONV ** -0.5),
        "b_igate": nrm(ks[10], (N_EVEN, N_DIR, N_MLSTM_HEADS), 0.1),
        "b_fgate": fgate_base + nrm(ks[11], (N_EVEN, N_DIR, N_MLSTM_HEADS), 0.1),
        "mh_norm_g": 1.0 + nrm(ks[12], (N_EVEN, D_MLSTM), 0.05),
        "pool_w": nrm(ks[13], (N_EVEN, N_POOL_GROUPS, POOL_GROUP_DIM, POOL_GROUP_DIM), POOL_GROUP_DIM ** -0.5),
        "pool_scale": 1.0 + nrm(ks[14], (N_EVEN, D_POOL), 0.1),
        "w_out_even": nrm(ks[15], (N_EVEN, D_MLSTM + D_POOL, d), DEEPNORM_BETA * (D_MLSTM + D_POOL) ** -0.5),
        "w_in_odd": nrm(ks[16], (N_ODD, d, N_IN_ODD), d ** -0.5),
        "sgu_ln_g": 1.0 + nrm(ks[17], (N_ODD, D_SGU), 0.05),
        "sgu_ln_b": nrm(ks[18], (N_ODD, D_SGU), 0.02),
        "w_sp": nrm(ks[19], (N_ODD, N_SGU_HEADS, SGU_CHUNK, SGU_CHUNK), SGU_CHUNK ** -0.5),
        "b_sp": 1.0 + nrm(ks[20], (N_ODD, N_SGU_HEADS, SGU_CHUNK), 0.1),
        "w_out_odd": nrm(ks[21], (N_ODD, D_SGU, d), DEEPNORM_BETA * D_SGU ** -0.5),
    }

def first_block(x, c, ctx, c_ctx, ada_w, ada_b, post_ln_g, post_ln_b, w_in_even, conv_qk, b_igate,
              b_fgate, mh_norm_g, pool_w, pool_scale, w_out_even, w_in_odd, sgu_ln_g, sgu_ln_b,
              w_sp, b_sp, w_out_odd):
    x_lat, x_ctx = x, ctx
    bsz = x.shape[0]
    for layer in range(DEPTH):
        last = layer == DEPTH - 1
        j = layer // 2
        sh_l, sc_l, g_l = ada_params(c, ada_w[layer], ada_b[layer])
        sh_l, sc_l, g_l = sh_l[:, None], sc_l[:, None], g_l[:, None]
        sh_c, sc_c, g_c = ada_params(c_ctx, ada_w[layer], ada_b[layer])
        xm_l = x_lat * (1.0 + sc_l) + sh_l
        xm_c = x_ctx * (1.0 + sc_c) + sh_c
        if layer % 2 == 0:
            ql, kl, vl, ol, zml, lil, lfl, upl, zpl = even_proj(xm_l, w_in_even[j], conv_qk[j], b_igate[j], b_fgate[j])
            qc, kc, vc, oc, zmc, lic, lfc, upc, zpc = even_proj(xm_c, w_in_even[j], conv_qk[j], b_igate[j], b_fgate[j])
            flip = lambda a: jnp.flip(a, axis=2)
            zero = zero_mlstm_state(bsz)
            hc_f, st_f = mlstm_scan(qc, kc, vc, lic[0], lfc[0], zero)
            hl_f, _ = mlstm_scan(ql, kl, vl, lil[0], lfl[0], st_f)
            hc_b, st_b = mlstm_scan(flip(qc), flip(kc), flip(vc), flip(lic[1]), flip(lfc[1]), zero)
            hl_b, _ = mlstm_scan(flip(ql), flip(kl), flip(vl), flip(lil[1]), flip(lfl[1]), st_b)
            y_l = even_out(hl_f + flip(hl_b), ol, zml, upl, zpl, GRID_W, mh_norm_g[j], pool_w[j], pool_scale[j])
            x_lat_new = layer_norm(DEEPNORM_ALPHA * x_lat + g_l * (y_l @ w_out_even[j]), post_ln_g[layer], post_ln_b[layer])
            if not last:
                y_c = even_out(hc_f + flip(hc_b), oc, zmc, upc, zpc, x_ctx.shape[1], mh_norm_g[j], pool_w[j], pool_scale[j])
                x_ctx = layer_norm(DEEPNORM_ALPHA * x_ctx + g_c * (y_c @ w_out_even[j]), post_ln_g[layer], post_ln_b[layer])
            x_lat = x_lat_new
        else:
            y_l = sgu_mixer(xm_l, w_in_odd[j], sgu_ln_g[j], sgu_ln_b[j], w_sp[j], b_sp[j])
            x_lat = layer_norm(DEEPNORM_ALPHA * x_lat + g_l * (y_l @ w_out_odd[j]), post_ln_g[layer], post_ln_b[layer])
            if not last:
                y_c = sgu_mixer(xm_c, w_in_odd[j], sgu_ln_g[j], sgu_ln_b[j], w_sp[j], b_sp[j])
                x_ctx = layer_norm(DEEPNORM_ALPHA * x_ctx + g_c * (y_c @ w_out_odd[j]), post_ln_g[layer], post_ln_b[layer])
    return x_lat


DEPTH_2 = 1

PLE_DIM = 256
RMS_EPS = 1e-6
N_HEADS = 16
QK_NOPE_DIM = 128
QK_ROPE_DIM = 64
V_HEAD_DIM = 128
QK_HEAD_DIM = QK_NOPE_DIM + QK_ROPE_DIM
Q_LORA_RANK = 768
KV_LORA_RANK = 512
ROPE_THETA = 10000.0
Q_BLOCK = 128
D_RNN = D_MODEL
RNN_BLOCKS = 16
RNN_BLOCK_DIM = D_RNN // RNN_BLOCKS
CONV_WIDTH = 4
LRU_C = 8.0
PEER_HEADS = 8
N_KEYS = 128
N_EXPERTS = N_KEYS * N_KEYS
PEER_QUERY_DIM = 256
PEER_HALF = PEER_QUERY_DIM // 2
PEER_TOPK = 16
PEER_CHUNK = 128
IN_SPLITS = (Q_LORA_RANK, KV_LORA_RANK, QK_ROPE_DIM, D_RNN, D_RNN, D_MODEL, D_MODEL)
IN_WIDTH = Q_LORA_RANK + KV_LORA_RANK + QK_ROPE_DIM + 2 * D_RNN + 2 * D_MODEL


def rms_norm(x, g):
    xf = x.astype(jnp.float32)
    y = xf * lax.rsqrt(jnp.mean(xf * xf, axis=-1, keepdims=True) + RMS_EPS)
    return (y * g.astype(jnp.float32)).astype(x.dtype)

def rope(x, pos):
    half = QK_ROPE_DIM // 2
    inv_freq = 1.0 / (ROPE_THETA ** (jnp.arange(half, dtype=jnp.float32) / half))
    ang = pos.astype(jnp.float32)[:, None] * inv_freq[None, :]
    cos = jnp.cos(ang)[:, None, :]
    sin = jnp.sin(ang)[:, None, :]
    xf = x.astype(jnp.float32)
    x1, x2 = xf[..., :half], xf[..., half:]
    return jnp.concatenate([x1 * cos - x2 * sin, x2 * cos + x1 * sin], axis=-1).astype(x.dtype)

def split_columns(z):
    offs, acc = [], 0
    for w in IN_SPLITS[:-1]:
        acc += w
        offs.append(acc)
    return jnp.split(z, offs, axis=-1)

def mla_branch(c_q, c_kv, k_r, q_norm, w_uq, kv_norm, w_ukv, w_attn_o):
    B, S, _ = c_q.shape
    pos = jnp.arange(S)
    q = (rms_norm(c_q, q_norm) @ w_uq).reshape(B, S, N_HEADS, QK_HEAD_DIM)
    q_nope = q[..., :QK_NOPE_DIM]
    q_pe = rope(q[..., QK_NOPE_DIM:], pos)
    kv = (rms_norm(c_kv, kv_norm) @ w_ukv).reshape(B, S, N_HEADS, QK_NOPE_DIM + V_HEAD_DIM)
    k_nope, v = kv[..., :QK_NOPE_DIM], kv[..., QK_NOPE_DIM:]
    k_pe = rope(k_r[:, :, None, :], pos)[:, :, 0, :]
    scale = QK_HEAD_DIM ** -0.5
    n_blk = S // Q_BLOCK

    def to_blocks(t):
        return t.reshape(B, n_blk, Q_BLOCK, *t.shape[2:]).swapaxes(0, 1)

    def attend(args):
        qn, qp, blk = args
        s = (jnp.einsum('bqhd,bkhd->bhqk', qn, k_nope, preferred_element_type=jnp.float32)
             + jnp.einsum('bqhd,bkd->bhqk', qp, k_pe, preferred_element_type=jnp.float32))
        q_pos = blk * Q_BLOCK + jnp.arange(Q_BLOCK)
        s = jnp.where(pos[None, :] <= q_pos[:, None], s * scale, -jnp.inf)
        prob = jax.nn.softmax(s, axis=-1)
        return jnp.einsum('bhqk,bkhd->bqhd', prob.astype(v.dtype), v)

    o = lax.map(attend, (to_blocks(q_nope), to_blocks(q_pe), jnp.arange(n_blk)))
    o = o.swapaxes(0, 1).reshape(B, S, N_HEADS * V_HEAD_DIM)
    return o @ w_attn_o

def rglru_branch(x_r, y_r, conv_w, conv_b, w_rg_a, b_rg_a, w_rg_x, b_rg_x, lru_lambda, w_rnn_o):
    B, S, C = x_r.shape
    xc = lax.conv_general_dilated(x_r, conv_w[:, None, :], window_strides=(1,),
                                  padding=[(CONV_WIDTH - 1, 0)],
                                  dimension_numbers=('NWC', 'WIO', 'NWC'),
                                  feature_group_count=C) + conv_b
    xb = xc.reshape(B, S, RNN_BLOCKS, RNN_BLOCK_DIM)
    r = jax.nn.sigmoid(jnp.einsum('bshi,hij->bshj', xb, w_rg_a) + b_rg_a).reshape(B, S, C)
    i = jax.nn.sigmoid(jnp.einsum('bshi,hij->bshj', xb, w_rg_x) + b_rg_x).reshape(B, S, C)
    log_a = -LRU_C * r.astype(jnp.float32) * jax.nn.softplus(-lru_lambda.astype(jnp.float32))
    a = jnp.exp(log_a)
    mult = jnp.sqrt(-jnp.expm1(2.0 * log_a))
    mult = jnp.where((jnp.arange(S) == 0)[None, :, None], 1.0, mult)
    b = mult * (i * xc).astype(jnp.float32)

    def combine(left, right):
        a1, b1 = left
        a2, b2 = right
        return a1 * a2, a2 * b1 + b2

    _, h = lax.associative_scan(combine, (a, b), axis=1)
    y = h.astype(x_r.dtype) * jax.nn.gelu(y_r)
    return y @ w_rnn_o

def peer_ffn(x, w_peer_q, peer_subkeys, peer_u, peer_v):
    B, S, D = x.shape
    q = (x @ w_peer_q).reshape(B, S, PEER_HEADS, 2, PEER_HALF)
    s = jnp.einsum('bshcd,hcnd->bshcn', q, peer_subkeys, preferred_element_type=jnp.float32)
    top_s, top_i = lax.top_k(s, PEER_TOPK)
    cand = top_s[..., 0, :, None] + top_s[..., 1, None, :]
    cand = cand.reshape(B, S, PEER_HEADS, PEER_TOPK * PEER_TOPK)
    best_s, best_c = lax.top_k(cand, PEER_TOPK)
    i1 = jnp.take_along_axis(top_i[..., 0, :], best_c // PEER_TOPK, axis=-1)
    i2 = jnp.take_along_axis(top_i[..., 1, :], best_c % PEER_TOPK, axis=-1)
    experts = i1 * N_KEYS + i2
    gates = jax.nn.softmax(best_s, axis=-1).astype(x.dtype)
    T = B * S
    HK = PEER_HEADS * PEER_TOPK
    xs = x.reshape(T // PEER_CHUNK, PEER_CHUNK, D)
    es = experts.reshape(T // PEER_CHUNK, PEER_CHUNK, HK)
    gs = gates.reshape(T // PEER_CHUNK, PEER_CHUNK, HK)

    def chunk(args):
        xc, ec, gc = args
        u = peer_u[ec]
        act = jax.nn.gelu(jnp.einsum('tkd,td->tk', u, xc))
        return jnp.einsum('tk,tkd->td', gc * act, peer_v[ec])

    return lax.map(chunk, (xs, es, gs)).reshape(B, S, D)

def second_inputs(seed: int = 0) -> dict:
    key = jax.random.key(seed)
    ks = iter(jax.random.split(key, 40))
    f32 = jnp.float32

    def nrm(shape, scale):
        return jax.random.normal(next(ks), shape, f32) * scale

    def gain(shape):
        return 1.0 + nrm(shape, 0.05)

    L = DEPTH_2
    u = jax.random.uniform(next(ks), (L, D_RNN), f32, 0.9, 0.999)
    s_root = u ** (1.0 / LRU_C)
    lru_lambda = jnp.log(s_root) - jnp.log1p(-s_root)
    return {
        'x': nrm((BATCH, SEQ, D_MODEL), 1.0),
        'p': nrm((DEPTH_2, BATCH, SEQ, PLE_DIM), 1.0),
        'attn_norm': gain((L, D_MODEL)),
        'w_in': nrm((L, D_MODEL, IN_WIDTH), D_MODEL ** -0.5),
        'b_gate': nrm((L, 2 * D_MODEL), 0.01),
        'q_norm': gain((L, Q_LORA_RANK)),
        'w_uq': nrm((L, Q_LORA_RANK, N_HEADS * QK_HEAD_DIM), Q_LORA_RANK ** -0.5),
        'kv_norm': gain((L, KV_LORA_RANK)),
        'w_ukv': nrm((L, KV_LORA_RANK, N_HEADS * (QK_NOPE_DIM + V_HEAD_DIM)), KV_LORA_RANK ** -0.5),
        'w_attn_o': nrm((L, N_HEADS * V_HEAD_DIM, D_MODEL), (N_HEADS * V_HEAD_DIM) ** -0.5),
        'conv_w': nrm((L, CONV_WIDTH, D_RNN), CONV_WIDTH ** -0.5),
        'conv_b': nrm((L, D_RNN), 0.01),
        'w_rg_a': nrm((L, RNN_BLOCKS, RNN_BLOCK_DIM, RNN_BLOCK_DIM), RNN_BLOCK_DIM ** -0.5),
        'b_rg_a': nrm((L, RNN_BLOCKS, RNN_BLOCK_DIM), 0.01),
        'w_rg_x': nrm((L, RNN_BLOCKS, RNN_BLOCK_DIM, RNN_BLOCK_DIM), RNN_BLOCK_DIM ** -0.5),
        'b_rg_x': nrm((L, RNN_BLOCKS, RNN_BLOCK_DIM), 0.01),
        'lru_lambda': lru_lambda,
        'w_rnn_o': nrm((L, D_RNN, D_MODEL), D_RNN ** -0.5),
        'w_out': nrm((L, D_MODEL, D_MODEL), D_MODEL ** -0.5),
        'ffn_norm': gain((L, D_MODEL)),
        'w_peer_q': nrm((L, D_MODEL, PEER_HEADS * PEER_QUERY_DIM), D_MODEL ** -0.5),
        'peer_subkeys': nrm((L, PEER_HEADS, 2, N_KEYS, PEER_HALF), PEER_HALF ** -0.5),
        'peer_u': nrm((L, N_EXPERTS, D_MODEL), D_MODEL ** -0.5),
        'peer_v': nrm((L, N_EXPERTS, D_MODEL), PEER_HEADS ** -0.5),
        'ple_norm': gain((L, D_MODEL)),
        'w_ple_gate': nrm((L, D_MODEL, D_MODEL), D_MODEL ** -0.5),
        'w_ple_proj': nrm((L, PLE_DIM, D_MODEL), PLE_DIM ** -0.5),
        'final_norm': gain((D_MODEL,)),
    }

def second_block(x, p, attn_norm, w_in, b_gate, q_norm, w_uq, kv_norm, w_ukv, w_attn_o,
              conv_w, conv_b, w_rg_a, b_rg_a, w_rg_x, b_rg_x, lru_lambda, w_rnn_o, w_out,
              ffn_norm, w_peer_q, peer_subkeys, peer_u, peer_v, ple_norm, w_ple_gate,
              w_ple_proj, final_norm):
    h = x
    for l in range(DEPTH_2):
        n = rms_norm(h, attn_norm[l])
        c_q, c_kv, k_r, x_r, y_r, ga, gr = split_columns(n @ w_in[l])
        g_attn = jax.nn.sigmoid(ga + b_gate[l, :D_MODEL])
        g_rnn = jax.nn.sigmoid(gr + b_gate[l, D_MODEL:])
        y_attn = mla_branch(c_q, c_kv, k_r, q_norm[l], w_uq[l], kv_norm[l], w_ukv[l], w_attn_o[l])
        y_rnn = rglru_branch(x_r, y_r, conv_w[l], conv_b[l], w_rg_a[l], b_rg_a[l],
                             w_rg_x[l], b_rg_x[l], lru_lambda[l], w_rnn_o[l])
        h = h + (g_attn * y_attn + g_rnn * y_rnn) @ w_out[l]
        h = h + peer_ffn(rms_norm(h, ffn_norm[l]), w_peer_q[l], peer_subkeys[l], peer_u[l], peer_v[l])
        gate = jax.nn.sigmoid(rms_norm(h, ple_norm[l]) @ w_ple_gate[l])
        h = h + gate * (p[l] @ w_ple_proj[l])
    return rms_norm(h, final_norm)


def setup_inputs(seed=0):
    out = dict(first_inputs(seed))
    for name, value in second_inputs(seed + 1).items():
        if name != "x":
            out[name + "_2"] = value
    return out


def reference(
    x, c, ctx, c_ctx, ada_w, ada_b, post_ln_g, post_ln_b, w_in_even, conv_qk, b_igate, b_fgate,
    mh_norm_g, pool_w, pool_scale, w_out_even, w_in_odd, sgu_ln_g, sgu_ln_b, w_sp, b_sp,
    w_out_odd, p_2, attn_norm_2, w_in_2, b_gate_2, q_norm_2, w_uq_2, kv_norm_2, w_ukv_2,
    w_attn_o_2, conv_w_2, conv_b_2, w_rg_a_2, b_rg_a_2, w_rg_x_2, b_rg_x_2, lru_lambda_2,
    w_rnn_o_2, w_out_2, ffn_norm_2, w_peer_q_2, peer_subkeys_2, peer_u_2, peer_v_2, ple_norm_2,
    w_ple_gate_2, w_ple_proj_2, final_norm_2,
):
    x = first_block(
        x, c, ctx, c_ctx, ada_w, ada_b, post_ln_g, post_ln_b, w_in_even, conv_qk, b_igate,
        b_fgate, mh_norm_g, pool_w, pool_scale, w_out_even, w_in_odd, sgu_ln_g, sgu_ln_b, w_sp,
        b_sp, w_out_odd,
    )
    return second_block(
        x, p_2, attn_norm_2, w_in_2, b_gate_2, q_norm_2, w_uq_2, kv_norm_2, w_ukv_2, w_attn_o_2,
        conv_w_2, conv_b_2, w_rg_a_2, b_rg_a_2, w_rg_x_2, b_rg_x_2, lru_lambda_2, w_rnn_o_2,
        w_out_2, ffn_norm_2, w_peer_q_2, peer_subkeys_2, peer_u_2, peer_v_2, ple_norm_2,
        w_ple_gate_2, w_ple_proj_2, final_norm_2,
    )


_drawn_inputs = setup_inputs


def setup_inputs(seed=0):
    import zlib

    import numpy as np

    out = dict(_drawn_inputs(seed))
    spreads = {}
    factors = {'ctx': 2.855,
     'conv_qk': 2.719,
     'b_igate': 64.0,
     'mh_norm_g': 5.963,
     'pool_scale': 4.221,
     'sgu_ln_g': 4.774,
     'sgu_ln_b': 7.933,
     'b_sp': 3.501,
     'b_gate_2': 8.0,
     'q_norm_2': 4.816,
     'kv_norm_2': 3.941,
     'b_rg_a_2': 64.0,
     'b_rg_x_2': 64.0,
     'ple_norm_2': 26.025,
     'conv_b_2': 5.63,
     'ffn_norm_2': 2.923}
    for name, (base, spread) in spreads.items():
        noise = np.random.default_rng([zlib.crc32(name.encode()), seed]).standard_normal(out[name].shape)
        drawn = base * np.exp(spread * noise) if base else spread * noise
        out[name] = __import__('jax').numpy.asarray(drawn.astype(out[name].dtype))
    for name, factor in factors.items():
        out[name] = (out[name] * factor).astype(out[name].dtype)
    return out
```

```python
from contextlib import ExitStack

import numpy as np
import concourse.bass as bass
from concourse import mybir

F32 = mybir.dt.float32
F32R = mybir.dt.float32r
U32 = mybir.dt.uint32
ALU = mybir.AluOpType
ACT = mybir.ActivationFunctionType
AX = mybir.AxisListType.X

P = 128
T = 256
D = 2048
KC = D // P
RING = 4
UNIT = 2048
NBUF = 4
HALF = UNIT // 2
TILES = 4
NH = 4
ALPHA = 4.0 ** 0.25
LN_EPS = 1e-5
RMS_EPS = 1e-6
ROW = 64
PAD = 8
ROWP = ROW + 2 * PAD
HEADS = 16
PEER_H = 8
TOPK = 16
NKEY = 128
I2 = NKEY // 2
TG = 8
BIG = 3.0e38
SCALE = 192.0 ** -0.5

VEC = [("ada_b", 96), ("pln_g", 32), ("pln_b", 32), ("conv_q", 24), ("conv_k", 24), ("mh_g", 8), ("pool_s", 8),
       ("sgu_g", 16), ("sgu_b", 16), ("gate_b", 2), ("attn_n", 16), ("b_gate", 32), ("q_n", 6), ("kv_n", 4),
       ("conv_w", 64), ("conv_b", 16), ("b_ra", 16), ("b_rx", 16), ("lam", 16), ("ffn_n", 16), ("ple_n", 16),
       ("fin_n", 16)]
VOFF, NVEC = {}, 0
for _n, _c in VEC:
    VOFF[_n] = NVEC
    NVEC += _c

CON = [("ident", 128), ("ones", 128), ("tri_u", 128), ("tri_l", 128), ("invcnt", 4 * ROW), ("iota", 128)]
COFF, NCON = {}, 0
for _n, _c in CON:
    COFF[_n] = NCON
    NCON += _c
CON2 = [("cos", 256), ("sin", 256), ("causal", 512), ("rot", 128)]
C2OFF, NCON2 = {}, 0
for _n, _c in CON2:
    C2OFF[_n] = NCON2
    NCON2 += _c

STAGES = [
    ("ada_ss", "PPPP", 8, 0, "D"),
    ("gates", "N", 1, 2, "D"),
    ("v", "NPPNPPNPPNPP", 2, 2, "D"),
    ("k", "NPPNPPNPPNPP", 2, 2, "D"),
    ("q", "NPNPNPNP", 2, 1, "D"),
    ("o", "NPNPNPNP", 2, 1, "A"),
    ("zm", "NPNPNPNP", 2, 1, "A"),
    ("up", "NPNPNPNP", 2, 1, "D"),
    ("zp", "NNNN", 2, 1, "A"),
    ("poolw", "P", 1, 0, "D"),
    ("out0", "NNNN", 4, 1, "D"),
    ("v1", "NNNN", 4, 1, "D"),
    ("u1", "NNNN", 4, 1, "D"),
    ("z1", "NNNN", 4, 1, "A"),
    ("wsp", "P", 1, 0, "D"),
    ("out1", "NNNN", 4, 1, "D"),
    ("cc", "N" * 11, 1, 1, "D"),
    ("uv", "NNNN", 1, 4, "D"),
    ("uk", "NNNN", 1, 4, "D"),
    ("uq", "NNNN", 3, 2, "D"),
    ("ao", "NNNN", 4, 1, "D"),
    ("xr", "NNNN", 4, 1, "D"),
    ("rg", "PP", 1, 0, "D"),
    ("ga", "NNNN", 4, 1, "A"),
    ("yr", "NNNN", 4, 1, "A"),
    ("gr", "NNNN", 4, 1, "A"),
    ("ro", "NNNN", 4, 1, "D"),
    ("wo", "NNNN", 4, 1, "D"),
    ("pq", "NNNN", 4, 1, "D"),
    ("sk", "P", 1, 0, "D"),
    ("peer_u0", "NNNN", I2 // 4, 1, "A"),
    ("peer_v0", "NNNN", I2 // 4, 0, "D"),
    ("peer_u1", "NNNN", I2 // 4, 1, "A"),
    ("peer_v1", "NNNN", I2 // 4, 0, "D"),
    ("pg", "NNNN", 4, 1, "A"),
    ("pp", "NN", 1, 8, "D"),
]


class Stage:
    pass


def plan():
    u = n = p = td = ta = t = 0
    out = {}
    for name, pattern, iters, tiles, eng in STAGES:
        s = Stage()
        s.name, s.pattern, s.iters, s.tiles, s.eng = name, pattern, iters, tiles, eng
        s.u0, s.n0, s.p0, s.t0, s.td, s.ta = u, n, p, t, td, ta
        s.npi, s.ppi = pattern.count("N"), pattern.count("P")
        s.npos = [i for i, k in enumerate(pattern) if k == "N"]
        s.base = s.ta if eng == "A" else s.td
        u += len(pattern) * iters
        n += s.npi * iters
        p += s.ppi * iters
        made = s.npi * iters * tiles
        t += made
        if eng == "A":
            ta += made
        else:
            td += made
        out[name] = s
    return out, u, n


PLAN, N_UNITS, N_SPLIT = plan()
ORDER = [PLAN[s[0]] for s in STAGES]


def first_n_after(stage):
    for s in ORDER[ORDER.index(stage) + 1:]:
        if s.npi:
            return s.u0 + s.npos[0]
    return None


def program(nc, A, out, dbg=None, stop=None):
    with ExitStack() as ctx:
        base0 = (nc.sbuf_base + 63) // 64 * 64
        at = [base0]

        def place(name, shape, dt, offset):
            return nc.alloc_sbuf_tensor_at(name, shape, dt, offset=offset)

        def fixed(name, shape, dt):
            t = place(name, shape, dt, at[0])
            at[0] += (int(np.prod(shape[1:])) * 4 + 63) // 64 * 64
            return t

        ring = [fixed(f"ring{i}", [P, UNIT], F32) for i in range(RING)]
        hb = [fixed(f"unit_hi{i}", [P, HALF], F32R) for i in range(NBUF)]
        lb = [fixed(f"unit_lo{i}", [P, HALF], F32R) for i in range(NBUF)]
        h = fixed("resid", [P, KC, T], F32)
        vec = fixed("vec", [P, NVEC], F32)
        con = fixed("con", [P, NCON], F32)
        mod = fixed("mod", [P, 96, 2], F32)
        cond = fixed("cond", [P, KC, 2], F32)
        mrow = fixed("mrow", [64, T], F32)
        erow = fixed("erow", [64, T], F32)
        acol = fixed("acol", [P, 2, 4, 4], F32)
        rstd = fixed("rstd", [P, T], F32)
        tick = fixed("tick", [1, 1], F32)
        lam_s = fixed("lam_s", [P, KC], F32)
        z0 = (at[0] + 63) // 64 * 64
        KB = 1024

        def zone(name, kb, shape, dt=F32):
            off = z0 + int(kb * KB)
            assert off + int(np.prod(shape[1:])) * 4 <= nc.sbuf_usable_end, (name, off)
            return place(name, shape, dt, off)

        bank = [ctx.enter_context(nc.psum_tensor(f"bank{i}", [P, 512], F32)) for i in range(8)]

        sems = {}

        def S(name):
            if name not in sems:
                sems[name] = ctx.enter_context(nc.semaphore(name))
            return sems[name]

        slot_loaded = [S(f"slot_loaded{i}") for i in range(RING)]
        hi_done, lo_done, half_done = S("hi_done"), S("lo_done"), S("half_done")
        plain_done = S("plain_done")
        tile_free = {"D": S("tile_free_dve"), "A": S("tile_free_act")}

        def V(name, i=0, n=1):
            return vec[:, VOFF[name] + i:VOFF[name] + i + n]

        def C(name, a=0, b=None):
            w = dict(CON)[name]
            return con[:, COFF[name] + a:COFF[name] + (w if b is None else b)]

        ident, ones = C("ident"), C("ones")

        def bc(ap, n):
            return ap.unsqueeze(1).to_broadcast([ap.shape[0], n, ap.shape[1]])

        def flat(ap):
            return ap.rearrange("p a b -> p (a b)")

        xl = [zone("xl_hi", 0, [P, KC, T], F32R), zone("xl_lo", 16, [P, KC, T], F32R)]
        xc = [zone("xc_hi", 32, [P, KC, T], F32R), zone("xc_lo", 48, [P, KC, T], F32R)]
        tc_ = zone("tmp_ctx", 66, [P, KC, T])
        tl_ = zone("tmp_lat", 82, [P, KC, T])
        kk = zone("k0", 66, [P, 8, 512])
        vv = zone("v0", 82, [P, 4, 1024])
        qq = zone("q0", 98, [P, 8, T])
        vst = zone("vstage", 106, [P, 2, 2, T])
        gi = zone("gate_i", 98, [64, 512])
        gf = zone("gate_f", 100, [64, 512])
        gt = zone("gate_t", 102, [64, 512])
        gw = zone("gate_w", 104, [64, 512])
        gp = zone("gate_p", 106, [64, 512])
        gq = zone("gate_q", 108, [64, 512])
        sigo = zone("sig_o", 32, [P, 8, T])
        y0 = zone("y0", 40, [P, KC, T])
        silm, silp = y0[:, 0:8, :], y0[:, 8:16, :]
        upad = zone("u_pad", 56, [P, 8, 4 * ROWP])
        ps_ = [zone("pool_a", 106, [P, 8, ROWP]), zone("pool_b", 108.5, [P, 8, ROWP])]
        pt = [zone("probs0", 0, [P, 4, T]), zone("probs1", 4, [P, 4, T])]
        hs = zone("h_sum", 8, [P, 8, T])
        ebc = [zone("ebc0", 16, [P, T]), zone("ebc1", 17, [P, T])]
        dn = zone("dn", 18, [P, T])
        dn2 = zone("dn2", 19, [P, T])
        ht = zone("h_tmp", 20, [P, 2, T])
        hq = zone("h_sq", 82, [P, 8, T])
        hr = zone("h_rstd", 90, [P, 4, T])
        arow = zone("ada_rows", 0, [2, 2 * D])
        acc = zone("ada_acc", 110.25, [P, D])
        sq0 = zone("ln_sq", 32, [P, KC, T])
        tx = zone("tmp_x1", 32, [P, KC, T])
        vf = zone("v1f", 48, [P, KC, T])
        uu = zone("u1f", 64, [P, KC, T])
        zz = zone("z1f", 80, [P, KC, T])
        sq1 = zone("v1_sq", 96, [P, KC, T])
        vt1 = zone("v1tok", 32, [P, 2, D])
        yh = [zone("y1_hi", 96, [P, KC, T], F32R), zone("y1_lo", 48, [P, KC, T], F32R)]
        rt = zone("rms_tmp", 84, [P, KC, T])
        rq = zone("rms_sq", 32, [P, KC, T])
        cr = zone("c_raw", 84, [P, 11, T])
        csq = zone("c_sq", 96, [P, 10, T])
        cn = [zone("cn_hi", 32, [P, 10, T], F32R), zone("cn_lo", 42, [P, 10, T], F32R)]
        vt2 = zone("v2tok", 52, [P, 2, D])
        kn = zone("k_nope", 68, [P, KC, T])
        q2 = zone("q2", 84, [P, 24, T])
        v2f = zone("v2f", 84, [P, KC, T])
        con2 = zone("con2", 108, [P, NCON2])
        kpe = zone("k_pe", 112.75, [P, 2, T])
        rr = zone("rope_t", 114.75, [P, T])
        sm = [zone("att_s0", 32, [P, 2, T]), zone("att_s1", 34, [P, 2, T])]
        ptt = [zone("att_pt0", 36, [P, 2, T]), zone("att_pt1", 38, [P, 2, T])]
        mx = zone("att_max", 40, [P, 64])
        oh = [zone("o_hi", 32, [P, KC, T], F32R), zone("o_lo", 48, [P, KC, T], F32R)]
        ya = zone("y_attn", 64, [P, KC, T])
        xr = zone("x_r", 80, [P, KC, T])
        yr = zone("y_r", 96, [P, KC, T])
        xcv = zone("x_conv", 32, [P, KC, T])
        la = zone("log_a", 48, [P, KC, T])
        rw = zone("rnn_w", 112, [P, 4, T])
        ry = [zone("ry_hi", 32, [P, KC, T], F32R), zone("ry_lo", 48, [P, KC, T], F32R)]
        mt = [zone("mix_hi", 0, [P, KC, T], F32R), zone("mix_lo", 16, [P, KC, T], F32R)]
        pqq = zone("peer_q", 32, [P, KC, T])
        ss = zone("peer_s", 48, [P, 2, 16, NKEY])
        cand = zone("peer_cand", 64, [P, 8, 256])
        ceq = zone("peer_eq", 72, [P, 8, 256])
        tv = zone("top_v", 80, [P, 2, 16, TOPK])
        ti = zone("top_i", 82, [P, 2, 16, TOPK], U32)
        tf = zone("top_f", 84, [P, 2, 16, TOPK])
        bv = zone("best_v", 86, [P, 2, 8, TOPK])
        bi = zone("best_i", 87, [P, 2, 8, TOPK], U32)
        bj = zone("best_j", 88, [P, 2, 8, TOPK], U32)
        bf = zone("best_f", 89, [P, 2, 8, TOPK])
        gg = zone("peer_g", 90, [P, 2, 3, 8, TOPK])
        gs = zone("peer_gs", 93, [P, 2, 2, 8])
        gT = zone("peer_gT", 113, [P, 3, T])
        W = zone("peer_w", 32, [P, I2, T])
        oa = [zone("hot1_0", 96, [P, TG, NKEY]), zone("hot1_1", 100, [P, TG, NKEY])]
        ob = [zone("hot2_0", 104, [P, TG, I2]), zone("hot2_1", 106, [P, TG, I2])]
        gl = [zone("gelu0", 96, [P, T]), zone("gelu1", 97, [P, T])]
        wr = [zone(f"w_r{i}", 100 + 2 * i, [P, 2, T], F32R) for i in range(2)]
        pt_x = zone("p_tmp", 64, [P, 2, T])
        pt_r = zone("p_r", 66, [P, 2, 2, T], F32R)
        sg = zone("ple_sig", 48, [P, KC, T])
        ptile = zone("ple_t", 70, [P, 2, T])

        block = ctx.enter_context(nc.Block())

        def upto(name):
            return stop is None or [s[0] for s in STAGES].index(name) <= [s[0] for s in STAGES].index(stop)

        @block.sync
        def _(sp):
            sp.dma_start(cond[:], A["cond"]).then_inc(S("cond_in"), 16)
            sp.dma_start(vec[:], A["vec"]).then_inc(S("vec_in"), 16)
            sp.dma_start(con[:], A["con"]).then_inc(S("con_in"), 16)

            def release(s, pos, it):
                if s.pattern[pos] == "N":
                    n = s.n0 + s.pattern[:pos].count("N")
                    sp.wait_ge(lo_done, 2 * (n + it * s.npi) + 2)
                else:
                    p = s.p0 + s.pattern[:pos].count("P")
                    sp.wait_ge(plain_done, p + it * s.ppi + 1)

            where = {}
            for s in ORDER:
                L = len(s.pattern)

                def load(u, pos, it, first):
                    uu_ = s.u0 + pos
                    if first:
                        if uu_ >= RING:
                            release(*where[uu_ - RING])
                    else:
                        release(s, pos - RING if pos >= RING else pos - RING + L, it if pos >= RING else it - 1)
                    sp.dma_start(ring[uu_ % RING][:], A["w"][bass.ds(u, 1)].rearrange("a p n -> (a p) n")
                                 ).then_inc(slot_loaded[uu_ % RING], 16)

                for it in range(s.iters):
                    for pos in range(L):
                        where[s.u0 + it * L + pos] = (s, pos, it)
                for pos in range(L):
                    load(s.u0 + pos, pos, 0, True)
                if s.iters > 1:
                    assert L % RING == 0
                    with sp.Fori(1, s.iters) as it:
                        for pos in range(L):
                            load(s.u0 + pos + it * L, pos, it, False)
                if stop == s.name:
                    break
            sp.wait_ge(S("final"), 1)
            sp.dma_start(out, h[:]).then_inc(S("out_done"), 16)
            sp.wait_ge(S("out_done"), 16)

        def iterations(eng, s, body):
            if s.iters > 1:
                with eng.Fori(0, s.iters - 1) as it:
                    body(it, False)
            body(s.iters - 1, True)

        @block.gpsimd
        def _(pool):
            for s in ORDER:
                if s.npi:
                    def body(it, last):
                        for j in range(s.npi):
                            n = s.n0 + j + it * s.npi
                            slot = (s.u0 + s.npos[j]) % RING
                            for f in range(2):
                                b = (2 * (s.n0 + j) + f) % NBUF
                                pool.wait_ge(hi_done, 2 * n + f + 1)
                                pool.tensor_tensor(lb[b][:], ring[slot][:, f * HALF:(f + 1) * HALF],
                                                   hb[b][:].bitcast(F32), ALU.subtract).then_inc(lo_done, 1)
                    assert (2 * s.npi) % NBUF == 0 or s.iters == 1
                    iterations(pool, s, body)
                if stop == s.name:
                    break

        @block.tensor
        def _(pe):
            def n_unit(s, movs, per_tile, it, j):
                n_tiles = s.tiles // len(movs)
                n = s.n0 + j + it * s.npi
                for f in range(2):
                    b = (2 * (s.n0 + j) + f) % NBUF
                    pe.wait_ge(lo_done, 2 * n + f + 1)
                    for i in range(8 * f, min(8 * f + 8, n_tiles * per_tile)):
                        t, k = i // per_tile, i % per_tile
                        tile = [(j * n_tiles + t) * len(movs) + m for m in range(len(movs))]
                        if k == 0:
                            pe.wait_ge(tile_free[s.eng], s.base + tile[-1] + 1 + it * (s.npi * s.tiles))
                        for w, x in ((hb, 0), (hb, 1), (lb, 0)):
                            for m, mv in enumerate(movs):
                                mm = pe.matmul(bank[(s.t0 + tile[m]) % TILES][:, 0:T],
                                               w[b][:, (i % 8) * P:(i % 8 + 1) * P], mv[x][:, k, :],
                                               start=(k == 0 and w is hb and x == 0),
                                               stop=(k == per_tile - 1 and w is lb))
                    mm.then_inc(half_done, 1)

            def ada_sum(b):
                pe.wait_ge(plain_done, 32 + KC * (b + 1))
                for c in range(KC):
                    mm = pe.matmul(bank[4][:, 64 + b * KC + c:65 + b * KC + c], acc[:, c * P:(c + 1) * P],
                                   ones[:, 0:1], start=True, stop=True, skip_group_check=True)
                mm.then_inc(S("ada_sum"), 1)

            def run(name, movs=None, per_tile=KC, extra=None):
                s = PLAN[name]
                if s.td:
                    pe.wait_ge(tile_free["D"], TILES + s.td)
                if s.ta:
                    pe.wait_ge(tile_free["A"], TILES + s.ta)

                def body(it, last):
                    j = 0
                    for pos, kind in enumerate(s.pattern):
                        if kind == "P":
                            continue
                        n_unit(s, movs, per_tile, it, j)
                        if extra is not None:
                            extra(it, j)
                        j += 1
                iterations(pe, s, body)

            def slot_wait(name, i=0):
                s = PLAN[name]
                u = s.u0 + i
                pe.wait_ge(slot_loaded[u % RING], 16 * (u // RING + 1))
                return ring[u % RING]

            def feature_sum(src, dst, ready, value, done):
                pe.wait_ge(ready if not isinstance(ready, str) else S(ready), value)
                n = src.shape[1]
                for k in range(n):
                    mm = pe.matmul(dst, ones, src[:, k, :], start=(k == 0), stop=(k == n - 1))
                mm.then_inc(S(done), 1)

            pe.wait_ge(S("cond_ready"), 1)
            for u in range(2 * KC):
                pe.wait_ge(slot_loaded[u % RING], 16 * (u // RING + 1))
                for i in range(4):
                    mm = pe.matmul(bank[4 * (u % 2) + i][0:2, :], cond[:, u // 2, :],
                                   ring[u % RING][:, i * 512:(i + 1) * 512], start=(u < 2), stop=(u >= 2 * KC - 2))
                mm.then_inc(plain_done, 1)
            pe.wait_ge(S("con_in"), 16)
            pe.wait_ge(S("ada_rows"), 8)
            for c in range(2 * KC):
                mm = pe.matmul(bank[4][:, 2 * c:2 * c + 2], arow[:, c * P:(c + 1) * P], ident[0:2, 0:2],
                               start=True, stop=True, skip_group_check=True)
            mm.then_inc(S("ada_cols"), 1)
            pe.wait_ge(S("xm_lat"), 1)
            pe.wait_ge(S("xm_ctx"), 1)
            run("gates", [xl, xc])
            pe.wait_ge(S("a_rows"), 1)
            for d in range(2):
                for t in range(4):
                    mm = pe.matmul(bank[5][:, (d * 4 + t) * 4:(d * 4 + t) * 4 + 4],
                                   gi[:, t * P:(t + 1) * P], ident[0:64, 32 * d:32 * d + 4],
                                   start=True, stop=True, skip_group_check=True)
            mm.then_inc(S("a_cols"), 1)
            sv = PLAN["v"]

            def v_transposes(it, j):
                pe.wait_ge(tile_free["D"], TILES + sv.td + 2 * (j + 1) + it * (2 * sv.npi))
                pe.wait_ge(S("v_tok"), j + 1 + it * sv.npi)
                for t in range(4):
                    mm = pe.transpose(bank[6][:, t * P:(t + 1) * P],
                                      vst[:, j % 2, 1 - t // 2, (t % 2) * P:(t % 2 + 1) * P], ident)
                mm.then_inc(S("vt_done"), 1)
            run("v", [xl, xc], extra=v_transposes)
            ada_sum(0)
            run("k", [xl, xc])
            ada_sum(1)
            run("q", [xl])
            run("o", [xl])
            ada_sum(2)
            run("zm", [xl])
            run("up", [xl])
            ada_sum(3)
            run("zp", [xl])
            w = slot_wait("poolw")
            pe.wait_ge(S("pooled"), 1)
            pe.wait_ge(tile_free["A"], TILES + PLAN["poolw"].ta)
            pe.wait_ge(tile_free["D"], TILES + PLAN["poolw"].td)
            for g in range(4):
                for j in range(2):
                    for k in range(2):
                        i = (g * 2 + k) * 2 + j
                        mv = upad[:, 2 * g + k, :].rearrange("p (r c) -> p r c", r=4)[:, :, PAD:PAD + ROW]
                        mm = pe.matmul(bank[g][:, j * T:(j + 1) * T], w[:, i * P:(i + 1) * P], mv,
                                       start=(k == 0), stop=(k == 1), skip_group_check=True)
            mm.then_inc(plain_done, 1)
            def gates_bc(i):
                hd, d = i // 2, i % 2
                if i >= 1:
                    pe.wait_ge(S("bc_used"), i)
                for r, row in enumerate((mrow, erow)):
                    pick = ident[0:64, 32 * d + hd:32 * d + hd + 1].to_broadcast([64, P])
                    mm = pe.matmul(bank[7][:, r * T:(r + 1) * T], pick, row[:], start=True, stop=True,
                                   skip_group_check=True)
                mm.then_inc(S("bc_done"), 1)

            def scores(hd):
                if hd >= 1:
                    pe.wait_ge(S("probs_ready"), 2 * hd)
                for t in range(4):
                    for c in range(2):
                        mm = pe.matmul(bank[5 + t // 2][:, (t % 2) * T:(t % 2 + 1) * T],
                                       kk[:, 2 * hd + c, t * P:(t + 1) * P], qq[:, 2 * hd + c, :],
                                       start=(c == 0), stop=(c == 1), skip_group_check=True)
                mm.then_inc(S("scores_done"), 1)

            def prob_value(i):
                hd, d = i // 2, i % 2
                pe.wait_ge(S("probs_ready"), i + 1)
                if i >= 2:
                    pe.wait_ge(S("num_used"), i - 1)
                order = [(0, 0, T), (1, 0, T), (2, 0, T), (3, P, T)] if d == 0 else \
                        [(0, 0, T), (1, 0, T), (3, 0, T), (2, 0, P)]
                num, den = bank[2 * (i % 2)], bank[2 * (i % 2) + 1]
                for c in range(3):
                    for n, (t, a, b) in enumerate(order):
                        dst = den[:, a:b] if c == 2 else num[:, c * T + a:c * T + b]
                        lhs = ones if c == 2 else vv[:, t, hd * 256 + c * P:hd * 256 + (c + 1) * P]
                        mm = pe.matmul(dst, lhs, pt[i % 2][:, t, a:b], start=(n == 0), stop=(n == 3),
                                       skip_group_check=True)
                mm.then_inc(S("num_done"), 1)

            pe.wait_ge(S("rows_ready"), 1)
            pe.wait_ge(S("k_silu"), 1)
            pe.wait_ge(S("q_silu"), 1)
            pe.wait_ge(S("v_tok"), 8 + 1)
            pe.wait_ge(S("yp_done"), 1)
            gates_bc(0)
            scores(0)
            for i in range(2 * NH):
                if i + 1 < 2 * NH:
                    gates_bc(i + 1)
                if i % 2 == 1 and i // 2 + 1 < NH:
                    scores(i // 2 + 1)
                prob_value(i)
            for r in range(2):
                pe.wait_ge(S("hn_in"), r + 1)
                src = hs if r == 0 else hq
                for g in range(NH):
                    for c in range(2):
                        mm = pe.matmul(bank[5 + g // 2][:, (g % 2) * T:(g % 2 + 1) * T], ones, src[:, 2 * g + c, :],
                                       start=(c == 0), stop=(c == 1), skip_group_check=True)
                mm.then_inc(S("hn_sum"), 1)
            pe.wait_ge(S("y0_ready"), 1)
            run("out0", [xl])
            feature_sum(h, bank[5][:, 0:T], tile_free["D"], TILES + PLAN["v1"].td, "ln0_sum")
            feature_sum(sq0, bank[6][:, 0:T], "ln0_in", 1, "ln0_sum")
            if not upto("v1"):
                return
            pe.wait_ge(S("xm1"), 1)
            run("v1", [xl])
            feature_sum(vf, bank[5][:, 0:T], tile_free["D"], TILES + PLAN["u1"].td, "lnv_sum")
            feature_sum(sq1, bank[6][:, 0:T], "lnv_in", 1, "lnv_sum")
            run("u1", [xl])
            pe.wait_ge(S("v1_norm"), 1)
            for g in range(8):
                if g >= 2:
                    pe.wait_ge(S("v1_tok"), g - 1)
                for i in range(4):
                    j = 4 * g + i
                    mm = pe.transpose(bank[5 + g % 2][:, i * P:(i + 1) * P], vf[:, j % 16, (j // 16) * P:(j // 16 + 1) * P],
                                      ident)
                mm.then_inc(S("v1_tp"), 1)
            run("z1", [xl])
            w = slot_wait("wsp")
            pe.wait_ge(S("v1_tok"), 8)
            for c in range(KC):
                b = bank[4 + c % 4]
                if c >= 4:
                    pe.wait_ge(S("sgu_used"), c - 3)
                for t in range(2):
                    pe.matmul(b[:, t * P:(t + 1) * P], vt1[:, t, c * P:(c + 1) * P], w[:, (c // 2) * P:(c // 2 + 1) * P],
                              start=True, stop=False, skip_group_check=True)
                    mm = pe.matmul(b[:, t * P:(t + 1) * P], ones[0:1, :],
                                   w[0:1, HALF + (c // 2) * P:HALF + (c // 2 + 1) * P], start=False, stop=True,
                                   skip_group_check=True)
                mm.then_inc(S("sgu_done") if c < KC - 1 else plain_done, 1)
            pe.wait_ge(S("y1_ready"), 1)
            run("out1", [yh])
            feature_sum(h, bank[5][:, 0:T], tile_free["D"], TILES + PLAN["cc"].td, "ln1_sum")
            feature_sum(sq0, bank[6][:, 0:T], "ln1_in", 1, "ln1_sum")
            if not upto("cc"):
                return
            feature_sum(rq, bank[7][:, 0:T], "rms_in", 1, "rms_sum")
            pe.wait_ge(S("n2"), 1)
            run("cc", [xl])
            for r, (a, b) in enumerate(((0, 6), (6, 10))):
                feature_sum(csq[:, a:b, :], bank[5 + r][:, 0:T], "csq", 1, "c_sum")
            pe.wait_ge(S("con2_in"), 16)
            rot = con2[:, C2OFF["rot"]:C2OFF["rot"] + 128]
            pe.matmul(bank[7][:, 0:T], rot, cr[:, 10, :], start=True, stop=True).then_inc(S("rope_done"), 1)
            pe.wait_ge(S("cn_ready"), 1)
            ckv = [cn[0][:, 6:10, :], cn[1][:, 6:10, :]]
            cq = [cn[0][:, 0:6, :], cn[1][:, 0:6, :]]
            run("uv", [ckv], per_tile=4)
            run("uk", [ckv], per_tile=4)
            for g in range(8):
                if g >= 2:
                    pe.wait_ge(S("v2_tok"), g - 1)
                for i in range(4):
                    j = 4 * g + i
                    mm = pe.transpose(bank[5 + g % 2][:, i * P:(i + 1) * P], v2f[:, j % 16, (j // 16) * P:(j // 16 + 1) * P], ident)
                mm.then_inc(S("v2_tp"), 1)
            run("uq", [cq], per_tile=6)
            pe.wait_ge(tile_free["D"], TILES + PLAN["ao"].td)
            for j in range(8):
                if j >= 2:
                    pe.wait_ge(S("rope_used"), j)
                pe.matmul(bank[5 + j % 2][:, 0:T], rot, q2[:, 16 + j, :], start=True, stop=True
                          ).then_inc(S("rope_done"), 1)
            def att_scores(hd):
                if hd >= 2:
                    pe.wait_ge(S("att_masked"), hd - 1)
                b = bank[hd % 2]
                for t in range(2):
                    pe.matmul(b[:, t * T:(t + 1) * T], q2[:, hd, t * P:(t + 1) * P], kn[:, hd, :],
                              start=True, stop=False, skip_group_check=True)
                    mm = pe.matmul(b[:, t * T:(t + 1) * T], q2[:, 16 + hd // 2, t * P:(t + 1) * P], kpe[:, hd % 2, :],
                                   start=False, stop=True, skip_group_check=True)
                mm.then_inc(S("att_s"), 1)

            def att_values(hd):
                pe.wait_ge(S("att_p"), hd + 1)
                if hd >= 1:
                    pe.wait_ge(S("att_pt"), hd)
                for k in range(2):
                    for t in range(2):
                        mm = pe.transpose(bank[2][:, k * T + t * P:k * T + (t + 1) * P],
                                          sm[hd % 2][:, t, k * P:(k + 1) * P], ident)
                mm.then_inc(S("att_tp"), 1)
                pe.wait_ge(S("att_pt"), hd + 1)
                if hd >= 2:
                    pe.wait_ge(S("att_o_used"), hd - 1)
                for k in range(2):
                    mm = pe.matmul(bank[5 + hd % 2][:, 0:T], vt2[:, k, hd * P:(hd + 1) * P], ptt[hd % 2][:, k, :],
                                   start=(k == 0), stop=(k == 1))
                mm.then_inc(S("att_o"), 1)
            pe.wait_ge(S("rope_used"), 9)
            att_scores(0)
            for hd in range(HEADS):
                if hd + 1 < HEADS:
                    att_scores(hd + 1)
                att_values(hd)
            pe.wait_ge(S("o_ready"), 1)
            run("ao", [oh])
            run("xr", [xl])
            wa, wx = slot_wait("rg", 0), slot_wait("rg", 1)
            pe.wait_ge(tile_free["D"], TILES + PLAN["rg"].td)
            for c in range(KC):
                if c >= 2:
                    pe.wait_ge(S("rg_used"), c - 1)
                b = bank[5 + c % 2]
                ma = pe.matmul(b[:, 0:T], wa[:, c * P:(c + 1) * P], xcv[:, c, :], start=True, stop=True,
                               skip_group_check=True)
                mx_ = pe.matmul(b[:, T:2 * T], wx[:, c * P:(c + 1) * P], xcv[:, c, :], start=True, stop=True,
                                skip_group_check=True)
                if c < KC - 1:
                    mx_.then_inc(S("rg_done"), 1)
                else:
                    ma.then_inc(plain_done, 1)
                    mx_.then_inc(plain_done, 1)
            run("ga", [xl])
            run("yr", [xl])
            run("gr", [xl])
            pe.wait_ge(S("ry_ready"), 1)
            run("ro", [ry])
            pe.wait_ge(S("mix_ready"), 1)
            run("wo", [mt])
            if not upto("pq"):
                return
            feature_sum(rq, bank[7][:, 0:T], "rms_in", 2, "rms_sum")
            pe.wait_ge(S("n2"), 2)
            run("pq", [xl])
            w = slot_wait("sk")
            pe.wait_ge(tile_free["D"], TILES + PLAN["sk"].td)
            for g in range(8):
                t = g // 4
                if g >= 2:
                    pe.wait_ge(S("s_evac"), g - 1)
                for i in range(4):
                    j = 4 * (g % 4) + i
                    mm = pe.matmul(bank[5 + g % 2][:, i * P:(i + 1) * P], pqq[:, j, t * P:(t + 1) * P],
                                   w[:, j * P:(j + 1) * P], start=True, stop=True, skip_group_check=True)
                mm.then_inc(S("s_done") if g < 7 else plain_done, 1)
            pe.wait_ge(S("gates_tok"), 2)
            for t in range(2):
                for i in range(3):
                    mm = pe.transpose(bank[5 + t][:, i * P:(i + 1) * P], flat(gg[:, t, i, :, :]), ident)
            mm.then_inc(S("gT_done"), 1)
            pe.wait_ge(S("gT_read"), 2)
            for r in range(2):
                if r == 1:
                    pe.wait_ge(S("acc_used"), 1)
                def build(it, last, r=r):
                    for k in range(2):
                        i = r * (T // TG) + k + it * 2
                        pe.wait_ge(S("hot1"), i + 1)
                        pe.wait_ge(S("hot2"), i + 1)
                        pe.wait_ge(S("g_used"), i + 1)
                        for t in range(TG):
                            mm = pe.matmul(bank[5 + k][:, t * I2:(t + 1) * I2], oa[k][:, t, :], ob[k][:, t, :],
                                           start=True, stop=True, skip_group_check=True)
                        mm.then_inc(S("g_done"), 1)
                with pe.Fori(0, T // TG // 2) as it:
                    build(it, False)
                run(f"peer_u{r}", [xl])
                s = PLAN[f"peer_v{r}"]
                pe.wait_ge(tile_free["A"], TILES + s.ta)
                pe.wait_ge(S("g_used"), (r + 1) * (T // TG) + 2)

                def body(it, first, r=r, s=s):
                    for j in range(4):
                        n = s.n0 + j + it * 4
                        pe.wait_ge(S("wr_ready"), r * I2 + j + 1 + it * 4)
                        for f in range(2):
                            b = (2 * (s.n0 + j) + f) % NBUF
                            pe.wait_ge(lo_done, 2 * n + f + 1)
                            for c in range(8):
                                cc = 8 * f + c
                                o = bank[cc // 2][:, (cc % 2) * T:(cc % 2 + 1) * T]
                                for w_, x in ((hb, 0), (hb, 1), (lb, 0)):
                                    mm = pe.matmul(o, w_[b][:, c * P:(c + 1) * P], wr[j % 2][:, x, :],
                                                   start=(first and j == 0 and cc % 2 == 0 and w_ is hb and x == 0),
                                                   stop=False, skip_group_check=True)
                            mm.then_inc(half_done, 1)
                body(0, True)
                with pe.Fori(1, s.iters) as it:
                    body(it, False)
            feature_sum(rq, bank[7][:, 0:T], "rms_in", 3, "rms_sum")
            pe.wait_ge(S("n2"), 3)
            run("pg", [xl])
            pe.wait_ge(S("p_ready"), 1)
            run("pp", [[pt_r[:, 0, :, :], pt_r[:, 1, :, :]]], per_tile=2)
            feature_sum(rq, bank[7][:, 0:T], "rms_in", 4, "rms_sum")

        @block.scalar
        def _(act):
            def hi(n, place):
                slot, loads, n_static = place
                act.wait_ge(slot_loaded[slot], 16 * loads)
                for f in range(2):
                    b = (2 * n_static + f) % NBUF
                    act.wait_ge(half_done, 2 * n + f + 1)
                    act.activation(hb[b][:], ring[slot][:, f * HALF:(f + 1) * HALF], ACT.Copy).then_inc(hi_done, 1)

            def ahead(s, j, it, last):
                L = len(s.pattern)
                n = s.n0 + j + 1 + it * s.npi
                if j + 1 < s.npi:
                    u = s.u0 + s.npos[j + 1]
                    hi(n, (u % RING, u // RING + 1 + it * (L // RING), s.n0 + j + 1))
                elif not last:
                    u = s.u0 + s.npos[0]
                    hi(n, (u % RING, u // RING + 1 + (it + 1) * (L // RING), s.n0 + s.npi))
                else:
                    u = first_n_after(s)
                    if u is not None and not (stop == s.name):
                        hi(n, (u % RING, u // RING + 1, s.n0 + s.npi * s.iters))

            roots = [0]

            def root(ap):
                roots[0] += 1
                act.wait_ge(S("var_ready"), roots[0])
                act.activation(ap, ap, ACT.Sqrt).then_inc(S("root_done"), 1)

            def run(name, evac=None):
                s = PLAN[name]

                def body(it, last):
                    for j in range(s.npi):
                        ahead(s, j, it, last)
                        if evac is not None:
                            act.wait_ge(half_done, NBUF + 2 * (s.n0 + j + it * s.npi) + 2)
                            i = j + it * s.npi
                            evac(i, bank[(s.t0 + j) % TILES][:, 0:T]).then_inc(tile_free["A"], 1)
                iterations(act, s, body)

            def at_chunk(t, i):
                if isinstance(i, int):
                    return t[:, i, :]
                return t[:, bass.ds(i, 1), :].rearrange("p a t -> p (a t)")

            act.dma_start(h[:], A["xT"]).then_inc(S("x_in"), 16)
            act.dma_start(tc_[:], A["ctxT"]).then_inc(S("ctx_in"), 16)
            act.wait_ge(S("cond_in"), 16)
            act.activation(flat(cond[:]), flat(cond[:]), ACT.Silu).then_inc(S("cond_ready"), 1)
            s0 = PLAN["gates"]
            act.wait_ge(S("init"), 1)
            hi(0, (s0.u0 % RING, s0.u0 // RING + 1, 0))
            act.wait_ge(plain_done, 2 * KC)
            for b in (1, 3, 5, 7):
                act.activation(arow[:, b * 512:(b + 1) * 512], bank[b][0:2, :], ACT.Copy).then_inc(S("ada_rows"), 1)
            act.wait_ge(S("xm_tmp"), 1)
            act.activation(flat(xl[0][:]), flat(tl_[:]), ACT.Copy).then_inc(S("xm_hi"), 1)
            act.wait_ge(S("xm_tmp"), 2)
            act.activation(flat(xc[0][:]), flat(tc_[:]), ACT.Copy).then_inc(S("xm_hi"), 1)
            act.activation(flat(h[:]), flat(h[:]), ACT.Copy, scale=ALPHA).then_inc(S("ax0"), 1)
            run("gates")
            act.wait_ge(S("gate_abs"), 1)
            act.activation(gw[:], gt[:], ACT.Exp, scale=-1.0).then_inc(S("gate_exp"), 1)
            run("v")
            act.wait_ge(S("m_rows"), 1)
            act.activation(erow[:], erow[:], ACT.Exp, scale=-1.0).then_inc(S("rows_ready"), 1)
            run("k")
            run("q")
            act.wait_ge(tile_free["D"], TILES + PLAN["q"].td)
            act.activation(flat(kk[:]), flat(kk[:]), ACT.Silu).then_inc(S("k_silu"), 1)
            act.wait_ge(tile_free["D"], TILES + PLAN["o"].td)
            act.activation(flat(qq[:]), flat(qq[:]), ACT.Silu).then_inc(S("q_silu"), 1)
            run("o", lambda i, ps: act.activation(at_chunk(sigo, i), ps, ACT.Sigmoid))
            run("zm", lambda i, ps: act.activation(at_chunk(silm, i), ps, ACT.Silu))
            run("up")
            run("zp", lambda i, ps: act.activation(at_chunk(silp, i), ps, ACT.Silu))
            for i in range(2 * NH):
                act.wait_ge(S("args"), i + 1)
                act.activation(flat(pt[i % 2][:]), flat(pt[i % 2][:]), ACT.Exp, scale=-1.0).then_inc(S("gexp"), 1)
            act.wait_ge(S("hc"), 1)
            act.activation(flat(hq[:]), flat(hs[:]), ACT.Square).then_inc(S("hn_in"), 1)
            root(flat(hr[:]))
            act.wait_ge(S("y0"), 1)
            act.activation(flat(xl[0][:]), flat(y0[:]), ACT.Copy).then_inc(S("y0_hi"), 1)
            run("out0")
            act.wait_ge(S("ln0_c"), 1)
            act.activation(flat(sq0[:]), flat(h[:]), ACT.Square).then_inc(S("ln0_in"), 1)
            root(rstd[:])
            if not upto("v1"):
                return
            act.wait_ge(S("xm1_tmp"), 1)
            act.activation(flat(xl[0][:]), flat(tx[:]), ACT.Copy).then_inc(S("xm1_hi"), 1)
            act.activation(flat(h[:]), flat(h[:]), ACT.Copy, scale=ALPHA).then_inc(S("ax1"), 1)
            run("v1")
            act.wait_ge(S("lnv_c"), 1)
            act.activation(flat(sq1[:]), flat(vf[:]), ACT.Square).then_inc(S("lnv_in"), 1)
            root(rstd[:])
            run("u1")
            run("z1", lambda i, ps: act.activation(at_chunk(zz, i), ps, ACT.Silu))
            act.wait_ge(S("y1"), 1)
            act.activation(flat(yh[0][:]), flat(uu[:]), ACT.Copy).then_inc(S("y1_hi"), 1)
            run("out1")
            act.wait_ge(S("ln1_c"), 1)
            act.activation(flat(sq0[:]), flat(h[:]), ACT.Square).then_inc(S("ln1_in"), 1)
            root(rstd[:])
            if not upto("cc"):
                return

            def rms(i):
                act.wait_ge(S("h_ready"), i)
                act.activation(flat(rq[:]), flat(h[:]), ACT.Square).then_inc(S("rms_in"), 1)
                root(rstd[:])
                if i < 4:
                    act.wait_ge(S("rms_t"), i)
                    act.activation(flat(xl[0][:]), flat(rt[:]), ACT.Copy).then_inc(S("n2_hi"), 1)
            rms(1)
            act.dma_start(con2[:], A["con2"]).then_inc(S("con2_in"), 16)
            run("cc")
            act.wait_ge(S("c_evac"), 1)
            act.activation(flat(csq[:]), flat(cr[:, 0:10, :]), ACT.Square).then_inc(S("csq"), 1)
            root(rstd[:])
            root(rstd[:])
            act.wait_ge(S("c_norm"), 1)
            act.activation(flat(cn[0][:]), flat(cr[:, 0:10, :]), ACT.Copy).then_inc(S("cn_hi"), 1)
            run("uv")
            run("uk")
            run("uq")
            for hd in range(HEADS):
                act.wait_ge(S("att_max"), hd + 1)
                for t in range(2):
                    ins = act.activation(sm[hd % 2][:, t, :], sm[hd % 2][:, t, :], ACT.Exp,
                                         bias=mx[:, 2 * (hd % 4) + t:2 * (hd % 4) + t + 1],
                                         accum_out=mx[:, 16 + 2 * (hd % 4) + t:17 + 2 * (hd % 4) + t])
                    ins.then_inc(S("att_exp"), 1)
            act.wait_ge(S("att_o_used"), HEADS)
            act.activation(flat(oh[0][:]), flat(q2[:, 0:KC, :]), ACT.Copy).then_inc(S("o_hi"), 1)
            run("ao")
            run("xr")
            act.wait_ge(S("lam_abs"), 1)
            act.activation(lam_s[:], lam_s[:], ACT.Exp, scale=-1.0).then_inc(S("lam_exp"), 1)
            for c in range(KC):
                if c < KC - 1:
                    act.wait_ge(S("rg_done"), c + 1)
                else:
                    act.wait_ge(plain_done, PLAN["rg"].p0 + 2)
                b = bank[5 + c % 2]
                act.activation(xr[:, c, :], b[:, 0:T], ACT.Sigmoid, bias=V("b_ra", c)).then_inc(S("rg_r"), 1)
                if c >= 2:
                    act.wait_ge(S("ix_used"), c - 1)
                act.activation(rw[:, c % 2, :], b[:, T:2 * T], ACT.Sigmoid, bias=V("b_rx", c)).then_inc(S("rg_used"), 1)
            act.wait_ge(S("la_ready"), 1)
            act.activation(flat(xr[:]), flat(la[:]), ACT.Exp).then_inc(S("a_ready"), 1)
            act.wait_ge(S("a_ready"), 1)
            act.activation(flat(la[:]), flat(la[:]), ACT.Tanh).then_inc(S("a_ready"), 1)

            def gate_bias(i):
                return V("b_gate", i) if isinstance(i, int) else vec[:, bass.ds(VOFF["b_gate"] + i, 1)]
            run("ga", lambda i, ps: act.activation(at_chunk(yr, i), ps, ACT.Sigmoid, bias=gate_bias(i)))
            act.wait_ge(S("m2_ready"), 1)
            act.activation(flat(la[:]), flat(la[:]), ACT.Sqrt).then_inc(S("mult_ready"), 1)
            act.wait_ge(S("ga_used"), 1)
            run("yr", lambda i, ps: act.activation(at_chunk(yr, i), ps, ACT.Gelu_apprx_tanh))

            act.wait_ge(S("scanned"), 1)
            run("gr", lambda i, ps: act.activation(at_chunk(xr, i), ps, ACT.Sigmoid, bias=gate_bias(16 + i)))
            act.wait_ge(S("ry_t"), 1)
            act.activation(flat(ry[0][:]), flat(yr[:]), ACT.Copy).then_inc(S("ry_hi"), 1)
            run("ro")
            act.wait_ge(S("mix_t"), 1)
            act.activation(flat(mt[0][:]), flat(ya[:]), ACT.Copy).then_inc(S("mix_hi"), 1)
            run("wo")
            if not upto("pq"):
                return
            rms(2)
            run("pq")
            for t in range(2):
                act.wait_ge(S("gate_d"), t + 1)
                act.activation(bv[:, t, :, :], bv[:, t, :, :], ACT.Exp).then_inc(S("gate_e"), 1)
            for r in range(2):
                if r == 1:
                    act.wait_ge(S("wr_ready"), I2)

                def gates_out(it, r=r):
                    for k in range(2):
                        i = r * (T // TG) + k + it * 2
                        act.wait_ge(S("g_done"), i + 3)
                        act.activation(W[:, :, bass.ds(it * (2 * TG) + k * TG, TG)],
                                       bank[5 + k][:, :].rearrange("p (t i) -> p i t", t=TG), ACT.Copy
                                       ).then_inc(S("g_used"), 1)
                with act.Fori(0, T // TG // 2) as it:
                    gates_out(it)
                s = PLAN[f"peer_u{r}"]

                def u_body(it, last, r=r, s=s):
                    for j in range(4):
                        ahead(s, j, it, last)
                        act.wait_ge(half_done, NBUF + 2 * (s.n0 + j + it * 4) + 2)
                        act.wait_ge(S("gelu_free"), r * I2 + j + 1 + it * 4)
                        act.activation(gl[j % 2][:], bank[(s.t0 + j) % TILES][:, 0:T], ACT.Gelu_apprx_tanh
                                       ).then_inc(tile_free["A"], 1)
                iterations(act, s, u_body)
                s = PLAN[f"peer_v{r}"]

                def v_body(it, last, r=r, s=s):
                    for j in range(4):
                        act.wait_ge(half_done, NBUF + 2 * (s.n0 + j + it * 4) - 2)
                        act.activation(wr[j % 2][:, 0, :], at_chunk(W, j + it * 4), ACT.Copy
                                       ).then_inc(S("wr_hi"), 1)
                        ahead(s, j, it, last)
                act.wait_ge(S("gelu_free"), (r + 1) * I2 + 2)
                iterations(act, s, v_body)
            act.wait_ge(S("wr_ready"), 2 * I2)
            act.dma_start(pt_x[:], A["pT"]).then_inc(S("p_in"), 16)
            rms(3)
            act.wait_ge(S("p_in"), 16)
            act.activation(flat(pt_r[:, 0, :, :]), flat(pt_x[:]), ACT.Copy).then_inc(S("p_hi"), 1)
            run("pg", lambda i, ps: act.activation(at_chunk(sg, i), ps, ACT.Sigmoid))
            run("pp")
            rms(4)

        @block.vector
        def _(dve):
            seq_sem = S("dve_seq")
            seq = [0, 0]

            def go(ins):
                seq[0] += 1
                return ins.then_inc(seq_sem, 1)

            def sync():
                dve.wait_ge(seq_sem, seq[1] + seq[0])

            def loop(n, per, body, tail=0):
                if n - tail > 1:
                    start = seq[0]
                    with dve.Fori(0, n - tail) as it:
                        seq[1] = it * per
                        body(it)
                    assert seq[0] - start == per, (seq[0] - start, per)
                    seq[0] = start + (n - tail) * per
                    seq[1] = 0
                    rest = range(n - tail, n)
                else:
                    rest = range(n)
                for i in rest:
                    start = seq[0]
                    body(i)
                    assert seq[0] - start == per, (seq[0] - start, per)

            def ada(s, j, it):
                pos = s.npos[j] + 1
                while pos < len(s.pattern) and s.pattern[pos] == "P":
                    u, before = s.u0 + pos, s.pattern[:pos].count("P")
                    k = (s.p0 + before) % KC + it * s.ppi
                    dve.wait_ge(slot_loaded[u % RING], 16 * (u // RING + 1 + it * (len(s.pattern) // RING)))
                    dve.wait_ge(plain_done, s.p0 + before + it * s.ppi)
                    col = cond[:, bass.ds(k, 1), 0:1].rearrange("p a s -> p (a s)")
                    dve.scalar_tensor_tensor(acc[:], ring[u % RING][:], col, acc[:], ALU.mult, ALU.add
                                             ).then_inc(plain_done, 1)
                    pos += 1

            def ada_start(b):
                if b:
                    dve.wait_ge(S("ada_sum"), b)
                go(dve.memset(acc[:], 0.0)); sync()

            def ada_only(name):
                s = PLAN[name]

                def body(it):
                    for j in range(s.npi):
                        ada(s, j, it)
                loop(s.iters, 0, body)

            def run(name, evac, per=0):
                s = PLAN[name]

                def body(it):
                    for j in range(s.npi):
                        ada(s, j, it)
                        for tl in range(s.tiles):
                            f = 1
                            if s.tiles > 2 or name == "uq":
                                f = ((tl + 1) * PER_TILE[name] - 1) // 8
                            if tl == 0 or s.tiles > 2 or name == "uq":
                                dve.wait_ge(half_done, NBUF + 2 * (s.n0 + j + it * s.npi) + f + 1)
                            i = j * s.tiles + tl + it * (s.npi * s.tiles)
                            evac(i, bank[(s.t0 + j * s.tiles + tl) % TILES][:, 0:T], j * s.tiles + tl
                                 ).then_inc(tile_free["D"], 1)
                loop(s.iters, per, body)

            def at(t, i, a=None, b=None):
                w = t.shape[2]
                a, b = 0 if a is None else a, w if b is None else b
                if isinstance(i, int):
                    return t[:, i, a:b]
                return t[:, bass.ds(i, 1), a:b].rearrange("p a t -> p (a t)")

            def vcol(name, i):
                return V(name, i) if isinstance(i, int) else vec[:, bass.ds(VOFF[name] + i, 1)]

            def mcol(i, s):
                return mod[:, i, s:s + 1] if isinstance(i, int) else \
                    mod[:, bass.ds(i, 1), s:s + 1].rearrange("p a s -> p (a s)")

            def lo(pair, src, hi_name, value, done):
                dve.wait_ge(S(hi_name), value)
                dve.tensor_tensor(pair[1], src, pair[0].bitcast(F32), ALU.subtract).then_inc(S(done), 1)

            def log1p(z, w, w2, acc):
                go(dve.tensor_scalar(w, z, 2.0, None, ALU.add)); sync()
                go(dve.reciprocal(w, w)); sync()
                go(dve.tensor_tensor(w, w, z, ALU.mult)); sync()
                go(dve.tensor_tensor(w2, w, w, ALU.mult)); sync()
                go(dve.tensor_scalar(acc, w2, 1.0 / 15, None, ALU.mult)); sync()
                for k in range(6, 0, -1):
                    go(dve.scalar_tensor_tensor(acc, acc, 1.0 / (2 * k + 1), w2, ALU.add, ALU.mult)); sync()
                go(dve.scalar_tensor_tensor(acc, acc, 1.0, w, ALU.add, ALU.mult)); sync()
                go(dve.tensor_scalar(acc, acc, 2.0, None, ALU.mult)); sync()

            def inv_sqrt(dst, total, n, eps):
                go(dve.tensor_scalar(dst, total, 1.0 / n, eps, ALU.mult, ALU.add))
                event("var_ready")
                dve.wait_ge(S("root_done"), events["var_ready"])
                go(dve.reciprocal(dst, dst)); sync()

            def layer_norm(x, total, sum_sem, centred, g, b, off):
                dve.wait_ge(S(sum_sem), 1)
                dve.scalar_tensor_tensor(x[:], bc(total[0][:, 0:T], KC), -1.0 / D, x[:], ALU.mult, ALU.add
                                         ).then_inc(S(centred), 1)
                dve.wait_ge(S(centred), 1)
                dve.wait_ge(S(sum_sem), 2)
                inv_sqrt(rstd[:], total[1][:, 0:T], D, LN_EPS)
                go(dve.tensor_tensor(x[:], x[:], bc(rstd[:], KC), ALU.mult)); sync()

                def body(c):
                    go(dve.tensor_scalar(at(x, c), at(x, c), vcol(g, off + c), vcol(b, off + c), ALU.mult, ALU.add))
                loop(KC, 1, body, tail=1)
                sync()

            def event(name):
                sync()
                dve.memset(tick[:], 0.0).then_inc(S(name), 1)
                dve.wait_ge(S(name), events.setdefault(name, 0) + 1)
                events[name] += 1
            events = {}

            for i, (sem_, n) in enumerate(((half_done, NBUF), (tile_free["D"], TILES), (tile_free["A"], TILES),
                                           (S("v_tok"), 1), (S("g_done"), 2), (S("g_used"), 2),
                                           (S("gelu_free"), 2), (S("init"), 1))):
                dve.memset(rstd[:, i:i + 1], 0.0).then_inc(sem_, n)

            ada_start(0)
            dve.wait_ge(plain_done, 2 * KC)
            for b in (0, 2, 4, 6):
                dve.tensor_copy(arow[:, b * 512:(b + 1) * 512], bank[b][0:2, :]).then_inc(S("ada_rows"), 1)
            dve.wait_ge(S("ada_cols"), 1)
            dve.wait_ge(S("vec_in"), 16)
            dve.wait_ge(S("init"), 1)
            go(dve.tensor_tensor(mod[:, 0:32, :], bank[4][:, 0:64].rearrange("p (c s) -> p c s", s=2),
                                 V("ada_b", 0, 32).unsqueeze(2).to_broadcast([P, 32, 2]), ALU.add)); sync()
            go(dve.tensor_scalar(mod[:, 16:32, :], mod[:, 16:32, :], 1.0, None, ALU.add)); sync()
            for x, s, tmp, name in ((h, 0, tl_, "x_in"), (tc_, 1, tc_, "ctx_in")):
                dve.wait_ge(S(name), 16)

                def body(c, x=x, s=s, tmp=tmp):
                    go(dve.tensor_scalar(at(tmp, c), at(x, c), mcol(16 + c, s), mcol(c, s), ALU.mult, ALU.add))
                loop(KC, 1, body)
                event("xm_tmp")
            lo([xl[0][:], xl[1][:]], tl_[:], "xm_hi", 1, "xm_lat")
            lo([xc[0][:], xc[1][:]], tc_[:], "xm_hi", 2, "xm_ctx")

            dve.wait_ge(S("xm_ctx"), 1)
            s = PLAN["gates"]
            dve.wait_ge(half_done, NBUF + 2 * s.n0 + 2)
            for m in range(2):
                a = T - m * T
                ps = bank[(s.t0 + m) % TILES]
                go(dve.tensor_scalar(gi[:, a:a + T], ps[0:64, 0:T], vec[0:64, VOFF["gate_b"]:VOFF["gate_b"] + 1], None,
                                     ALU.add))
                dve.tensor_copy(gf[:, a:a + T], ps[64:128, 0:T]).then_inc(tile_free["D"], 1)
            dve.wait_ge(tile_free["D"], TILES + 2)
            go(dve.tensor_scalar(gf[:], gf[:], vec[0:64, VOFF["gate_b"] + 1:VOFF["gate_b"] + 2], None, ALU.add)); sync()
            go(dve.scalar_tensor_tensor(gt[:], gf[:], -1.0, gf[:], ALU.mult, ALU.max))
            event("gate_abs")
            dve.wait_ge(S("gate_exp"), 1)
            log1p(gw[:], gt[:], gp[:], gq[:])
            go(dve.tensor_scalar(gf[:], gf[:], 0.0, None, ALU.min)); sync()
            go(dve.tensor_tensor(gf[:], gf[:], gq[:], ALU.subtract))
            go(dve.memset(gp[:], 0.0)); sync()

            def scan(dst, src, other, op, init):
                go(dve.tensor_tensor_scan(dst[0:4, :], src[0:4, :], other[0:4, :], init, op, op))
                go(dve.tensor_tensor_scan(dst[32:36, T - 1::-1], src[32:36, T - 1::-1], other[32:36, T - 1::-1],
                                          init, op, op)); sync()
                go(dve.tensor_tensor_scan(dst[32:36, 2 * T - 1:T - 1:-1], src[32:36, 2 * T - 1:T - 1:-1],
                                          other[32:36, 2 * T - 1:T - 1:-1], dst[32:36, 0:1], op, op)); sync()
            scan(gt, gf, gp, ALU.add, 0.0)
            go(dve.tensor_tensor(gi[:], gi[:], gt[:], ALU.subtract))
            event("a_rows")
            scan(gw, gi, gi, ALU.max, 0.0)
            go(dve.tensor_copy(mrow[:], gw[:, T:2 * T]))
            go(dve.tensor_tensor(erow[:], gw[:, T:2 * T], gt[:, T:2 * T], ALU.add))
            sync()
            go(dve.tensor_scalar(erow[:], erow[:], -88.0, None, ALU.max))
            event("m_rows")
            dve.wait_ge(S("a_cols"), 1)
            go(dve.tensor_copy(acol[:].rearrange("p d t h -> p (d t h)"), bank[5][:, 0:32])); sync()

            s = PLAN["v"]

            def v_body(it):
                for j in range(s.npi):
                    ada(s, j, it)
                    dve.wait_ge(half_done, NBUF + 2 * (s.n0 + j + it * s.npi) + 2)
                    for m in range(2):
                        dve.tensor_copy(vst[:, j % 2, m, :], bank[(s.t0 + 2 * j + m) % TILES][:, 0:T]
                                        ).then_inc(tile_free["D"], 1)
                    dve.wait_ge(S("vt_done"), j + 1 + it * s.npi)
                    dve.tensor_copy(vv[:, :, bass.ds((it * s.npi + j) * P, P)],
                                    bank[6][:].rearrange("p (t f) -> p t f", t=4)).then_inc(S("v_tok"), 1)
            with dve.Fori(0, s.iters) as it:
                v_body(it)

            def conv3(name, dst, i, ps, a):
                go(dve.tensor_scalar(at(dst, i, a, a + T), ps, vcol(name, 8 + i), None, ALU.mult)); sync()
                go(dve.scalar_tensor_tensor(at(dst, i, a + 1, a + T), ps[:, 0:T - 1], vcol(name, i),
                                            at(dst, i, a + 1, a + T), ALU.mult, ALU.add)); sync()
                return dve.scalar_tensor_tensor(at(dst, i, a, a + T - 1), ps[:, 1:T], vcol(name, 16 + i),
                                                at(dst, i, a, a + T - 1), ALU.mult, ALU.add)
            s = PLAN["k"]

            def k_body(it):
                for j in range(s.npi):
                    ada(s, j, it)
                    dve.wait_ge(half_done, NBUF + 2 * (s.n0 + j + it * s.npi) + 2)
                    for m in range(2):
                        conv3("conv_k", kk, it * s.npi + j, bank[(s.t0 + 2 * j + m) % TILES][:, 0:T], T - m * T
                              ).then_inc(tile_free["D"], 1)
            ada_start(1)
            loop(s.iters, 4 * s.npi, k_body)
            ada_start(2)
            run("q", lambda i, ps, _: conv3("conv_q", qq, i, ps, 0), per=2 * 4)
            ada_only("o")
            ada_start(3)
            ada_only("zm")
            dve.wait_ge(half_done, NBUF + 2 * PLAN["q"].n0)
            go(dve.memset(upad[:], 0.0)); sync()
            run("up", lambda i, ps, _: dve.tensor_copy(
                at(upad, i).rearrange("p (r c) -> p r c", r=4)[:, :, PAD:PAD + ROW],
                ps.rearrange("p (r c) -> p r c", r=4)))
            dve.wait_ge(tile_free["D"], TILES + PLAN["zp"].td)
            dve.wait_ge(S("ada_sum"), 4)
            go(dve.tensor_tensor(mod[:, 32:96, 0], bank[4][:, 64:128], V("ada_b", 32, 64), ALU.add)); sync()
            go(dve.tensor_scalar(mod[:, 64:80, 0], mod[:, 64:80, 0], 1.0, None, ALU.add))
            pa, pb_ = ps_[0], ps_[1]
            for g in range(4):
                u = upad[:, 2 * g:2 * g + 2, :].rearrange("p c (r w) -> p (c r) w", r=4)
                go(dve.tensor_tensor(pa[:, :, 1:80], u[:, :, 0:79], u[:, :, 1:80], ALU.add)); sync()
                res, oth = pa, pb_
                for half, a, b in ((1, 2, 79), (2, 4, 77), (4, 8, 73))[:g]:
                    go(dve.tensor_tensor(oth[:, :, a:b], res[:, :, a - half:b - half], res[:, :, a + half:b + half],
                                         ALU.add)); sync()
                    res, oth = oth, res
                go(dve.tensor_tensor(oth[:, :, 0:ROW], res[:, :, PAD:PAD + ROW],
                                     bc(C("invcnt", g * ROW, (g + 1) * ROW), 8), ALU.mult)); sync()
                go(dve.tensor_tensor(u[:, :, PAD:PAD + ROW], oth[:, :, 0:ROW], u[:, :, PAD:PAD + ROW], ALU.subtract))
                sync()
            event("pooled")
            dve.wait_ge(plain_done, 97)
            dve.wait_ge(tile_free["A"], TILES + PLAN["poolw"].ta)
            for c in range(8):
                go(dve.scalar_tensor_tensor(silp[:, c, :], bank[c // 2][:, (c % 2) * T:(c % 2 + 1) * T],
                                            V("pool_s", c), silp[:, c, :], ALU.mult, ALU.mult))
            event("yp_done")

            tri = {0: C("tri_u"), 1: C("tri_l")}

            def h_math(i):
                hd, d = i // 2, i % 2
                num, den = bank[2 * (i % 2)], bank[2 * (i % 2) + 1]
                dve.wait_ge(S("num_done"), i + 1)
                go(dve.scalar_tensor_tensor(dn[:], den[:, 0:T], -1.0, ebc[i % 2][:], ALU.mult, ALU.max)); sync()
                go(dve.tensor_tensor(dn2[:], den[:, 0:T], dn[:], ALU.max)); sync()
                go(dve.reciprocal(dn[:], dn2[:])); sync()
                dst = hs[:, 2 * hd:2 * hd + 2, :] if d == 0 else ht[:]
                dve.tensor_tensor(dst, num[:].rearrange("p (c t) -> p c t", c=2), bc(dn[:], 2), ALU.mult
                                  ).then_inc(S("num_used"), 1)
                dve.wait_ge(S("num_used"), i + 1)
                if d == 1:
                    go(dve.tensor_tensor(hs[:, 2 * hd:2 * hd + 2, :], hs[:, 2 * hd:2 * hd + 2, :], ht[:], ALU.add))
                    sync()

            for i in range(2 * NH):
                hd, d = i // 2, i % 2
                dve.wait_ge(S("bc_done"), i + 1)
                for t in range(4):
                    go(dve.tensor_scalar(pt[i % 2][:, t, :], bank[7][:, 0:T], acol[:, d, t, hd:hd + 1], 0.0,
                                         ALU.subtract, ALU.max))
                dve.tensor_copy(ebc[i % 2][:], bank[7][:, T:2 * T]).then_inc(S("bc_used"), 1)
                dve.wait_ge(S("bc_used"), i + 1)
                event("args")
                dve.wait_ge(S("gexp"), i + 1)
                a = pt[i % 2]
                for t, q in ((2, 0), (3, 1)):
                    go(dve.tensor_tensor(a[:, t, q * P:(q + 1) * P], a[:, t, q * P:(q + 1) * P], tri[d], ALU.mult))
                sync()
                if d == 0:
                    dve.wait_ge(S("scores_done"), hd + 1)
                for b in range(2):
                    go(dve.scalar_tensor_tensor(a[:, 2 * b:2 * b + 2, :],
                                                bank[5 + b][:].rearrange("p (t q) -> p t q", t=2), 1.0 / 16,
                                                a[:, 2 * b:2 * b + 2, :], ALU.mult, ALU.mult))
                event("probs_ready")
                if i >= 1:
                    h_math(i - 1)
            h_math(2 * NH - 1)
            go(dve.tensor_tensor(hs[:], hs[:], sigo[:], ALU.mult))
            sync()
            dve.memset(tick[:], 0.0).then_inc(S("hn_in"), 1)
            dve.wait_ge(S("hn_sum"), 1)

            def by_head(t, b):
                return t[:, 4 * b:4 * b + 4, :].rearrange("p (g c) t -> p g c t", c=2)
            for g in range(NH):
                tot = bank[5 + g // 2][:, (g % 2) * T:(g % 2 + 1) * T]
                go(dve.scalar_tensor_tensor(hs[:, 2 * g:2 * g + 2, :], bc(tot, 2), -1.0 / 256,
                                            hs[:, 2 * g:2 * g + 2, :], ALU.mult, ALU.add))
            event("hc")
            dve.wait_ge(S("hn_sum"), 2)
            for b in range(2):
                go(dve.tensor_scalar(flat(hr[:, 2 * b:2 * b + 2, :]), bank[5 + b][:], 1.0 / 256, LN_EPS,
                                     ALU.mult, ALU.add))
            event("var_ready")
            dve.wait_ge(S("root_done"), events["var_ready"])
            go(dve.reciprocal(hr[:], hr[:])); sync()
            for b in range(2):
                go(dve.tensor_tensor(by_head(hs, b), by_head(hs, b),
                                     hr[:, 2 * b:2 * b + 2, :].unsqueeze(2).to_broadcast([P, 2, 2, T]), ALU.mult))
            sync()
            for c in range(8):
                go(dve.scalar_tensor_tensor(silm[:, c, :], hs[:, c, :], V("mh_g", c), silm[:, c, :],
                                            ALU.mult, ALU.mult))
            event("y0")
            lo([xl[0][:], xl[1][:]], y0[:], "y0_hi", 1, "y0_ready")

            dve.wait_ge(S("ax0"), 1)
            run("out0", lambda i, ps, _: dve.scalar_tensor_tensor(at(h, i), ps, mcol(32 + i, 0), at(h, i),
                                                                  ALU.mult, ALU.add))
            layer_norm(h, (bank[5], bank[6]), "ln0_sum", "ln0_c", "pln_g", "pln_b", 0)
            if not upto("v1"):
                event("final")
                return

            def body(c):
                go(dve.tensor_scalar(at(tx, c), at(h, c), mcol(64 + c, 0), mcol(48 + c, 0), ALU.mult, ALU.add))
            loop(KC, 1, body)
            event("xm1_tmp")
            lo([xl[0][:], xl[1][:]], tx[:], "xm1_hi", 1, "xm1")
            run("v1", lambda i, ps, _: dve.tensor_copy(at(vf, i), ps))
            layer_norm(vf, (bank[5], bank[6]), "lnv_sum", "lnv_c", "sgu_g", "sgu_b", 0)
            event("v1_norm")
            run("u1", lambda i, ps, _: dve.tensor_copy(at(uu, i), ps))
            for g in range(8):
                dve.wait_ge(S("v1_tp"), g + 1)
                dve.tensor_copy(vt1[:, g // 4, (g % 4) * 512:(g % 4 + 1) * 512], bank[5 + g % 2][:]
                                ).then_inc(S("v1_tok"), 1)
            for c in range(KC):
                if c < KC - 1:
                    dve.wait_ge(S("sgu_done"), c + 1)
                else:
                    dve.wait_ge(plain_done, PLAN["wsp"].p0 + 1)
                dve.tensor_tensor(uu[:, c, :], uu[:, c, :], bank[4 + c % 4][:, 0:T], ALU.mult
                                  ).then_inc(S("sgu_used"), 1)
            dve.wait_ge(S("sgu_used"), KC)
            dve.wait_ge(tile_free["A"], TILES + PLAN["wsp"].ta)
            go(dve.tensor_tensor(uu[:], uu[:], zz[:], ALU.mult))
            event("y1")
            lo([yh[0][:], yh[1][:]], uu[:], "y1_hi", 1, "y1_ready")
            dve.wait_ge(S("ax1"), 1)
            run("out1", lambda i, ps, _: dve.scalar_tensor_tensor(at(h, i), ps, mcol(80 + i, 0), at(h, i),
                                                                  ALU.mult, ALU.add))
            layer_norm(h, (bank[5], bank[6]), "ln1_sum", "ln1_c", "pln_g", "pln_b", 16)
            if not upto("cc"):
                event("final")
                return
            event("h_ready")

            def normed(i, g, dst):
                dve.wait_ge(S("rms_sum"), i)
                inv_sqrt(rstd[:], bank[7][:, 0:T], D, RMS_EPS)

                def body(c):
                    go(dve.scalar_tensor_tensor(at(dst, c), at(h, c), vcol(g, c), rstd[:], ALU.mult, ALU.mult))
                loop(KC, 1, body)
            normed(1, "attn_n", rt)
            event("rms_t")
            lo([xl[0][:], xl[1][:]], rt[:], "n2_hi", 1, "n2")
            run("cc", lambda i, ps, _: dve.tensor_copy(at(cr, i), ps))
            dve.wait_ge(tile_free["D"], TILES + PLAN["uv"].td)
            event("c_evac")
            dve.wait_ge(S("c_sum"), 2)
            for b, n, a, name in ((5, 6, 0, "q_n"), (6, 4, 6, "kv_n")):
                inv_sqrt(rstd[:], bank[b][:, 0:T], n * P, RMS_EPS)
                for c in range(n):
                    go(dve.scalar_tensor_tensor(cr[:, a + c, :], cr[:, a + c, :], V(name, c), rstd[:],
                                                ALU.mult, ALU.mult))
                sync()
            event("c_norm")
            lo([cn[0][:], cn[1][:]], cr[:, 0:10, :], "cn_hi", 1, "cn_ready")

            def c2(name):
                return con2[:, C2OFF[name]:C2OFF[name] + dict(CON2)[name]]

            def rotate(x, value):
                dve.wait_ge(S("rope_done"), value)
                ps = bank[7] if value == 1 else bank[5 + value % 2]
                go(dve.tensor_tensor(rr[:], ps[:, 0:T], c2("sin"), ALU.mult))
                go(dve.tensor_tensor(x, x, c2("cos"), ALU.mult)); sync()
                ins = dve.tensor_tensor(x, x, rr[:], ALU.add).then_inc(S("rope_used"), 1)
                dve.wait_ge(S("rope_used"), value)
                return ins
            dve.wait_ge(S("con2_in"), 16)
            rotate(cr[:, 10, :], 1)
            go(dve.memset(kpe[:], 0.0)); sync()
            for a in range(2):
                go(dve.tensor_copy(kpe[64 * a:64 * a + 64, a, :], cr[64 * a:64 * a + 64, 10, :]))
            sync()
            dve.wait_ge(S("cn_ready"), 1)
            run("uv", lambda i, ps, _: dve.tensor_copy(at(v2f, i), ps))
            run("uk", lambda i, ps, _: dve.tensor_copy(at(kn, i), ps))
            for g in range(8):
                dve.wait_ge(S("v2_tp"), g + 1)
                dve.tensor_copy(vt2[:, g // 4, (g % 4) * 512:(g % 4 + 1) * 512], bank[5 + g % 2][:]
                                ).then_inc(S("v2_tok"), 1)
            run("uq", lambda i, ps, _: dve.tensor_copy(at(q2, i), ps))
            dve.wait_ge(tile_free["D"], TILES + PLAN["ao"].td)
            for j in range(8):
                rotate(q2[:, 16 + j, :], j + 2)

            def att_mask(hd):
                dve.wait_ge(S("att_s"), hd + 1)
                dve.scalar_tensor_tensor(flat(sm[hd % 2][:]), bank[hd % 2][:], SCALE, c2("causal"), ALU.mult, ALU.add
                                         ).then_inc(S("att_masked"), 1)
                dve.wait_ge(S("att_masked"), hd + 1)
                m = mx[:, 2 * (hd % 4):2 * (hd % 4) + 2]
                go(dve.tensor_reduce(m, sm[hd % 2][:], AX, ALU.max)); sync()
                go(dve.tensor_scalar(m, m, -1.0, None, ALU.mult))
                event("att_max")

            def att_norm(hd):
                dve.wait_ge(S("att_exp"), 2 * hd + 2)
                a = 2 * (hd % 4)
                go(dve.reciprocal(mx[:, 32 + a:34 + a], mx[:, 16 + a:18 + a])); sync()
                for t in range(2):
                    go(dve.tensor_scalar(sm[hd % 2][:, t, :], sm[hd % 2][:, t, :], mx[:, 32 + a + t:33 + a + t], None,
                                         ALU.mult))
                event("att_p")
                dve.wait_ge(S("att_tp"), hd + 1)
                dve.tensor_copy(flat(ptt[hd % 2][:]), bank[2][:]).then_inc(S("att_pt"), 1)

            def att_out(hd):
                dve.wait_ge(S("att_o"), hd + 1)
                dve.tensor_copy(q2[:, hd, :], bank[5 + hd % 2][:, 0:T]).then_inc(S("att_o_used"), 1)

            dve.wait_ge(S("cn_ready"), 1)
            for i in range(HEADS + 2):
                if i < HEADS:
                    att_mask(i)
                if 1 <= i <= HEADS:
                    att_norm(i - 1)
                if i >= 2:
                    att_out(i - 2)
            dve.wait_ge(S("att_o_used"), HEADS)
            lo([oh[0][:], oh[1][:]], q2[:, 0:KC, :], "o_hi", 1, "o_ready")
            run("ao", lambda i, ps, _: dve.tensor_copy(at(ya, i), ps))

            s1, s2, s3 = (rw[:, 3, i * KC:(i + 1) * KC] for i in range(3))
            go(dve.scalar_tensor_tensor(lam_s[:], V("lam", 0, KC), -1.0, V("lam", 0, KC), ALU.mult, ALU.max))
            event("lam_abs")

            def conv4(i, ps, _):
                x = at(xcv, i)
                go(dve.tensor_scalar(x, ps, vcol("conv_w", 48 + i), vcol("conv_b", i), ALU.mult, ALU.add)); sync()
                for j in (2, 1, 0):
                    ins = dve.scalar_tensor_tensor(at(xcv, i, 3 - j, T), ps[:, 0:T - 3 + j], vcol("conv_w", 16 * j + i),
                                                   at(xcv, i, 3 - j, T), ALU.mult, ALU.add)
                    if j:
                        go(ins); sync()
                return ins
            run("xr", conv4, per=3 * 4)
            dve.wait_ge(S("lam_exp"), 1)
            log1p(lam_s[:], s1, s2, s3)
            go(dve.tensor_scalar(s1, V("lam", 0, KC), -1.0, 0.0, ALU.mult, ALU.max)); sync()
            go(dve.tensor_tensor(lam_s[:], s1, s3, ALU.add)); sync()
            go(dve.tensor_scalar(lam_s[:], lam_s[:], -8.0, None, ALU.mult)); sync()
            for c in range(KC):
                dve.wait_ge(S("rg_r"), c + 1)
                go(dve.tensor_scalar(la[:, c, :], xr[:, c, :], lam_s[:, c:c + 1], None, ALU.mult))
                dve.wait_ge(S("rg_used"), c + 1)
                dve.tensor_tensor(xcv[:, c, :], xcv[:, c, :], rw[:, c % 2, :], ALU.mult).then_inc(S("ix_used"), 1)
            event("la_ready")
            dve.wait_ge(S("a_ready"), 2)
            for c in range(KC):
                go(dve.tensor_scalar(rw[:, c % 2, :], la[:, c, :], -1.0, 1.0, ALU.mult, ALU.add)); sync()
                go(dve.reciprocal(rw[:, 2 + c % 2, :], rw[:, c % 2, :])); sync()
                go(dve.scalar_tensor_tensor(la[:, c, :], la[:, c, :], -2.0, rw[:, 2 + c % 2, :], ALU.mult, ALU.mult))
            sync()
            go(dve.tensor_scalar(flat(la[:]), flat(la[:]), 1e-30, None, ALU.max))
            event("m2_ready")
            dve.wait_ge(S("mult_ready"), 1)
            go(dve.memset(la[:, :, 0:1], 1.0)); sync()
            dve.wait_ge(S("ix_used"), KC)
            go(dve.tensor_tensor(xcv[:], xcv[:], la[:], ALU.mult)); sync()
            for c in range(KC):
                go(dve.tensor_tensor_scan(la[:, c, :], xr[:, c, :], xcv[:, c, :], 0.0, ALU.mult, ALU.add))
            event("scanned")
            dve.wait_ge(tile_free["A"], TILES + PLAN["yr"].ta)
            go(dve.tensor_tensor(ya[:], ya[:], yr[:], ALU.mult))
            event("ga_used")
            dve.wait_ge(tile_free["A"], TILES + PLAN["gr"].ta)
            go(dve.tensor_tensor(yr[:], yr[:], la[:], ALU.mult))
            event("ry_t")
            lo([ry[0][:], ry[1][:]], yr[:], "ry_hi", 1, "ry_ready")
            dve.wait_ge(tile_free["A"], TILES + PLAN["ro"].ta)

            def mix(i, ps, k):
                go(dve.tensor_tensor(rw[:, k % 2, :], ps, at(xr, i), ALU.mult)); sync()
                return dve.tensor_tensor(at(ya, i), at(ya, i), rw[:, k % 2, :], ALU.add)
            run("ro", mix, per=4)
            dve.wait_ge(tile_free["D"], TILES + PLAN["wo"].td)
            event("mix_t")
            lo([mt[0][:], mt[1][:]], ya[:], "mix_hi", 1, "mix_ready")

            def add_h(i, ps, _):
                return dve.tensor_tensor(at(h, i), ps, at(h, i), ALU.add)
            run("wo", add_h)
            dve.wait_ge(tile_free["D"], TILES + PLAN["pq"].td)
            if not upto("pq"):
                event("final")
                return
            event("h_ready")

            normed(2, "ffn_n", rt)
            event("rms_t")
            lo([xl[0][:], xl[1][:]], rt[:], "n2_hi", 2, "n2")
            run("pq", lambda i, ps, _: dve.tensor_copy(at(pqq, i), ps))
            for g in range(8):
                if g < 7:
                    dve.wait_ge(S("s_done"), g + 1)
                else:
                    dve.wait_ge(plain_done, PLAN["sk"].p0 + 1)
                dve.tensor_copy(flat(ss[:, g // 4, 4 * (g % 4):4 * (g % 4) + 4, :]), bank[5 + g % 2][:]
                                ).then_inc(S("s_evac"), 1)
            dve.wait_ge(S("s_evac"), 8)

            def top16(rows, vals, idx):
                for r in range(2):
                    for x, v, _ in zip(rows, vals, idx):
                        go(dve.max(v[:, 8 * r:8 * r + 8], x))
                    sync()
                    for x, v, i in zip(rows, vals, idx):
                        go(dve.max_index(i[:, 8 * r:8 * r + 8], v[:, 8 * r:8 * r + 8], x))
                    sync()
                    if r == 0:
                        for x, v, _ in zip(rows, vals, idx):
                            go(dve.match_replace(x, v[:, 0:8], x, -BIG))
                        sync()
            pairs = [(t, c) for t in range(2) for c in range(16)]
            top16([ss[:, t, c, :] for t, c in pairs], [tv[:, t, c, :] for t, c in pairs],
                  [ti[:, t, c, :] for t, c in pairs])
            go(dve.tensor_copy(tf[:], ti[:])); sync()
            four = [P, 8, TOPK, TOPK]
            for t in range(2):
                v2 = tv[:, t, :, :].rearrange("p (h c) k -> p h c k", c=2)
                i2 = tf[:, t, :, :].rearrange("p (h c) k -> p h c k", c=2)
                go(dve.tensor_tensor(cand[:].rearrange("p h (a b) -> p h a b", a=TOPK),
                                     v2[:, :, 0, :].unsqueeze(3).to_broadcast(four),
                                     v2[:, :, 1, :].unsqueeze(2).to_broadcast(four), ALU.add)); sync()
                top16([cand[:, k, :] for k in range(8)], [bv[:, t, k, :] for k in range(8)],
                      [bi[:, t, k, :] for k in range(8)])
                dst = gg[:, t, 2, :, :]
                go(dve.tensor_copy(dst, bv[:, t, :, 0:1].to_broadcast([P, 8, TOPK]))); sync()
                go(dve.tensor_tensor(bv[:, t, :, :], bv[:, t, :, :], dst, ALU.subtract))
                event("gate_d")
                for c in range(2):
                    if c == 0:
                        go(dve.tensor_scalar(bj[:, t, :, :], bi[:, t, :, :], 4, None, ALU.logical_shift_right))
                    else:
                        go(dve.tensor_scalar(bj[:, t, :, :], bi[:, t, :, :], 15, None, ALU.bitwise_and))
                    sync()
                    go(dve.tensor_copy(bf[:, t, :, :], bj[:, t, :, :])); sync()
                    e = ceq[:].rearrange("p h (k a) -> p h k a", k=TOPK)
                    for k in range(8):
                        go(dve.tensor_tensor(e[:, k], bf[:, t, k, :].unsqueeze(2).to_broadcast([P, TOPK, TOPK]),
                                             bc(C("iota", 0, TOPK), TOPK), ALU.is_equal))
                    sync()
                    go(dve.tensor_tensor(e, e, i2[:, :, c, :].unsqueeze(2).to_broadcast(four), ALU.mult)); sync()
                    go(dve.tensor_reduce(gg[:, t, c, :, :], e, AX, ALU.add)); sync()
                dve.wait_ge(S("gate_e"), t + 1)
                go(dve.tensor_reduce(gs[:, t, 0, :], bv[:, t, :, :], AX, ALU.add)); sync()
                go(dve.reciprocal(gs[:, t, 1, :], gs[:, t, 0, :])); sync()
                go(dve.tensor_tensor(dst, bv[:, t, :, :], gs[:, t, 1, :].unsqueeze(2).to_broadcast([P, 8, TOPK]),
                                     ALU.mult))
                event("gates_tok")
            dve.wait_ge(S("gT_done"), 1)
            for t in range(2):
                dve.tensor_copy(gT[:, :, t * P:(t + 1) * P], bank[5 + t][:, 0:3 * P].rearrange("p (i t) -> p i t", i=3)
                                ).then_inc(S("gT_read"), 1)
            dve.wait_ge(S("gT_read"), 2)
            for r in range(2):
                def hot2(it, r=r):
                    for k in range(2):
                        dve.wait_ge(S("g_done"), r * (T // TG) + k + 1 + it * 2)
                        tok = it * (2 * TG) + k * TG
                        dve.tensor_tensor(oa[k][:], bc(C("iota"), TG), gT[:, 0, bass.ds(tok, TG)].unsqueeze(2)
                                          .to_broadcast([P, TG, NKEY]), ALU.is_equal).then_inc(S("hot1"), 1)
                        go(dve.tensor_tensor(ob[k][:], bc(C("iota", r * I2, (r + 1) * I2), TG),
                                             gT[:, 1, bass.ds(tok, TG)].unsqueeze(2).to_broadcast([P, TG, I2]),
                                             ALU.is_equal)); sync()
                        dve.tensor_tensor(ob[k][:], ob[k][:],
                                          gT[:, 2, bass.ds(tok, TG)].unsqueeze(2).to_broadcast([P, TG, I2]),
                                          ALU.mult).then_inc(S("hot2"), 1)
                loop(T // TG // 2, 2, hot2)
                dve.wait_ge(S("g_used"), (r + 1) * (T // TG) + 2)
                s = PLAN[f"peer_u{r}"]

                def w_body(it, r=r, s=s):
                    for j in range(4):
                        dve.wait_ge(tile_free["A"], TILES + s.ta + j + 1 + it * 4)
                        i = it * 4 + j
                        dve.tensor_tensor(at(W, i), at(W, i), gl[j % 2][:], ALU.mult).then_inc(S("gelu_free"), 1)
                loop(s.iters, 0, w_body)
                dve.wait_ge(S("gelu_free"), (r + 1) * I2 + 2)

                def wl_body(it, r=r):
                    for j in range(4):
                        i = it * 4 + j
                        dve.wait_ge(S("wr_hi"), r * I2 + j + 1 + it * 4)
                        dve.tensor_tensor(wr[j % 2][:, 1, :], at(W, i), wr[j % 2][:, 0, :].bitcast(F32), ALU.subtract
                                          ).then_inc(S("wr_ready"), 1)
                loop(s.iters, 0, wl_body)
                s = PLAN[f"peer_v{r}"]
                dve.wait_ge(half_done, NBUF + 2 * (s.n0 + s.npi * s.iters))
                for b in range(8):
                    ins = dve.tensor_tensor(flat(h[:, 2 * b:2 * b + 2, :]), flat(h[:, 2 * b:2 * b + 2, :]), bank[b][:],
                                            ALU.add)
                ins.then_inc(S("acc_used"), 1)
                dve.wait_ge(S("acc_used"), r + 1)
            event("h_ready")

            normed(3, "ple_n", rt)
            event("rms_t")
            lo([xl[0][:], xl[1][:]], rt[:], "n2_hi", 3, "n2")
            lo([pt_r[:, 0, :, :], pt_r[:, 1, :, :]], pt_x[:], "p_hi", 1, "p_ready")
            dve.wait_ge(tile_free["A"], TILES + PLAN["pp"].ta)

            def ple(i, ps, k):
                go(dve.tensor_tensor(ptile[:, k % 2, :], ps, at(sg, i), ALU.mult)); sync()
                return dve.tensor_tensor(at(h, i), at(h, i), ptile[:, k % 2, :], ALU.add)
            run("pp", ple, per=16)
            dve.wait_ge(tile_free["D"], TILES + PLAN["pp"].td + 16)
            event("h_ready")
            normed(4, "fin_n", h)
            event("final")


PER_TILE = {"uv": 4, "uk": 4, "uq": 6, "pp": 2}


def columns(v):
    return np.asarray(v).reshape(-1, P).T


def units(w, per=1):
    k, n = w.shape
    a = w.reshape(k // P, P, n // P // per, per, P).transpose(2, 1, 3, 0, 4)
    return a.reshape(n // P // per, P, -1)


def feature_major(x):
    return np.ascontiguousarray(np.asarray(x).reshape(x.shape[0], -1, P).transpose(2, 1, 0))


def constants():
    c = {"ident": np.eye(P), "ones": np.ones((P, P)), "tri_u": np.triu(np.ones((P, P))),
         "tri_l": np.tril(np.ones((P, P))), "iota": np.tile(np.arange(P), (P, 1))}
    pos = np.arange(ROW)
    inv = []
    for w in (2, 4, 8, 16):
        low, high = np.maximum(pos - w // 2, 0), np.minimum(pos + (w - 1 - w // 2), ROW - 1)
        inv.append(1.0 / (high - low + 1))
    c["invcnt"] = np.tile(np.concatenate(inv), (P, 1))
    inv_freq = (1.0 / (np.float32(10000.0) ** (np.arange(32, dtype=np.float32) / np.float32(32)))).astype(np.float32)
    ang = np.arange(T, dtype=np.float32)[None, :] * inv_freq[:, None]
    rot = np.zeros((P, P))
    for b in (0, 64):
        for i in range(32):
            rot[b + i + 32, b + i] = -1.0
            rot[b + i, b + i + 32] = 1.0
    q = np.arange(P)[:, None, None] + P * np.arange(2)[None, :, None]
    k = np.arange(T)[None, None, :]
    c2 = {"cos": np.tile(np.cos(ang), (4, 1)), "sin": np.tile(np.sin(ang), (4, 1)),
          "causal": np.where(k <= q, 0.0, -BIG).reshape(P, -1), "rot": rot}
    return (np.concatenate([c[n] for n, _ in CON], 1).astype(np.float32),
            np.concatenate([c2[n] for n, _ in CON2], 1).astype(np.float32))


def layout(a):
    f = np.float32
    w = np.zeros((N_UNITS, P, UNIT), f)

    def put(name, ns, ps=None):
        s = PLAN[name]
        if ns is not None:
            at = [s.u0 + it * len(s.pattern) + p for it in range(s.iters) for p in s.npos]
            w[at[:len(ns)], :, :ns.shape[2]] = ns
        if ps is not None:
            at = [s.u0 + it * len(s.pattern) + p for it in range(s.iters)
                  for p, kind in enumerate(s.pattern) if kind == "P"]
            w[at, :, :ps.shape[2]] = ps

    ada = a["ada_w"].reshape(2, KC, P, 3, D).transpose(0, 3, 1, 2, 4).reshape(6, KC, P, D)
    we = a["w_in_even"][0]
    m = D // 2
    put("ada_ss", None, ada[0:2].transpose(1, 0, 2, 3).reshape(2 * KC, P, D))
    ada = ada.reshape(6 * KC, P, D)
    g = np.zeros((D, P), f)
    gc = 5 * m
    for kind in range(2):
        for d in range(2):
            g[:, 64 * kind + 32 * d:64 * kind + 32 * d + 4] = we[:, gc + 8 * kind + 4 * d:gc + 8 * kind + 4 * d + 4]
    put("gates", units(g))
    left = 32
    cols = {"q": 0, "k": m, "v": 2 * m, "o": 3 * m, "zm": 4 * m, "up": gc + 16, "zp": gc + 16 + m}
    for name in ("v", "k", "q", "o", "zm", "up", "zp"):
        n = PLAN[name].ppi * PLAN[name].iters
        put(name, units(we[:, cols[name]:cols[name] + m]), ada[left:left + n] if n else None)
        left += n
    assert left == 96
    pw = a["pool_w"][0].reshape(4, 2, P, 2, P).transpose(2, 0, 1, 3, 4).reshape(1, P, -1)
    put("poolw", None, pw)
    put("out0", units(a["w_out_even"][0]))
    wo = a["w_in_odd"][0]
    put("u1", units(wo[:, 0:D]))
    put("v1", units(wo[:, D:2 * D]))
    put("z1", units(wo[:, 2 * D:]))
    sp = np.concatenate([a["w_sp"][0].transpose(2, 0, 1).reshape(P, -1),
                         np.broadcast_to(a["b_sp"][0].reshape(1, -1), (P, 8 * P))], 1)
    put("wsp", None, sp[None])
    put("out1", units(a["w_out_odd"][0]))
    wi = a["w_in_2"][0]
    kr = wi[:, 1280:1344]
    put("cc", units(np.concatenate([wi[:, 0:1280], kr, kr], 1)))
    o = 1344
    put("xr", units(wi[:, o:o + D]))
    put("yr", units(wi[:, o + D:o + 2 * D]))
    put("ga", units(wi[:, o + 2 * D:o + 3 * D]))
    put("gr", units(wi[:, o + 3 * D:o + 4 * D]))
    ukv = a["w_ukv_2"][0].reshape(512, HEADS, 2, P)
    put("uk", units(ukv[:, :, 0].reshape(512, D), 4))
    put("uv", units(ukv[:, :, 1].reshape(512, D), 4))
    uq = a["w_uq_2"][0].reshape(768, HEADS, 192)
    uq = np.concatenate([uq[:, :, 0:128].reshape(768, -1), uq[:, :, 128:].reshape(768, -1)], 1)
    put("uq", units(uq, 2))
    put("ao", units(a["w_attn_o_2"][0]))
    put("rg", None, np.stack([a["w_rg_a_2"][0].transpose(1, 0, 2).reshape(P, -1),
                              a["w_rg_x_2"][0].transpose(1, 0, 2).reshape(P, -1)]))
    put("ro", units(a["w_rnn_o_2"][0]))
    put("wo", units(a["w_out_2"][0]))
    put("pq", units(a["w_peer_q_2"][0]))
    put("sk", None, a["peer_subkeys_2"][0].reshape(16, NKEY, P).transpose(2, 0, 1).reshape(1, P, -1))
    pu = a["peer_u_2"][0].reshape(NKEY, NKEY, KC, P).transpose(1, 3, 2, 0).reshape(NKEY, P, -1)
    pv = a["peer_v_2"][0].reshape(NKEY, NKEY, D).transpose(1, 0, 2)
    for r in range(2):
        put(f"peer_u{r}", pu[r * I2:(r + 1) * I2])
        put(f"peer_v{r}", pv[r * I2:(r + 1) * I2])
    put("pg", units(a["w_ple_gate_2"][0]))
    put("pp", units(a["w_ple_proj_2"][0], 8))

    gb = np.zeros((2, P), f)
    for i, name in enumerate(("b_igate", "b_fgate")):
        for d in range(2):
            gb[i, 32 * d:32 * d + 4] = a[name][0, d]
    v = {"ada_b": a["ada_b"], "pln_g": a["post_ln_g"], "pln_b": a["post_ln_b"],
         "conv_q": a["conv_qk"][0][:, 0:m], "conv_k": a["conv_qk"][0][:, m:], "mh_g": a["mh_norm_g"],
         "pool_s": a["pool_scale"], "sgu_g": a["sgu_ln_g"], "sgu_b": a["sgu_ln_b"], "gate_b": gb,
         "attn_n": a["attn_norm_2"], "b_gate": a["b_gate_2"], "q_n": a["q_norm_2"], "kv_n": a["kv_norm_2"],
         "conv_w": a["conv_w_2"], "conv_b": a["conv_b_2"], "b_ra": a["b_rg_a_2"], "b_rx": a["b_rg_x_2"],
         "lam": a["lru_lambda_2"], "ffn_n": a["ffn_norm_2"], "ple_n": a["ple_norm_2"], "fin_n": a["final_norm_2"]}
    vecs = np.ascontiguousarray(np.concatenate([columns(np.ascontiguousarray(v[n])) for n, _ in VEC], 1))
    con, con2 = constants()
    cond = np.ascontiguousarray(np.stack([columns(a["c"][0]), columns(a["c_ctx"])], 2))
    return {"w": w, "vec": vecs, "con": con, "con2": con2, "cond": cond, "xT": feature_major(a["x"][0]),
            "ctxT": feature_major(a["ctx"][0]), "pT": feature_major(a["p_2"][0, 0])}


STOP = None


def kernel(**inputs):
    import concourse.bacc as bacc
    from concourse.bass_utils import run_bass_kernel_spmd

    arrays = layout({k: np.asarray(v) for k, v in inputs.items()})
    nc = bacc.Bacc("TRN2", target_bir_lowering=False, num_devices=1)
    aps = {k: nc.dram_tensor(f"in_{k}", v.shape, mybir.dt.from_np(v.dtype), kind="ExternalInput").ap()
           for k, v in arrays.items()}
    out = nc.dram_tensor("out_0", (P, KC, T), F32, kind="ExternalOutput").ap()
    program(nc, aps, out, stop=STOP)
    r = run_bass_kernel_spmd(nc, [{f"in_{k}": v for k, v in arrays.items()}], core_ids=[0])
    y = r.results[0]["out_0"]
    return np.ascontiguousarray(y.transpose(2, 1, 0)).reshape(1, T, D)
```

```python
from contextlib import ExitStack

import numpy as np
import concourse.bass as bass
from concourse import mybir

F32 = mybir.dt.float32
F32R = mybir.dt.float32r
U32 = mybir.dt.uint32
BF16 = mybir.dt.bfloat16
ALU = mybir.AluOpType
ACT = mybir.ActivationFunctionType
AX = mybir.AxisListType.X

P = 128
T = 256
D = 2048
KC = D // P
RING = 4
UNIT = 2048
NBUF = 4
HALF = UNIT // 2
TILES = 4
NH = 4
ALPHA = 4.0 ** 0.25
LN_EPS = 1e-5
RMS_EPS = 1e-6
ROW = 64
PAD = 8
ROWP = ROW + 2 * PAD
HEADS = 16
TOPK = 16
NKEY = 128
I2 = NKEY // 2
TG = 8
GR = 4
NG = KC // GR
BIG = 3.0e38
SCALE = 192.0 ** -0.5

VEC = [("ada_b", 96), ("pln_g", 32), ("pln_b", 32), ("conv_q", 24), ("conv_k", 24), ("mh_g", 8), ("pool_s", 8),
       ("sgu_g", 16), ("sgu_b", 16), ("gate_b", 2), ("attn_n", 16), ("b_gate", 32), ("q_n", 6), ("kv_n", 4),
       ("conv_w", 64), ("conv_b", 16), ("b_ra", 16), ("b_rx", 16), ("lam", 16), ("ffn_n", 16), ("ple_n", 16),
       ("fin_n", 16)]
VOFF, NVEC = {}, 0
for _n, _c in VEC:
    VOFF[_n] = NVEC
    NVEC += _c

CON = [("ident", 128), ("ones", 128), ("tri_u", 128), ("tri_l", 128), ("invcnt", 4 * ROW), ("iota", 128)]
COFF, NCON = {}, 0
for _n, _c in CON:
    COFF[_n] = NCON
    NCON += _c
CON2 = [("cos", 256), ("sin", 256), ("causal", 512), ("rot", 128)]
C2OFF, NCON2 = {}, 0
for _n, _c in CON2:
    C2OFF[_n] = NCON2
    NCON2 += _c

STAGES = [
    ("ada_ss", "PPPP", 8, 0, "D"),
    ("gates", "N", 1, 2, "D"),
    ("v", "NPPNPPNPPNPP", 2, 2, "D"),
    ("k", "NPPNPPNPPNPP", 2, 2, "D"),
    ("q", "NNPNNPNNPNNP", 1, 1, "D"),
    ("o", "NNPNNPNNPNNP", 1, 1, "A"),
    ("zm", "NNPNNPNNPNNP", 1, 1, "A"),
    ("up", "NNPNNPNNPNNP", 1, 1, "D"),
    ("zp", "NNNN", 2, 1, "A"),
    ("poolw", "P", 1, 0, "D"),
    ("out0", "NPNPNPNP", 4, 1, "D"),
    ("v1", "NNNN", 4, 1, "D"),
    ("u1", "NNNN", 4, 1, "D"),
    ("z1", "NNNN", 4, 1, "A"),
    ("wsp", "P", 1, 0, "D"),
    ("out1", "NNNN", 4, 1, "D"),
    ("cc", "N" * 11, 1, 1, "D"),
    ("uv", "NNNN", 1, 4, "D"),
    ("uk", "NNNN", 1, 4, "D"),
    ("uq", "NNNN", 3, 2, "D"),
    ("ao", "NNNN", 4, 1, "D"),
    ("xr", "NNNN", 4, 1, "D"),
    ("rg", "PP", 1, 0, "D"),
    ("ga", "NNNN", 4, 1, "A"),
    ("yr", "NNNN", 4, 1, "A"),
    ("gr", "NNNN", 4, 1, "A"),
    ("ro", "NNNN", 4, 1, "D"),
    ("wo", "NNNN", 4, 1, "D"),
    ("pq", "NNNN", 4, 1, "D"),
    ("sk", "P", 1, 0, "D"),
    ("peer_u0", "NNNN", I2 // 4, 1, "A"),
    ("peer_v0", "NNNN", I2 // 4, 0, "D"),
    ("peer_u1", "NNNN", I2 // 4, 1, "A"),
    ("peer_v1", "NNNN", I2 // 4, 0, "D"),
    ("pg", "NNNN", 4, 1, "A"),
    ("pp", "NN", 1, 8, "D"),
]


class Stage:
    pass


def plan():
    u = n = p = td = ta = t = 0
    out = {}
    for name, pattern, iters, tiles, eng in STAGES:
        s = Stage()
        s.name, s.pattern, s.iters, s.tiles, s.eng = name, pattern, iters, tiles, eng
        s.u0, s.n0, s.p0, s.t0, s.td, s.ta = u, n, p, t, td, ta
        s.npi, s.ppi = pattern.count("N"), pattern.count("P")
        s.k0 = (p if p < 80 else p - 1) % KC
        s.npos = [i for i, k in enumerate(pattern) if k == "N"]
        s.base = s.ta if eng == "A" else s.td
        u += len(pattern) * iters
        n += s.npi * iters
        p += s.ppi * iters
        made = s.npi * iters * tiles
        t += made
        if eng == "A":
            ta += made
        else:
            td += made
        out[name] = s
    return out, u, n


PLAN, N_UNITS, N_SPLIT = plan()
ORDER = [PLAN[s[0]] for s in STAGES]


def first_n_after(stage):
    for s in ORDER[ORDER.index(stage) + 1:]:
        if s.npi:
            return s.u0 + s.npos[0]
    return None


def program(nc, A, out):
    with ExitStack() as ctx:
        base0 = (nc.sbuf_base + 63) // 64 * 64
        at = [base0]

        def place(name, shape, dt, offset):
            return nc.alloc_sbuf_tensor_at(name, shape, dt, offset=offset)

        def fixed(name, shape, dt):
            t = place(name, shape, dt, at[0])
            at[0] += (int(np.prod(shape[1:])) * 4 + 63) // 64 * 64
            return t

        ring = [fixed(f"ring{i}", [P, UNIT], F32) for i in range(RING)]
        hb = [fixed(f"unit_hi{i}", [P, HALF], F32R) for i in range(NBUF)]
        lb = [fixed(f"unit_lo{i}", [P, HALF], F32R) for i in range(NBUF)]
        h = fixed("resid", [P, KC, T], F32)
        vec = fixed("vec", [P, NVEC], F32)
        con = fixed("con", [P, NCON], F32)
        mod = fixed("mod", [P, 96, 2], F32)
        cond = fixed("cond", [P, KC, 2], F32)
        mrow = fixed("mrow", [64, T], F32)
        erow = fixed("erow", [64, T], F32)
        acol = fixed("acol", [P, 2, 4, 4], F32)
        rstd = fixed("rstd", [P, T], F32)
        tick = fixed("tick", [1, 1], F32)
        lam_s = fixed("lam_s", [P, KC], F32)
        z0 = (at[0] + 63) // 64 * 64
        KB = 1024

        def zone(name, kb, shape, dt=F32):
            off = z0 + int(kb * KB)
            assert off + int(np.prod(shape[1:])) * 4 <= nc.sbuf_usable_end, (name, off)
            return place(name, shape, dt, off)

        bank = [ctx.enter_context(nc.psum_tensor(f"bank{i}", [P, 512], F32)) for i in range(8)]

        sems = {}

        def S(name):
            if name not in sems:
                sems[name] = ctx.enter_context(nc.semaphore(name))
            return sems[name]

        slot_loaded = [S(f"slot_loaded{i}") for i in range(RING)]
        hi_done, lo_done, half_done = S("hi_done"), S("lo_done"), S("half_done")
        plain_done = S("plain_done")
        tile_free = {"D": S("tile_free_dve"), "A": S("tile_free_act")}

        def V(name, i=0, n=1):
            return vec[:, VOFF[name] + i:VOFF[name] + i + n]

        def C(name, a=0, b=None):
            w = dict(CON)[name]
            return con[:, COFF[name] + a:COFF[name] + (w if b is None else b)]

        ident, ones = C("ident"), C("ones")

        def bc(ap, n):
            return ap.unsqueeze(1).to_broadcast([ap.shape[0], n, ap.shape[1]])

        def flat(ap):
            return ap.rearrange("p a b -> p (a b)")

        xl = [zone("xl_hi", 0, [P, KC, T], F32R), zone("xl_lo", 16, [P, KC, T], F32R)]
        xc = [zone("xc_hi", 32, [P, KC, T], F32R), zone("xc_lo", 48, [P, KC, T], F32R)]
        tc_ = zone("tmp_ctx", 66, [P, KC, T])
        tl_ = zone("tmp_lat", 82, [P, KC, T])
        kk = zone("k0", 66, [P, 8, 512])
        vv = zone("v0", 82, [P, 4, 1024])
        qq = zone("q0", 98, [P, 8, T])
        vst = zone("vstage", 66, [P, 2, 2, T])
        gi = zone("gate_i", 98, [64, 512])
        gf = zone("gate_f", 100, [64, 512])
        gt = zone("gate_t", 102, [64, 512])
        gw = zone("gate_w", 104, [64, 512])
        gp = zone("gate_p", 106, [64, 512])
        gq = zone("gate_q", 108, [64, 512])
        sigo = zone("sig_o", 32, [P, 8, T])
        y0 = zone("y0", 40, [P, KC, T])
        silm, silp = y0[:, 0:8, :], y0[:, 8:16, :]
        upad = zone("u_pad", 56, [P, 8, 4 * ROWP])
        ps_ = [zone("pool_a", 106, [P, 8, ROWP]), zone("pool_b", 108.5, [P, 8, ROWP])]
        pt = [zone("probs0", 0, [P, 4, T]), zone("probs1", 4, [P, 4, T])]
        hs = zone("h_sum", 8, [P, 8, T])
        ebc = [zone("ebc0", 16, [P, T]), zone("ebc1", 17, [P, T])]
        dn = zone("dn", 18, [P, T])
        dn2 = zone("dn2", 19, [P, T])
        ht = zone("h_tmp", 20, [P, 2, T])
        hq = zone("h_sq", 106, [P, 2, T])
        hr = zone("h_rstd", 108, [P, 4, T])
        hacc = zone("h_acc", 116.25, [P, T])
        hsq = zone("h_square", 117.25, [P, T])
        arow = zone("ada_rows", 0, [2, 2 * D])
        acc = zone("ada_acc", 110.25, [P, D])
        acc3 = zone("ada_acc3", 66, [P, D])
        sq0 = zone("ln_sq", 32, [P, KC, T])
        tx = zone("tmp_x1", 32, [P, KC, T])
        vf = zone("v1f", 48, [P, KC, T])
        uu = zone("u1f", 64, [P, KC, T])
        zz = zone("z1f", 80, [P, KC, T])
        sq1 = zone("v1_sq", 96, [P, KC, T])
        vt1 = zone("v1tok", 32, [P, 2, D])
        yh = [zone("y1_hi", 96, [P, KC, T], F32R), zone("y1_lo", 48, [P, KC, T], F32R)]
        rt = zone("rms_tmp", 84, [P, KC, T])
        rq = zone("rms_sq", 32, [P, KC, T])
        cr = zone("c_raw", 84, [P, 11, T])
        csq = zone("c_sq", 96, [P, 10, T])
        cn = [zone("cn_hi", 32, [P, 10, T], F32R), zone("cn_lo", 42, [P, 10, T], F32R)]
        vt2 = zone("v2tok", 52, [P, 2, D])
        kn = zone("k_nope", 68, [P, KC, T])
        q2 = zone("q2", 84, [P, 24, T])
        v2f = zone("v2f", 84, [P, KC, T])
        con2 = zone("con2", 108, [P, NCON2])
        kpe = zone("k_pe", 112.75, [P, 2, T])
        rr = zone("rope_t", 114.75, [P, T])
        sm = [zone("att_s0", 32, [P, 2, T]), zone("att_s1", 34, [P, 2, T])]
        ptt = [zone("att_pt0", 36, [P, 2, T]), zone("att_pt1", 38, [P, 2, T])]
        mx = zone("att_max", 40, [P, 64])
        oh = [zone("o_hi", 84, [P, KC, T], F32R), zone("o_lo", 68, [P, KC, T], F32R)]
        ya = zone("y_attn", 32, [P, KC, T])
        xr = zone("x_r", 80, [P, KC, T])
        yr = zone("y_r", 96, [P, KC, T])
        xcv = zone("x_conv", 64, [P, KC, T])
        la = zone("log_a", 48, [P, KC, T])
        rw = zone("rnn_w", 112, [P, 4, T])
        ry = [zone("ry_hi", 64, [P, KC, T], F32R), zone("ry_lo", 48, [P, KC, T], F32R)]
        mt = [zone("mix_hi", 0, [P, KC, T], F32R), zone("mix_lo", 16, [P, KC, T], F32R)]
        W = zone("peer_w", 32, [P, I2, T])
        pqq = zone("peer_q", 32, [P, KC, T])
        ss = zone("peer_s", 64, [P, 2, 16, NKEY])
        cand = zone("peer_cand", 80, [P, 8, 256])
        ceq = zone("peer_eq", 88, [P, 8, 256])
        tv = zone("top_v", 96, [P, 2, 16, TOPK])
        ti = zone("top_i", 98, [P, 2, 16, TOPK], U32)
        tf = zone("top_f", 100, [P, 2, 16, TOPK])
        bv = zone("best_v", 102, [P, 2, 8, TOPK])
        bi = zone("best_i", 103, [P, 2, 8, TOPK], U32)
        bj = zone("best_j", 104, [P, 2, 8, TOPK], U32)
        bf = zone("best_f", 105, [P, 2, 8, TOPK])
        gg = zone("peer_g", 106, [P, 2, 3, 8, TOPK])
        gs = zone("peer_gs", 109, [P, 2, 2, 8])
        gT = zone("peer_gT", 113, [P, 3, T])
        oa = [zone("hot1_0", 96, [P, TG, NKEY], BF16), zone("hot1_1", 98, [P, TG, NKEY], BF16)]
        oe = [zone("hot2_0", 100, [P, TG, I2], BF16), zone("hot2_1", 101, [P, TG, I2], BF16)]
        ob = [zone("hotg_0", 102, [P, 3, TG, I2], BF16), zone("hotg_1", 105, [P, 3, TG, I2], BF16)]
        gb = zone("gate_parts", 109.5, [P, 3, T], BF16)
        gres = zone("gate_rest", 111, [P, T])
        wr = [zone(f"w_r{i}", 100 + 2 * i, [P, 2, T], F32R) for i in range(2)]
        pt_x = zone("p_tmp", 64, [P, 2, T])
        pt_r = zone("p_r", 66, [P, 2, 2, T], F32R)
        sg = zone("ple_sig", 48, [P, KC, T])
        ptile = zone("ple_t", 70, [P, 2, T])

        SPLITS = {
            "gates": (xl, tl_, "xm_hi", 0, "xm_lat", NG), "out0": (xl, y0, "y0_hi", 0, "y0_ready", 2),
            "v1": (xl, tx, "xm1_hi", 0, "xm1", 2), "out1": (yh, uu, "y1_hi", 0, "y1_ready", 2),
            "cc": (xl, rt, "n2_hi", 0, "n2", 2), "ro": (ry, yr, "ry_hi", 0, "ry_ready", 2),
            "wo": (mt, ya, "mix_hi", 0, "mix_ready", 2), "pq": (xl, rt, "n2_hi", NG, "n2", 2),
            "pg": (xl, rt, "n2_hi", 2 * NG, "n2", 2)}

        block = ctx.enter_context(nc.Block())

        @block.sync
        def _(sp):
            sp.dma_start(cond[:], A["cond"]).then_inc(S("cond_in"), 16)

            def release(s, pos, it):
                if s.pattern[pos] == "N":
                    n = s.n0 + s.pattern[:pos].count("N")
                    sp.wait_ge(lo_done, 2 * (n + it * s.npi) + 2)
                else:
                    p = s.p0 + s.pattern[:pos].count("P")
                    sp.wait_ge(plain_done, p + it * s.ppi + 1)

            where = {}
            for s in ORDER:
                L = len(s.pattern)

                def load(u, pos, it, first):
                    uu_ = s.u0 + pos
                    if first:
                        if uu_ >= RING:
                            release(*where[uu_ - RING])
                    else:
                        release(s, pos - RING if pos >= RING else pos - RING + L, it if pos >= RING else it - 1)
                    sp.dma_start(ring[uu_ % RING][:], A["w"][bass.ds(u, 1)].rearrange("a p n -> (a p) n")
                                 ).then_inc(slot_loaded[uu_ % RING], 16)

                for it in range(s.iters):
                    for pos in range(L):
                        where[s.u0 + it * L + pos] = (s, pos, it)
                for pos in range(L):
                    load(s.u0 + pos, pos, 0, True)
                if s.iters > 1:
                    assert L % RING == 0
                    with sp.Fori(1, s.iters) as it:
                        for pos in range(L):
                            load(s.u0 + pos + it * L, pos, it, False)
            for g in range(NG):
                sp.wait_ge(S("final"), g + 1)
                sp.dma_start(out[:, g * GR:(g + 1) * GR, :], h[:, g * GR:(g + 1) * GR, :]).then_inc(S("out_done"), 16)
            sp.wait_ge(S("out_done"), 16 * NG)

        def iterations(eng, s, body, mid=None, peel=0):
            if s.iters > 1:
                cuts = sorted({0, peel, s.iters - 1} | (set() if mid is None else {mid[0]}))
                for a, b in zip(cuts, cuts[1:]):
                    if mid is not None and a == mid[0]:
                        mid[1]()
                    if b - a == 1:
                        body(a, False)
                        continue
                    with eng.Fori(a, b) as it:
                        body(it, False)
            body(s.iters - 1, True)

        @block.gpsimd
        def _(pool):
            def split_lo(name):
                if name in SPLITS:
                    pair, src, hi_name, before, done, n = SPLITS[name]
                    for g in range(n):
                        pool.wait_ge(S(hi_name), before + g + 1)
                        pool.tensor_tensor(flat(pair[1][:, g * GR:(g + 1) * GR, :]), flat(src[:, g * GR:(g + 1) * GR, :]),
                                           flat(pair[0][:, g * GR:(g + 1) * GR, :]).bitcast(F32), ALU.subtract
                                           ).then_inc(S(done), 1)

            for s in ORDER:
                if s.npi:
                    def body(it, last):
                        for j in range(s.npi):
                            if j == 1 and isinstance(it, int) and it == 0:
                                split_lo(s.name)
                            n = s.n0 + j + it * s.npi
                            slot = (s.u0 + s.npos[j]) % RING
                            for f in range(2):
                                b = (2 * (s.n0 + j) + f) % NBUF
                                pool.wait_ge(hi_done, 2 * n + f + 1)
                                pool.tensor_tensor(lb[b][:], ring[slot][:, f * HALF:(f + 1) * HALF],
                                                   hb[b][:].bitcast(F32), ALU.subtract).then_inc(lo_done, 1)
                    assert (2 * s.npi) % NBUF == 0 or s.iters == 1
                    body(0, False)
                    if s.iters > 1:
                        with pool.Fori(1, s.iters) as it:
                            body(it, False)
                    if s.npi == 1:
                        split_lo(s.name)
                    if s.name in ("peer_u0", "peer_u1"):
                        pool.wait_ge(S("gate_parts"), 1)
                        with pool.Fori(0, T // TG // 2) as it:
                            for k in range(2):
                                before = int(s.name[-1]) * (T // TG) + k + 1
                                pool.wait_ge(S("hot_2"), before + it * 2)
                                pool.wait_ge(S("g_done"), before + it * 2)
                                for x in (1, 2):
                                    ins = pool.tensor_tensor(
                                        ob[k][:, x], oe[k][:], gb[:, x, bass.ds(it * (2 * TG) + k * TG, TG)].unsqueeze(2)
                                        .to_broadcast([P, TG, I2]), ALU.mult)
                                ins.then_inc(S("hot_g12"), 1)

        @block.tensor
        def _(pe):
            def moving_ready(name, g):
                before, done, n = SPLITS[name][3:]
                uses = before // NG
                if g < n:
                    pe.wait_ge(S(done), uses * n + g + 1)
                else:
                    pe.wait_ge(S(done + "_dve"), uses * (NG - n) + g - n + 1)

            def n_unit(s, movs, per_tile, it, j):
                n_tiles = s.tiles // len(movs)
                n = s.n0 + j + it * s.npi
                for f in range(2):
                    b = (2 * (s.n0 + j) + f) % NBUF
                    pe.wait_ge(lo_done, 2 * n + f + 1)
                    for i in range(8 * f, min(8 * f + 8, n_tiles * per_tile)):
                        t, k = i // per_tile, i % per_tile
                        if s.name in SPLITS and isinstance(it, int) and it == 0 and j == 0 and k % GR == 0:
                            moving_ready(s.name, k // GR)
                        tile = [(j * n_tiles + t) * len(movs) + m for m in range(len(movs))]
                        if k == 0:
                            pe.wait_ge(tile_free[s.eng], s.base + tile[-1] + 1 + it * (s.npi * s.tiles))
                        for w, x in ((hb, 0), (hb, 1), (lb, 0)):
                            for m, mv in enumerate(movs):
                                mm = pe.matmul(bank[(s.t0 + tile[m]) % TILES][:, 0:T],
                                               w[b][:, (i % 8) * P:(i % 8 + 1) * P], mv[x][:, k, :],
                                               start=(k == 0 and w is hb and x == 0),
                                               stop=(k == per_tile - 1 and w is lb))
                    mm.then_inc(half_done, 1)

            def ada_sum(b):
                pe.wait_ge(plain_done, PLAN["out0"].p0 + KC if b == 3 else 2 * KC + KC * (b + 1))
                for c in range(KC):
                    mm = pe.matmul(bank[4][:, 64 + b * KC + c:65 + b * KC + c], (acc3 if b == 3 else acc)[:, c * P:(c + 1) * P],
                                   ones[:, 0:1], start=True, stop=True, skip_group_check=True)
                mm.then_inc(S("ada_sum"), 1)

            def run(name, movs=None, per_tile=KC, extra=None, mid=None):
                s = PLAN[name]
                if s.td:
                    pe.wait_ge(tile_free["D"], TILES + s.td)
                if s.ta:
                    pe.wait_ge(tile_free["A"], TILES + s.ta)

                def body(it, last):
                    j = 0
                    for pos, kind in enumerate(s.pattern):
                        if kind == "P":
                            continue
                        n_unit(s, movs, per_tile, it, j)
                        if extra is not None:
                            extra(it, j)
                        j += 1
                iterations(pe, s, body, mid, 1 if name in SPLITS else 0)

            def slot_wait(name, i=0):
                s = PLAN[name]
                u = s.u0 + i
                pe.wait_ge(slot_loaded[u % RING], 16 * (u // RING + 1))
                return ring[u % RING]

            def feature_sum(src, dst, ready, value, done):
                n = src.shape[1]
                for k in range(n):
                    if k % GR == 0 and (k == 0 or n == KC):
                        pe.wait_ge(S(ready), value + k // GR)
                    mm = pe.matmul(dst, ones, src[:, k, :], start=(k == 0), stop=(k == n - 1))
                mm.then_inc(S(done), 1)

            def acc_sum(dst, value, done):
                pe.wait_ge(S("h_acc"), value)
                pe.matmul(dst, ones, hacc[:], start=True, stop=True).then_inc(S(done), 1)

            pe.wait_ge(S("cond_ready"), 1)
            for u in range(2 * KC):
                pe.wait_ge(slot_loaded[u % RING], 16 * (u // RING + 1))
                for i in range(4):
                    mm = pe.matmul(bank[4 * (u % 2) + i][0:2, :], cond[:, u // 2, :],
                                   ring[u % RING][:, i * 512:(i + 1) * 512], start=(u < 2), stop=(u >= 2 * KC - 2))
                mm.then_inc(plain_done, 1)
            pe.wait_ge(S("con_in"), 16)
            pe.wait_ge(S("ada_rows"), 8)
            for c in range(2 * KC):
                mm = pe.matmul(bank[4][:, 2 * c:2 * c + 2], arow[:, c * P:(c + 1) * P], ident[0:2, 0:2],
                               start=True, stop=True, skip_group_check=True)
            mm.then_inc(S("ada_cols"), 1)
            pe.wait_ge(S("xm_ctx"), 1)
            run("gates", [xl, xc])
            sv = PLAN["v"]

            def v_transposes(j):
                pe.wait_ge(tile_free["D"], TILES + sv.td + 2 * (j + 1))
                pe.wait_ge(S("v_tok"), j + 1)
                for t in range(4):
                    mm = pe.transpose(bank[6][:, t * P:(t + 1) * P],
                                      vst[:, j % 2, 1 - t // 2, (t % 2) * P:(t % 2 + 1) * P], ident)
                mm.then_inc(S("vt_done"), 1)

            def v_before(it, j):
                if it * sv.npi + j:
                    v_transposes(it * sv.npi + j - 1)
            run("v", [xl, xc], extra=v_before)
            v_transposes(sv.npi * sv.iters - 1)
            ada_sum(0)
            pe.wait_ge(S("a_rows"), 1)
            for d in range(2):
                for t in range(4):
                    mm = pe.matmul(bank[5][:, (d * 4 + t) * 4:(d * 4 + t) * 4 + 4],
                                   gi[:, t * P:(t + 1) * P], ident[0:64, 32 * d:32 * d + 4],
                                   start=True, stop=True, skip_group_check=True)
            mm.then_inc(S("a_cols"), 1)
            run("k", [xl, xc])
            ada_sum(1)
            run("q", [xl])
            run("o", [xl])
            run("zm", [xl])
            run("up", [xl])
            ada_sum(2)
            run("zp", [xl])
            w = slot_wait("poolw")
            pe.wait_ge(S("pooled"), 1)
            pe.wait_ge(tile_free["A"], TILES + PLAN["poolw"].ta)
            pe.wait_ge(tile_free["D"], TILES + PLAN["poolw"].td)
            for g in range(4):
                for j in range(2):
                    for k in range(2):
                        i = (g * 2 + k) * 2 + j
                        mv = upad[:, 2 * g + k, :].rearrange("p (r c) -> p r c", r=4)[:, :, PAD:PAD + ROW]
                        mm = pe.matmul(bank[g][:, j * T:(j + 1) * T], w[:, i * P:(i + 1) * P], mv,
                                       start=(k == 0), stop=(k == 1), skip_group_check=True)
            mm.then_inc(plain_done, 1)
            def gates_bc(i):
                hd, d = i // 2, i % 2
                if i >= 1:
                    pe.wait_ge(S("bc_used"), i)
                for r, row in enumerate((mrow, erow)):
                    pick = ident[0:64, 32 * d + hd:32 * d + hd + 1].to_broadcast([64, P])
                    mm = pe.matmul(bank[7][:, r * T:(r + 1) * T], pick, row[:], start=True, stop=True,
                                   skip_group_check=True)
                mm.then_inc(S("bc_done"), 1)

            def scores(hd):
                if hd >= 1:
                    pe.wait_ge(S("probs_ready"), 2 * hd)
                for t in range(4):
                    for c in range(2):
                        mm = pe.matmul(bank[5 + t // 2][:, (t % 2) * T:(t % 2 + 1) * T],
                                       kk[:, 2 * hd + c, t * P:(t + 1) * P], qq[:, 2 * hd + c, :],
                                       start=(c == 0), stop=(c == 1), skip_group_check=True)
                mm.then_inc(S("scores_done"), 1)

            def prob_value(i):
                hd, d = i // 2, i % 2
                pe.wait_ge(S("probs_ready"), i + 1)
                if i >= 2:
                    pe.wait_ge(S("num_used"), i - 1)
                order = [(0, 0, T), (1, 0, T), (2, 0, T), (3, P, T)] if d == 0 else \
                        [(0, 0, T), (1, 0, T), (3, 0, T), (2, 0, P)]
                num, den = bank[2 * (i % 2)], bank[2 * (i % 2) + 1]
                for c in range(3):
                    for n, (t, a, b) in enumerate(order):
                        dst = den[:, a:b] if c == 2 else num[:, c * T + a:c * T + b]
                        lhs = ones if c == 2 else vv[:, t, hd * 256 + c * P:hd * 256 + (c + 1) * P]
                        mm = pe.matmul(dst, lhs, pt[i % 2][:, t, a:b], start=(n == 0), stop=(n == 3),
                                       skip_group_check=True)
                mm.then_inc(S("num_done"), 1)

            pe.wait_ge(S("rows_ready"), 1)
            pe.wait_ge(S("k_silu"), 1)
            pe.wait_ge(S("q_silu"), 1)
            pe.wait_ge(S("v_tok"), 8 + 1)
            pe.wait_ge(S("yp_done"), 1)
            gates_bc(0)
            scores(0)
            def head_sum(g, r):
                pe.wait_ge(S("hn_in") if r == 0 else S("hn_sq"), g + 1)
                for c in range(2):
                    mm = pe.matmul(bank[4][:, r * T:(r + 1) * T], ones, hs[:, 2 * g + c, :] if r == 0 else hq[:, c, :],
                                   start=(c == 0), stop=(c == 1), skip_group_check=True)
                mm.then_inc(S("hn_sum"), 1)

            for i in range(2 * NH + 2):
                if i + 1 < 2 * NH:
                    gates_bc(i + 1)
                if i % 2 == 1 and i // 2 + 1 < NH:
                    scores(i // 2 + 1)
                if i < 2 * NH:
                    prob_value(i)
                if i >= 2:
                    head_sum((i - 2) // 2, i % 2)
            run("out0", [xl])
            acc_sum(bank[5][:, 0:T], 1, "ln0_sum")
            feature_sum(sq0, bank[6][:, 0:T], "ln0_in", 1, "ln0_sum")
            ada_sum(3)
            run("v1", [xl])
            acc_sum(bank[5][:, 0:T], 2, "lnv_sum")
            feature_sum(sq1, bank[6][:, 0:T], "lnv_in", 1, "lnv_sum")
            run("u1", [xl])
            pe.wait_ge(S("v1_norm"), NG)
            for g in range(8):
                if g >= 2:
                    pe.wait_ge(S("v1_tok"), g - 1)
                for i in range(4):
                    j = 4 * g + i
                    mm = pe.transpose(bank[5 + g % 2][:, i * P:(i + 1) * P], vf[:, j % 16, (j // 16) * P:(j // 16 + 1) * P],
                                      ident)
                mm.then_inc(S("v1_tp"), 1)
            run("z1", [xl])
            w = slot_wait("wsp")
            pe.wait_ge(S("v1_tok"), 8)
            for c in range(KC):
                b = bank[4 + c % 4]
                if c >= 4:
                    pe.wait_ge(S("sgu_used"), c - 3)
                for t in range(2):
                    pe.matmul(b[:, t * P:(t + 1) * P], vt1[:, t, c * P:(c + 1) * P], w[:, (c // 2) * P:(c // 2 + 1) * P],
                              start=True, stop=False, skip_group_check=True)
                    mm = pe.matmul(b[:, t * P:(t + 1) * P], ones[0:1, :],
                                   w[0:1, HALF + (c // 2) * P:HALF + (c // 2 + 1) * P], start=False, stop=True,
                                   skip_group_check=True)
                mm.then_inc(S("sgu_done") if c < KC - 1 else plain_done, 1)
            run("out1", [yh])
            acc_sum(bank[5][:, 0:T], 3, "ln1_sum")
            feature_sum(sq0, bank[6][:, 0:T], "ln1_in", 1, "ln1_sum")
            feature_sum(rq, bank[7][:, 0:T], "rms_in", 1, "rms_sum")
            run("cc", [xl])
            for r, (a, b) in enumerate(((6, 10), (0, 6))):
                feature_sum(csq[:, a:b, :], bank[5 + r][:, 0:T], "csq", r + 1, "c_sum")
            pe.wait_ge(S("con2_in"), 16)
            rot = con2[:, C2OFF["rot"]:C2OFF["rot"] + 128]
            pe.matmul(bank[7][:, 0:T], rot, cr[:, 10, :], start=True, stop=True).then_inc(S("rope_done"), 1)
            pe.wait_ge(S("cn_ready"), 1)
            ckv = [cn[0][:, 6:10, :], cn[1][:, 6:10, :]]
            cq = [cn[0][:, 0:6, :], cn[1][:, 0:6, :]]
            run("uv", [ckv], per_tile=4)
            run("uk", [ckv], per_tile=4)
            for g in range(8):
                if g >= 2:
                    pe.wait_ge(S("v2_tok"), g - 1)
                for i in range(4):
                    j = 4 * g + i
                    mm = pe.transpose(bank[5 + g % 2][:, i * P:(i + 1) * P], v2f[:, j % 16, (j // 16) * P:(j // 16 + 1) * P], ident)
                mm.then_inc(S("v2_tp"), 1)
            pe.wait_ge(S("cn_ready"), 2)
            run("uq", [cq], per_tile=6)
            pe.wait_ge(tile_free["D"], TILES + PLAN["ao"].td)
            for j in range(8):
                if j >= 2:
                    pe.wait_ge(S("rope_used"), j)
                pe.matmul(bank[5 + j % 2][:, 0:T], rot, q2[:, 16 + j, :], start=True, stop=True
                          ).then_inc(S("rope_done"), 1)
            def att_scores(hd):
                if hd >= 2:
                    pe.wait_ge(S("att_masked"), hd - 1)
                b = bank[hd % 2]
                for t in range(2):
                    pe.matmul(b[:, t * T:(t + 1) * T], q2[:, hd, t * P:(t + 1) * P], kn[:, hd, :],
                              start=True, stop=False, skip_group_check=True)
                    mm = pe.matmul(b[:, t * T:(t + 1) * T], q2[:, 16 + hd // 2, t * P:(t + 1) * P], kpe[:, hd % 2, :],
                                   start=False, stop=True, skip_group_check=True)
                mm.then_inc(S("att_s"), 1)

            def att_transposes(hd):
                pe.wait_ge(S("att_p"), hd + 1)
                if hd >= 1:
                    pe.wait_ge(S("att_pt"), hd)
                for k in range(2):
                    for t in range(2):
                        mm = pe.transpose(bank[2][:, k * T + t * P:k * T + (t + 1) * P],
                                          sm[hd % 2][:, t, k * P:(k + 1) * P], ident)
                mm.then_inc(S("att_tp"), 1)

            def att_values(hd):
                pe.wait_ge(S("att_pt"), hd + 1)
                if hd >= 2:
                    pe.wait_ge(S("o_ready"), hd - 1)
                for k in range(2):
                    mm = pe.matmul(bank[5 + hd % 2][:, 0:T], vt2[:, k, hd * P:(hd + 1) * P], ptt[hd % 2][:, k, :],
                                   start=(k == 0), stop=(k == 1))
                mm.then_inc(S("att_o"), 1)
            pe.wait_ge(S("rope_used"), 9)
            att_scores(0)
            att_scores(1)
            for hd in range(HEADS):
                att_transposes(hd)
                if hd + 2 < HEADS:
                    att_scores(hd + 2)
                att_values(hd)
            pe.wait_ge(S("o_ready"), HEADS)
            run("ao", [oh])
            run("xr", [xl])
            wa, wx = slot_wait("rg", 0), slot_wait("rg", 1)
            pe.wait_ge(tile_free["D"], TILES + PLAN["rg"].td)
            for c in range(KC):
                if c >= 2:
                    pe.wait_ge(S("rg_used"), c - 1)
                b = bank[5 + c % 2]
                ma = pe.matmul(b[:, 0:T], wa[:, c * P:(c + 1) * P], xcv[:, c, :], start=True, stop=True,
                               skip_group_check=True)
                mx_ = pe.matmul(b[:, T:2 * T], wx[:, c * P:(c + 1) * P], xcv[:, c, :], start=True, stop=True,
                                skip_group_check=True)
                if c < KC - 1:
                    mx_.then_inc(S("rg_done"), 1)
                else:
                    ma.then_inc(plain_done, 1)
                    mx_.then_inc(plain_done, 1)
            run("ga", [xl])
            run("yr", [xl])
            run("gr", [xl])
            run("ro", [ry])
            run("wo", [mt])
            acc_sum(bank[7][:, 0:T], 4, "rms_sum")
            run("pq", [xl])
            w = slot_wait("sk")
            pe.wait_ge(tile_free["D"], TILES + PLAN["sk"].td)
            for g in range(8):
                t = g // 4
                if g >= 2:
                    pe.wait_ge(S("s_evac"), g - 1)
                for i in range(4):
                    j = 4 * (g % 4) + i
                    mm = pe.matmul(bank[5 + g % 2][:, i * P:(i + 1) * P], pqq[:, j, t * P:(t + 1) * P],
                                   w[:, j * P:(j + 1) * P], start=True, stop=True, skip_group_check=True)
                mm.then_inc(S("s_done") if g < 7 else plain_done, 1)
            def gates_tp():
                pe.wait_ge(S("gates_tok"), 2)
                for t in range(2):
                    for i in range(3):
                        mm = pe.transpose(bank[5 + t][:, i * P:(i + 1) * P], flat(gg[:, t, i, :, :]), ident)
                mm.then_inc(S("gT_done"), 1)
            for r in range(2):
                if r == 1:
                    pe.wait_ge(S("acc_used"), 1)
                run(f"peer_u{r}", [xl], mid=(12, gates_tp) if r == 0 else None)

                def build(it, r=r):
                    for k in range(2):
                        i = r * (T // TG) + k + it * 2
                        pe.wait_ge(S("hot_1"), i + 1)
                        pe.wait_ge(S("hot_g0"), i + 1)
                        pe.wait_ge(S("hot_g12"), i + 1)
                        pe.wait_ge(S("g_used"), i + 1)
                        for t in range(TG):
                            for x in range(3):
                                mm = pe.matmul(bank[5 + k][:, t * I2:(t + 1) * I2], oa[k][:, t, :], ob[k][:, x, t, :],
                                               start=(x == 0), stop=(x == 2), skip_group_check=True)
                        mm.then_inc(S("g_done"), 1)
                if r == 1:
                    pe.wait_ge(S("acc_used"), 2)
                with pe.Fori(0, T // TG // 2) as it:
                    build(it)
                s = PLAN[f"peer_v{r}"]
                pe.wait_ge(tile_free["A"], TILES + s.ta)
                pe.wait_ge(S("g_used"), (r + 1) * (T // TG) + 2)

                def body(it, first, r=r, s=s):
                    for j in range(4):
                        n = s.n0 + j + it * 4
                        pe.wait_ge(S("wr_ready"), r * I2 + j + 1 + it * 4)
                        for f in range(2):
                            b = (2 * (s.n0 + j) + f) % NBUF
                            pe.wait_ge(lo_done, 2 * n + f + 1)
                            for c in range(8):
                                cc = 8 * f + c
                                o = bank[cc // 2][:, (cc % 2) * T:(cc % 2 + 1) * T]
                                for w_, x in ((hb, 0), (hb, 1), (lb, 0)):
                                    mm = pe.matmul(o, w_[b][:, c * P:(c + 1) * P], wr[j % 2][:, x, :],
                                                   start=(first and j == 0 and cc % 2 == 0 and w_ is hb and x == 0),
                                                   stop=False, skip_group_check=True)
                            mm.then_inc(half_done, 1)
                body(0, True)
                with pe.Fori(1, s.iters) as it:
                    body(it, False)
            feature_sum(rq, bank[0][:, 0:T], "rms_in", NG + 1, "rms_sum")
            run("pg", [xl])
            pe.wait_ge(S("p_ready"), 1)
            run("pp", [[pt_r[:, 0, :, :], pt_r[:, 1, :, :]]], per_tile=2)
            acc_sum(bank[7][:, 0:T], 5, "rms_sum")

        @block.scalar
        def _(act):
            def hi(n, place):
                slot, loads, n_static = place
                act.wait_ge(slot_loaded[slot], 16 * loads)
                for f in range(2):
                    b = (2 * n_static + f) % NBUF
                    act.wait_ge(half_done, 2 * n + f + 1)
                    act.activation(hb[b][:], ring[slot][:, f * HALF:(f + 1) * HALF], ACT.Copy).then_inc(hi_done, 1)

            def ahead(s, j, it, last):
                L = len(s.pattern)
                n = s.n0 + j + 1 + it * s.npi
                if j + 1 < s.npi:
                    u = s.u0 + s.npos[j + 1]
                    hi(n, (u % RING, u // RING + 1 + it * (L // RING), s.n0 + j + 1))
                elif not last:
                    u = s.u0 + s.npos[0]
                    hi(n, (u % RING, u // RING + 1 + (it + 1) * (L // RING), s.n0 + s.npi))
                else:
                    u = first_n_after(s)
                    if u is not None :
                        hi(n, (u % RING, u // RING + 1, s.n0 + s.npi * s.iters))

            def by_group(dst, src, func, ready, before, done):
                for g in range(NG):
                    act.wait_ge(S(ready), before + g + 1)
                    act.activation(flat(dst[:, g * GR:(g + 1) * GR, :]), flat(src[:, g * GR:(g + 1) * GR, :]), func
                                   ).then_inc(S(done), 1)

            roots = [0]

            def root(ap):
                roots[0] += 1
                act.preload_act_table(ACT.Sqrt)
                act.wait_ge(S("var_ready"), roots[0])
                act.activation(ap, ap, ACT.Sqrt).then_inc(S("root_done"), 1)

            def run(name, evac=None, first=(), mid=None, table=None):
                s = PLAN[name]
                if table is not None:
                    act.preload_act_table(table)

                def body(it, last):
                    for j in range(s.npi):
                        ahead(s, j, it, last)
                        if evac is not None:
                            act.wait_ge(half_done, NBUF + 2 * (s.n0 + j + it * s.npi) + 2)
                            i = j + it * s.npi
                            evac(i, bank[(s.t0 + j) % TILES][:, 0:T]).then_inc(tile_free["A"], 1)
                        if first and isinstance(it, int) and it == 0 and j < len(first):
                            first[j]()
                iterations(act, s, body, mid, 1 if first else 0)

            def at_chunk(t, i):
                if isinstance(i, int):
                    return t[:, i, :]
                return t[:, bass.ds(i, 1), :].rearrange("p a t -> p (a t)")

            act.wait_ge(S("cond_in"), 16)
            act.activation(flat(cond[:]), flat(cond[:]), ACT.Silu).then_inc(S("cond_ready"), 1)
            act.wait_ge(plain_done, 4)
            act.dma_start(vec[:], A["vec"]).then_inc(S("vec_in"), 16)
            act.dma_start(con[:], A["con"]).then_inc(S("con_in"), 16)
            act.dma_start(h[:], A["xT"]).then_inc(S("x_in"), 16)
            act.wait_ge(plain_done, 16)
            act.dma_start(tc_[:], A["ctxT"]).then_inc(S("ctx_in"), 16)
            s0 = PLAN["gates"]
            act.wait_ge(S("init"), 1)
            hi(0, (s0.u0 % RING, s0.u0 // RING + 1, 0))
            act.wait_ge(plain_done, 2 * KC)
            for b in (1, 3, 5, 7):
                act.activation(arow[:, b * 512:(b + 1) * 512], bank[b][0:2, :], ACT.Copy).then_inc(S("ada_rows"), 1)
            by_group(xl[0], tl_, ACT.Copy, "xm_tmp", 0, "xm_hi")
            by_group(xc[0], tc_, ACT.Copy, "xm_tmp", NG, "xm_hi")
            run("gates")
            act.wait_ge(S("gate_abs"), 1)
            act.activation(gw[:], gt[:], ACT.Exp, scale=-1.0).then_inc(S("gate_exp"), 1)
            run("v")
            act.wait_ge(S("m_rows"), 1)
            act.activation(erow[:], erow[:], ACT.Exp, scale=-1.0).then_inc(S("rows_ready"), 1)

            def alpha_x(i):
                if i:
                    act.wait_ge(S("h1_ready"), 1)
                act.activation(flat(h[:]), flat(h[:]), ACT.Copy, scale=ALPHA).then_inc(S(f"ax{i}"), 1)
            run("k", first=(lambda: alpha_x(0),))
            run("q")
            act.wait_ge(tile_free["D"], TILES + PLAN["q"].td)
            act.activation(flat(kk[:]), flat(kk[:]), ACT.Silu).then_inc(S("k_silu"), 1)
            act.wait_ge(tile_free["D"], TILES + PLAN["o"].td)
            act.activation(flat(qq[:]), flat(qq[:]), ACT.Silu).then_inc(S("q_silu"), 1)
            run("o", lambda i, ps: act.activation(at_chunk(sigo, i), ps, ACT.Sigmoid), table=ACT.Sigmoid)
            run("zm", lambda i, ps: act.activation(at_chunk(silm, i), ps, ACT.Silu), table=ACT.Silu)
            run("up")
            run("zp", lambda i, ps: act.activation(at_chunk(silp, i), ps, ACT.Silu), table=ACT.Silu)
            for i in range(2 * NH + 3):
                if i < 2 * NH:
                    act.wait_ge(S("args"), i + 1)
                    act.activation(flat(pt[i % 2][:]), flat(pt[i % 2][:]), ACT.Exp, scale=-1.0).then_inc(S("gexp"), 1)
                if i >= 3 and i % 2:
                    g = (i - 3) // 2
                    act.wait_ge(S("hc"), g + 1)
                    act.activation(flat(hq[:]), flat(hs[:, 2 * g:2 * g + 2, :]), ACT.Square
                                   ).then_inc(S("hn_sq"), 1)
                if i >= 4 and i % 2 == 0:
                    root(hr[:, (i - 4) // 2, :])
            by_group(xl[0], y0, ACT.Copy, "y0", 0, "y0_hi")
            run("out0")
            by_group(sq0, h, ACT.Square, "ln0_c", 0, "ln0_in")
            root(rstd[:])
            by_group(xl[0], tx, ACT.Copy, "xm1_tmp", 0, "xm1_hi")
            run("v1", first=(lambda: alpha_x(1),))
            by_group(sq1, vf, ACT.Square, "lnv_c", 0, "lnv_in")
            root(rstd[:])
            run("u1")
            run("z1", lambda i, ps: act.activation(at_chunk(zz, i), ps, ACT.Silu), table=ACT.Silu)
            by_group(yh[0], uu, ACT.Copy, "y1", 0, "y1_hi")
            run("out1")
            by_group(sq0, h, ACT.Square, "ln1_c", 0, "ln1_in")
            root(rstd[:])

            def rms(i):
                if i in (1, 3):
                    by_group(rq, h, ACT.Square, "h_ready", (i // 2) * NG, "rms_in")
                root(rstd[:])
                if i < 4:
                    by_group(xl[0], rt, ACT.Copy, "rms_t", (i - 1) * NG, "n2_hi")
            rms(1)
            act.dma_start(con2[:], A["con2"]).then_inc(S("con2_in"), 16)
            run("cc")
            act.wait_ge(S("c_evac"), 1)
            for a, b in ((6, 10), (0, 6)):
                act.activation(flat(csq[:, a:b, :]), flat(cr[:, a:b, :]), ACT.Square).then_inc(S("csq"), 1)
            for i, (a, b) in enumerate(((6, 10), (0, 6))):
                root(rstd[:])
                act.wait_ge(S("c_norm"), i + 1)
                act.activation(flat(cn[0][:, a:b, :]), flat(cr[:, a:b, :]), ACT.Copy).then_inc(S("cn_hi"), 1)
            run("uv")
            run("uk")
            run("uq")
            def o_hi(hd):
                act.wait_ge(S("att_o"), hd + 1)
                act.activation(oh[0][:, hd, :], bank[5 + hd % 2][:, 0:T], ACT.Copy).then_inc(S("o_hi"), 1)
            for hd in range(HEADS):
                act.wait_ge(S("att_max"), hd + 1)
                for t in range(2):
                    ins = act.activation(sm[hd % 2][:, t, :], sm[hd % 2][:, t, :], ACT.Exp,
                                         bias=mx[:, 2 * (hd % 4) + t:2 * (hd % 4) + t + 1],
                                         accum_out=mx[:, 16 + 2 * (hd % 4) + t:17 + 2 * (hd % 4) + t])
                    ins.then_inc(S("att_exp"), 1)
                if hd >= 1:
                    o_hi(hd - 1)
            o_hi(HEADS - 1)
            run("ao")
            run("xr")
            act.wait_ge(S("lam_abs"), 1)
            act.activation(lam_s[:], lam_s[:], ACT.Exp, scale=-1.0).then_inc(S("lam_exp"), 1)
            for c in range(KC):
                if c < KC - 1:
                    act.wait_ge(S("rg_done"), c + 1)
                else:
                    act.wait_ge(plain_done, PLAN["rg"].p0 + 2)
                b = bank[5 + c % 2]
                act.activation(xr[:, c, :], b[:, 0:T], ACT.Sigmoid, bias=V("b_ra", c)).then_inc(S("rg_r"), 1)
                if c >= 2:
                    act.wait_ge(S("ix_used"), c - 1)
                act.activation(rw[:, c % 2, :], b[:, T:2 * T], ACT.Sigmoid, bias=V("b_rx", c)).then_inc(S("rg_used"), 1)

            def decay():
                act.wait_ge(S("la_ready"), 1)
                act.activation(flat(xr[:]), flat(la[:]), ACT.Exp).then_inc(S("a_ready"), 1)

            def tanh():
                act.wait_ge(S("a_ready"), 1)
                act.activation(flat(la[:]), flat(la[:]), ACT.Tanh).then_inc(S("a_ready"), 1)

            def mult_root():
                act.wait_ge(S("m2_ready"), 1)
                act.activation(flat(la[:]), flat(la[:]), ACT.Sqrt).then_inc(S("mult_ready"), 1)
                act.preload_act_table(ACT.Sigmoid)

            def gate_bias(i):
                return V("b_gate", i) if isinstance(i, int) else vec[:, bass.ds(VOFF["b_gate"] + i, 1)]
            run("ga", lambda i, ps: act.activation(at_chunk(yr, i), ps, ACT.Sigmoid, bias=gate_bias(i)),
                (decay, tanh), (2, mult_root), ACT.Sigmoid)
            act.wait_ge(S("ga_used"), KC)
            run("yr", lambda i, ps: act.activation(at_chunk(yr, i), ps, ACT.Gelu_apprx_tanh),
                table=ACT.Gelu_apprx_tanh)

            act.wait_ge(S("scanned"), 1)
            run("gr", lambda i, ps: act.activation(at_chunk(xr, i), ps, ACT.Sigmoid, bias=gate_bias(16 + i)),
                table=ACT.Sigmoid)
            by_group(ry[0], yr, ACT.Copy, "ry_t", 0, "ry_hi")
            run("ro")
            by_group(mt[0], ya, ACT.Copy, "mix_t", 0, "mix_hi")
            run("wo")
            rms(2)
            run("pq")
            def gate_exp():
                act.wait_ge(S("topk_done"), 1)
                act.activation(flat(bv[:].rearrange("p t h k -> p t (h k)")),
                               flat(bv[:].rearrange("p t h k -> p t (h k)")), ACT.Exp).then_inc(S("gate_e"), 1)
                act.preload_act_table(ACT.Gelu_apprx_tanh)
            for r in range(2):
                if r == 1:
                    act.wait_ge(S("wr_ready"), I2)
                s = PLAN[f"peer_u{r}"]

                def u_body(it, last, r=r, s=s):
                    for j in range(4):
                        ahead(s, j, it, last)
                        act.wait_ge(half_done, NBUF + 2 * (s.n0 + j + it * 4) + 2)
                        act.activation(at_chunk(W, j + it * 4), bank[(s.t0 + j) % TILES][:, 0:T],
                                       ACT.Gelu_apprx_tanh).then_inc(tile_free["A"], 1)
                act.preload_act_table(ACT.Gelu_apprx_tanh)
                iterations(act, s, u_body, (8, gate_exp) if r == 0 else None)
                act.wait_ge(S("gate_parts"), 1)

                def gate_part(it, r=r):
                    for k in range(2):
                        i = r * (T // TG) + k + it * 2
                        act.wait_ge(S("hot_2"), i + 1)
                        act.wait_ge(S("g_done"), i + 1)
                        for t in range(TG):
                            ins = act.activation(ob[k][:, 0, t, :], oe[k][:, t, :], ACT.Copy,
                                                 scale=gT[:, 2:3, bass.ds(it * (2 * TG) + (k * TG + t), 1)]
                                                 .rearrange("p a t -> p (a t)"))
                        ins.then_inc(S("hot_g0"), 1)
                with act.Fori(0, T // TG // 2) as it:
                    gate_part(it)
                s = PLAN[f"peer_v{r}"]

                def v_body(it, last, r=r, s=s):
                    for j in range(4):
                        act.wait_ge(half_done, NBUF + 2 * (s.n0 + j + it * 4) - 2)
                        act.activation(wr[j % 2][:, 0, :], at_chunk(W, j + it * 4), ACT.Copy
                                       ).then_inc(S("wr_hi"), 1)
                        ahead(s, j, it, last)
                act.wait_ge(S("g_used"), (r + 1) * (T // TG) + 2)
                iterations(act, s, v_body)
            act.wait_ge(S("wr_ready"), 2 * I2)
            act.dma_start(pt_x[:], A["pT"]).then_inc(S("p_in"), 16)
            rms(3)
            act.wait_ge(S("p_in"), 16)
            act.activation(flat(pt_r[:, 0, :, :]), flat(pt_x[:]), ACT.Copy).then_inc(S("p_hi"), 1)
            run("pg", lambda i, ps: act.activation(at_chunk(sg, i), ps, ACT.Sigmoid), table=ACT.Sigmoid)
            run("pp")
            rms(4)

        @block.vector
        def _(dve):
            seq_sem = S("dve_seq")
            seq = [0, 0]

            def go(ins):
                seq[0] += 1
                return ins.then_inc(seq_sem, 1)

            def sync():
                dve.wait_ge(seq_sem, seq[1] + seq[0])

            def chunks(body, name=None):
                for c in range(KC):
                    body(c)
                    if name is not None and c % GR == GR - 1:
                        event(name)

            def loop(n, per, body):
                if n == 1:
                    body(0)
                    return
                start = seq[0]
                with dve.Fori(0, n) as it:
                    seq[1] = it * per
                    body(it)
                assert seq[0] - start == per, (seq[0] - start, per)
                seq[0] = start + n * per
                seq[1] = 0

            def ada(s, j, it):
                pos = s.npos[j] + 1
                while pos < len(s.pattern) and s.pattern[pos] == "P":
                    u, before = s.u0 + pos, s.pattern[:pos].count("P")
                    k = s.k0 + before + it * s.ppi
                    a = acc3 if s.name == "out0" else acc
                    dve.wait_ge(slot_loaded[u % RING], 16 * (u // RING + 1 + it * (len(s.pattern) // RING)))
                    dve.wait_ge(plain_done, s.p0 + before + it * s.ppi)
                    col = cond[:, k, 0:1] if isinstance(k, int) else \
                        cond[:, bass.ds(k, 1), 0:1].rearrange("p a s -> p (a s)")
                    dve.scalar_tensor_tensor(a[:], ring[u % RING][:], col, a[:], ALU.mult, ALU.add
                                             ).then_inc(plain_done, 1)
                    pos += 1

            def ada_start(b):
                if b in (1, 2):
                    dve.wait_ge(S("ada_sum"), b)
                go(dve.memset(acc3[:] if b == 3 else acc[:], 0.0)); sync()

            def ada_only(name):
                s = PLAN[name]

                def body(it):
                    for j in range(s.npi):
                        ada(s, j, it)
                loop(s.iters, 0, body)

            def run(name, evac, per=0):
                s = PLAN[name]

                def body(it):
                    for j in range(s.npi):
                        ada(s, j, it)
                        for tl in range(s.tiles):
                            f = 1
                            if s.tiles > 2 or name == "uq":
                                f = ((tl + 1) * PER_TILE[name] - 1) // 8
                            if tl == 0 or s.tiles > 2 or name == "uq":
                                dve.wait_ge(half_done, NBUF + 2 * (s.n0 + j + it * s.npi) + f + 1)
                            i = j * s.tiles + tl + it * (s.npi * s.tiles)
                            evac(i, bank[(s.t0 + j * s.tiles + tl) % TILES][:, 0:T], j * s.tiles + tl
                                 ).then_inc(tile_free["D"], 1)
                loop(s.iters, per, body)

            def at(t, i, a=None, b=None):
                w = t.shape[2]
                a, b = 0 if a is None else a, w if b is None else b
                if isinstance(i, int):
                    return t[:, i, a:b]
                return t[:, bass.ds(i, 1), a:b].rearrange("p a t -> p (a t)")

            def vcol(name, i):
                return V(name, i) if isinstance(i, int) else vec[:, bass.ds(VOFF[name] + i, 1)]

            def mcol(i, s):
                return mod[:, i, s:s + 1] if isinstance(i, int) else \
                    mod[:, bass.ds(i, 1), s:s + 1].rearrange("p a s -> p (a s)")

            def lo(pair, src, hi_name, value, done):
                dve.wait_ge(S(hi_name), value)
                dve.tensor_tensor(pair[1], src, pair[0].bitcast(F32), ALU.subtract).then_inc(S(done), 1)

            def lo_rest(name):
                pair, src, hi_name, before, done, n = SPLITS[name]
                for g in range(n, NG):
                    dve.wait_ge(S(hi_name), before + g + 1)
                    dve.tensor_tensor(group(pair[1], g), group(src, g), group(pair[0], g).bitcast(F32), ALU.subtract
                                      ).then_inc(S(done + "_dve"), 1)

            def log1p(z, w, w2, acc):
                go(dve.tensor_scalar(w, z, 2.0, None, ALU.add)); sync()
                go(dve.reciprocal(w, w)); sync()
                go(dve.tensor_tensor(w, w, z, ALU.mult)); sync()
                go(dve.tensor_tensor(w2, w, w, ALU.mult)); sync()
                go(dve.tensor_scalar(acc, w2, 1.0 / 15, None, ALU.mult)); sync()
                for k in range(6, 0, -1):
                    go(dve.scalar_tensor_tensor(acc, acc, 1.0 / (2 * k + 1), w2, ALU.add, ALU.mult)); sync()
                go(dve.scalar_tensor_tensor(acc, acc, 1.0, w, ALU.add, ALU.mult)); sync()
                go(dve.tensor_scalar(acc, acc, 2.0, None, ALU.mult)); sync()

            def inv_sqrt(dst, total, n, eps):
                go(dve.tensor_scalar(dst, total, 1.0 / n, eps, ALU.mult, ALU.add))
                event("var_ready")
                dve.wait_ge(S("root_done"), events["var_ready"])
                go(dve.reciprocal(dst, dst)); sync()

            def group(t, g):
                return t[:, g * GR:(g + 1) * GR, :]

            def layer_norm(x, total, sum_sem, centred, each, name, scaled=None):
                dve.wait_ge(S(sum_sem), 1)
                for g in range(NG):
                    dve.scalar_tensor_tensor(group(x, g), bc(total[0][:, 0:T], GR), -1.0 / D, group(x, g),
                                             ALU.mult, ALU.add).then_inc(S(centred), 1)
                dve.wait_ge(S(centred), NG)
                dve.wait_ge(S(sum_sem), 2)
                inv_sqrt(rstd[:], total[1][:, 0:T], D, LN_EPS)
                for g in range(NG):
                    go(dve.tensor_tensor(group(x, g), group(x, g), bc(rstd[:], GR), ALU.mult)); sync()
                    for c in range(g * GR, (g + 1) * GR):
                        each(c)
                    event(name)

            def acc_start():
                go(dve.memset(hacc[:], 0.0)); sync()

            def add_acc(x, s, i):
                dve.wait_ge(tile_free["D"], TILES + s.td + i)
                return dve.tensor_tensor(hacc[:], hacc[:], x, ALU.add)

            def add_square(x, s, i):
                sync()
                dve.wait_ge(tile_free["D"], TILES + s.td + i)
                go(dve.tensor_tensor(hsq[:], x, x, ALU.mult)); sync()
                return dve.tensor_tensor(hacc[:], hacc[:], hsq[:], ALU.add)

            def acc_done(s):
                dve.wait_ge(tile_free["D"], TILES + s.td + s.npi * s.iters * s.tiles)
                event("h_acc")

            def event(name):
                sync()
                dve.memset(tick[:], 0.0).then_inc(S(name), 1)
                dve.wait_ge(S(name), events.setdefault(name, 0) + 1)
                events[name] += 1
            events = {}

            for i, (sem_, n) in enumerate(((half_done, NBUF), (tile_free["D"], TILES), (tile_free["A"], TILES),
                                           (S("v_tok"), 1), (S("g_done"), 2), (S("g_used"), 2),
                                           (S("init"), 1))):
                dve.memset(rstd[:, i:i + 1], 0.0).then_inc(sem_, n)

            ada_start(0)
            dve.wait_ge(plain_done, 2 * KC)
            for b in (0, 2, 4, 6):
                dve.tensor_copy(arow[:, b * 512:(b + 1) * 512], bank[b][0:2, :]).then_inc(S("ada_rows"), 1)
            dve.wait_ge(S("ada_cols"), 1)
            dve.wait_ge(S("vec_in"), 16)
            dve.wait_ge(S("init"), 1)
            go(dve.tensor_tensor(mod[:, 0:32, :], bank[4][:, 0:64].rearrange("p (c s) -> p c s", s=2),
                                 V("ada_b", 0, 32).unsqueeze(2).to_broadcast([P, 32, 2]), ALU.add)); sync()
            go(dve.tensor_scalar(mod[:, 16:32, :], mod[:, 16:32, :], 1.0, None, ALU.add)); sync()
            for x, s, tmp, name in ((h, 0, tl_, "x_in"), (tc_, 1, tc_, "ctx_in")):
                dve.wait_ge(S(name), 16)

                def body(c, x=x, s=s, tmp=tmp):
                    go(dve.tensor_scalar(at(tmp, c), at(x, c), mcol(16 + c, s), mcol(c, s), ALU.mult, ALU.add))
                chunks(body, "xm_tmp")
            lo([xc[0][:], xc[1][:]], tc_[:], "xm_hi", 2 * NG, "xm_ctx")

            dve.wait_ge(S("xm_ctx"), 1)
            s = PLAN["gates"]
            dve.wait_ge(half_done, NBUF + 2 * s.n0 + 2)
            for m in range(2):
                a = T - m * T
                ps = bank[(s.t0 + m) % TILES]
                go(dve.tensor_scalar(gi[:, a:a + T], ps[0:64, 0:T], vec[0:64, VOFF["gate_b"]:VOFF["gate_b"] + 1], None,
                                     ALU.add))
                dve.tensor_copy(gf[:, a:a + T], ps[64:128, 0:T]).then_inc(tile_free["D"], 1)
            dve.wait_ge(tile_free["D"], TILES + 2)
            go(dve.tensor_scalar(gf[:], gf[:], vec[0:64, VOFF["gate_b"] + 1:VOFF["gate_b"] + 2], None, ALU.add)); sync()
            go(dve.scalar_tensor_tensor(gt[:], gf[:], -1.0, gf[:], ALU.mult, ALU.max))
            event("gate_abs")
            dve.wait_ge(S("gate_exp"), 1)
            s = sv = PLAN["v"]

            def v_out(i):
                dve.wait_ge(S("vt_done"), i + 1)
                dve.tensor_copy(vv[:, :, i * P:(i + 1) * P], bank[6][:].rearrange("p (t f) -> p t f", t=4)
                                ).then_inc(S("v_tok"), 1)

            def v_step(i):
                it, j = i // sv.npi, i % sv.npi
                if i >= 2:
                    ada(sv, j, it)
                dve.wait_ge(half_done, NBUF + 2 * (sv.n0 + i) + 2)
                for m in range(2):
                    dve.tensor_copy(vst[:, j % 2, m, :], bank[(sv.t0 + 2 * j + m) % TILES][:, 0:T]
                                    ).then_inc(tile_free["D"], 1)
                if i:
                    v_out(i - 1)
                if i < 2:
                    ada(sv, j, it)

            log1p(gw[:], gt[:], gp[:], gq[:])
            v_step(0)
            go(dve.tensor_scalar(gf[:], gf[:], 0.0, None, ALU.min)); sync()
            go(dve.tensor_tensor(gf[:], gf[:], gq[:], ALU.subtract))
            go(dve.memset(gp[:], 0.0)); sync()

            def scan(dst, src, other, op, init):
                go(dve.tensor_tensor_scan(dst[0:4, :], src[0:4, :], other[0:4, :], init, op, op))
                go(dve.tensor_tensor_scan(dst[32:36, T - 1::-1], src[32:36, T - 1::-1], other[32:36, T - 1::-1],
                                          init, op, op)); sync()
                go(dve.tensor_tensor_scan(dst[32:36, 2 * T - 1:T - 1:-1], src[32:36, 2 * T - 1:T - 1:-1],
                                          other[32:36, 2 * T - 1:T - 1:-1], dst[32:36, 0:1], op, op)); sync()
            scan(gt, gf, gp, ALU.add, 0.0)
            go(dve.tensor_tensor(gi[:], gi[:], gt[:], ALU.subtract))
            event("a_rows")
            v_step(1)
            scan(gw, gi, gi, ALU.max, 0.0)
            go(dve.tensor_copy(mrow[:], gw[:, T:2 * T]))
            go(dve.tensor_tensor(erow[:], gw[:, T:2 * T], gt[:, T:2 * T], ALU.add))
            sync()
            go(dve.tensor_scalar(erow[:], erow[:], -88.0, None, ALU.max))
            event("m_rows")

            for i in range(2, sv.npi * sv.iters):
                v_step(i)
            v_out(sv.npi * sv.iters - 1)

            def conv3(name, dst, i, ps, a):
                go(dve.tensor_scalar(at(dst, i, a, a + T), ps, vcol(name, 8 + i), None, ALU.mult)); sync()
                go(dve.scalar_tensor_tensor(at(dst, i, a + 1, a + T), ps[:, 0:T - 1], vcol(name, i),
                                            at(dst, i, a + 1, a + T), ALU.mult, ALU.add)); sync()
                return dve.scalar_tensor_tensor(at(dst, i, a, a + T - 1), ps[:, 1:T], vcol(name, 16 + i),
                                                at(dst, i, a, a + T - 1), ALU.mult, ALU.add)
            dve.wait_ge(S("a_cols"), 1)
            go(dve.tensor_copy(acol[:].rearrange("p d t h -> p (d t h)"), bank[5][:, 0:32])); sync()
            s = PLAN["k"]

            def k_body(it):
                for j in range(s.npi):
                    ada(s, j, it)
                    dve.wait_ge(half_done, NBUF + 2 * (s.n0 + j + it * s.npi) + 2)
                    for m in range(2):
                        conv3("conv_k", kk, it * s.npi + j, bank[(s.t0 + 2 * j + m) % TILES][:, 0:T], T - m * T
                              ).then_inc(tile_free["D"], 1)
            ada_start(1)
            loop(s.iters, 4 * s.npi, k_body)
            ada_start(2)
            run("q", lambda i, ps, _: conv3("conv_q", qq, i, ps, 0), per=2 * 4)
            ada_only("o")
            ada_only("zm")
            dve.wait_ge(half_done, NBUF + 2 * PLAN["q"].n0)
            go(dve.memset(upad[:], 0.0)); sync()
            run("up", lambda i, ps, _: dve.tensor_copy(
                at(upad, i).rearrange("p (r c) -> p r c", r=4)[:, :, PAD:PAD + ROW],
                ps.rearrange("p (r c) -> p r c", r=4)))
            dve.wait_ge(tile_free["D"], TILES + PLAN["zp"].td)
            dve.wait_ge(S("ada_sum"), 3)
            go(dve.tensor_tensor(mod[:, 32:80, 0], bank[4][:, 64:112], V("ada_b", 32, 48), ALU.add)); sync()
            go(dve.tensor_scalar(mod[:, 64:80, 0], mod[:, 64:80, 0], 1.0, None, ALU.add))
            pa, pb_ = ps_[0], ps_[1]
            for g in range(4):
                u = upad[:, 2 * g:2 * g + 2, :].rearrange("p c (r w) -> p (c r) w", r=4)
                go(dve.tensor_tensor(pa[:, :, 1:80], u[:, :, 0:79], u[:, :, 1:80], ALU.add)); sync()
                res, oth = pa, pb_
                for half, a, b in ((1, 2, 79), (2, 4, 77), (4, 8, 73))[:g]:
                    go(dve.tensor_tensor(oth[:, :, a:b], res[:, :, a - half:b - half], res[:, :, a + half:b + half],
                                         ALU.add)); sync()
                    res, oth = oth, res
                go(dve.tensor_tensor(oth[:, :, 0:ROW], res[:, :, PAD:PAD + ROW],
                                     bc(C("invcnt", g * ROW, (g + 1) * ROW), 8), ALU.mult)); sync()
                go(dve.tensor_tensor(u[:, :, PAD:PAD + ROW], oth[:, :, 0:ROW], u[:, :, PAD:PAD + ROW], ALU.subtract))
                sync()
            event("pooled")
            dve.wait_ge(plain_done, PLAN["poolw"].p0 + 1)
            dve.wait_ge(tile_free["A"], TILES + PLAN["poolw"].ta)
            for c in range(8):
                go(dve.scalar_tensor_tensor(silp[:, c, :], bank[c // 2][:, (c % 2) * T:(c % 2 + 1) * T],
                                            V("pool_s", c), silp[:, c, :], ALU.mult, ALU.mult))
            event("yp_done")

            tri = {0: C("tri_u"), 1: C("tri_l")}

            def h_math(i):
                hd, d = i // 2, i % 2
                num, den = bank[2 * (i % 2)], bank[2 * (i % 2) + 1]
                dve.wait_ge(S("num_done"), i + 1)
                go(dve.scalar_tensor_tensor(dn[:], den[:, 0:T], -1.0, ebc[i % 2][:], ALU.mult, ALU.max)); sync()
                go(dve.tensor_tensor(dn2[:], den[:, 0:T], dn[:], ALU.max)); sync()
                go(dve.reciprocal(dn[:], dn2[:])); sync()
                dst = hs[:, 2 * hd:2 * hd + 2, :] if d == 0 else ht[:]
                dve.tensor_tensor(dst, num[:].rearrange("p (c t) -> p c t", c=2), bc(dn[:], 2), ALU.mult
                                  ).then_inc(S("num_used"), 1)
                dve.wait_ge(S("num_used"), i + 1)
                if d == 1:
                    go(dve.tensor_tensor(hs[:, 2 * hd:2 * hd + 2, :], hs[:, 2 * hd:2 * hd + 2, :], ht[:], ALU.add))
                    sync()

            def probs_args(i):
                hd, d = i // 2, i % 2
                dve.wait_ge(S("bc_done"), i + 1)
                for t in range(4):
                    go(dve.tensor_scalar(pt[i % 2][:, t, :], bank[7][:, 0:T], acol[:, d, t, hd:hd + 1], 0.0,
                                         ALU.subtract, ALU.max))
                dve.tensor_copy(ebc[i % 2][:], bank[7][:, T:2 * T]).then_inc(S("bc_used"), 1)
                dve.wait_ge(S("bc_used"), i + 1)
                event("args")

            def probs(i):
                hd, d = i // 2, i % 2
                dve.wait_ge(S("gexp"), i + 1)
                a = pt[i % 2]
                for t, q in ((2, 0), (3, 1)):
                    go(dve.tensor_tensor(a[:, t, q * P:(q + 1) * P], a[:, t, q * P:(q + 1) * P], tri[d], ALU.mult))
                sync()
                if d == 0:
                    dve.wait_ge(S("scores_done"), hd + 1)
                for b in range(2):
                    go(dve.scalar_tensor_tensor(a[:, 2 * b:2 * b + 2, :],
                                                bank[5 + b][:].rearrange("p (t q) -> p t q", t=2), 1.0 / 16,
                                                a[:, 2 * b:2 * b + 2, :], ALU.mult, ALU.mult))
                event("probs_ready")

            def head_gate(g):
                x = hs[:, 2 * g:2 * g + 2, :]
                go(dve.tensor_tensor(x, x, sigo[:, 2 * g:2 * g + 2, :], ALU.mult))
                event("hn_in")

            def head_centre(g):
                x = hs[:, 2 * g:2 * g + 2, :]
                dve.wait_ge(S("hn_sum"), 2 * g + 1)
                go(dve.scalar_tensor_tensor(x, bc(bank[4][:, 0:T], 2), -1.0 / 256, x, ALU.mult, ALU.add))
                event("hc")

            def head_var(g):
                dve.wait_ge(S("hn_sum"), 2 * g + 2)
                go(dve.tensor_scalar(hr[:, g, :], bank[4][:, T:2 * T], 1.0 / 256, LN_EPS, ALU.mult, ALU.add))
                event("var_ready")
                return events["var_ready"]

            def head_out(g, value):
                x = hs[:, 2 * g:2 * g + 2, :]
                dve.wait_ge(S("root_done"), value)
                go(dve.reciprocal(hr[:, g, :], hr[:, g, :])); sync()
                go(dve.tensor_tensor(x, x, bc(hr[:, g, :], 2), ALU.mult)); sync()
                for c in (2 * g, 2 * g + 1):
                    go(dve.scalar_tensor_tensor(silm[:, c, :], hs[:, c, :], V("mh_g", c), silm[:, c, :],
                                                ALU.mult, ALU.mult))
                if g % 2:
                    event("y0")

            for i in range(2 * NH + 3):
                if i < 2 * NH:
                    probs_args(i)
                if i >= 4 and i % 2 == 0:
                    value = head_var((i - 4) // 2)
                if i < 2 * NH:
                    probs(i)
                if 1 <= i <= 2 * NH:
                    h_math(i - 1)
                if i >= 3 and i % 2:
                    head_centre((i - 3) // 2)
                if 2 <= i <= 2 * NH and i % 2 == 0:
                    head_gate((i - 2) // 2)
                if i >= 4 and i % 2 == 0:
                    head_out((i - 4) // 2, value)
            for g in range(2):
                event("y0")
            lo_rest("out0")

            go(dve.tensor_tensor(mod[:, 64:80, 1], mod[:, 64:80, 0], V("pln_g", 0, KC), ALU.mult))
            go(dve.tensor_tensor(mod[:, 48:64, 1], mod[:, 64:80, 0], V("pln_b", 0, KC), ALU.mult)); sync()
            go(dve.tensor_tensor(mod[:, 48:64, 1], mod[:, 48:64, 1], mod[:, 48:64, 0], ALU.add)); sync()
            dve.wait_ge(S("ax0"), 1)

            def residual(name, col):
                s = PLAN[name]
                acc_start()

                def evac(i, ps, _):
                    go(dve.scalar_tensor_tensor(at(h, i), ps, mcol(col + i, 0), at(h, i), ALU.mult, ALU.add)); sync()
                    return add_acc(at(h, i), s, i)
                run(name, evac, per=4)
                acc_done(s)
            ada_start(3)
            residual("out0", 32)

            def body(c):
                go(dve.tensor_scalar(tx[:, c, :], h[:, c, :], mcol(64 + c, 1), mcol(48 + c, 1), ALU.mult, ALU.add))
            layer_norm(h, (bank[5], bank[6]), "ln0_sum", "ln0_c", body, "xm1_tmp")
            lo_rest("v1")
            for c in range(KC):
                go(dve.tensor_scalar(h[:, c, :], h[:, c, :], V("pln_g", c), V("pln_b", c), ALU.mult, ALU.add))
            event("h1_ready")
            dve.wait_ge(S("ada_sum"), 4)
            go(dve.tensor_tensor(mod[:, 80:96, 0], bank[4][:, 112:128], V("ada_b", 80, 16), ALU.add)); sync()
            acc_start()

            def v1_evac(i, ps, _):
                go(dve.tensor_copy(at(vf, i), ps)); sync()
                return add_acc(at(vf, i), PLAN["v1"], i)
            run("v1", v1_evac, per=4)
            acc_done(PLAN["v1"])

            def body(c):
                go(dve.tensor_scalar(vf[:, c, :], vf[:, c, :], V("sgu_g", c), V("sgu_b", c), ALU.mult, ALU.add))
            layer_norm(vf, (bank[5], bank[6]), "lnv_sum", "lnv_c", body, "v1_norm")
            run("u1", lambda i, ps, _: dve.tensor_copy(at(uu, i), ps))
            for g in range(8):
                dve.wait_ge(S("v1_tp"), g + 1)
                dve.tensor_copy(vt1[:, g // 4, (g % 4) * 512:(g % 4 + 1) * 512], bank[5 + g % 2][:]
                                ).then_inc(S("v1_tok"), 1)
            for c in range(KC):
                if c < KC - 1:
                    dve.wait_ge(S("sgu_done"), c + 1)
                else:
                    dve.wait_ge(plain_done, PLAN["wsp"].p0 + 1)
                dve.tensor_tensor(uu[:, c, :], uu[:, c, :], bank[4 + c % 4][:, 0:T], ALU.mult
                                  ).then_inc(S("sgu_used"), 1)
            dve.wait_ge(S("sgu_used"), KC)
            dve.wait_ge(tile_free["A"], TILES + PLAN["wsp"].ta)
            for g in range(NG):
                go(dve.tensor_tensor(group(uu, g), group(uu, g), group(zz, g), ALU.mult))
                event("y1")
            lo_rest("out1")
            dve.wait_ge(S("ax1"), 1)
            residual("out1", 80)

            def body(c):
                go(dve.tensor_scalar(h[:, c, :], h[:, c, :], V("pln_g", 16 + c), V("pln_b", 16 + c), ALU.mult, ALU.add))
            layer_norm(h, (bank[5], bank[6]), "ln1_sum", "ln1_c", body, "h_ready")
            def normed(i, g, dst, name):
                dve.wait_ge(S("rms_sum"), i)
                inv_sqrt(rstd[:], bank[0 if i == 3 else 7][:, 0:T], D, RMS_EPS)

                def body(c):
                    go(dve.scalar_tensor_tensor(at(dst, c), at(h, c), vcol(g, c), rstd[:], ALU.mult, ALU.mult))
                chunks(body, name)
            normed(1, "attn_n", rt, "rms_t")
            lo_rest("cc")
            run("cc", lambda i, ps, _: dve.tensor_copy(at(cr, i), ps))
            dve.wait_ge(tile_free["D"], TILES + PLAN["uv"].td)
            event("c_evac")
            for i, (b, n, a, name) in enumerate(((5, 4, 6, "kv_n"), (6, 6, 0, "q_n"))):
                dve.wait_ge(S("c_sum"), i + 1)
                inv_sqrt(rstd[:], bank[b][:, 0:T], n * P, RMS_EPS)
                for c in range(n):
                    go(dve.scalar_tensor_tensor(cr[:, a + c, :], cr[:, a + c, :], V(name, c), rstd[:],
                                                ALU.mult, ALU.mult))
                event("c_norm")
                lo([cn[0][:, a:a + n, :], cn[1][:, a:a + n, :]], cr[:, a:a + n, :], "cn_hi", i + 1, "cn_ready")

            def c2(name):
                return con2[:, C2OFF[name]:C2OFF[name] + dict(CON2)[name]]

            def rotate(x, value):
                dve.wait_ge(S("rope_done"), value)
                ps = bank[7] if value == 1 else bank[5 + value % 2]
                go(dve.tensor_tensor(rr[:], ps[:, 0:T], c2("sin"), ALU.mult))
                go(dve.tensor_tensor(x, x, c2("cos"), ALU.mult)); sync()
                ins = dve.tensor_tensor(x, x, rr[:], ALU.add).then_inc(S("rope_used"), 1)
                dve.wait_ge(S("rope_used"), value)
                return ins
            dve.wait_ge(S("con2_in"), 16)
            rotate(cr[:, 10, :], 1)
            go(dve.memset(kpe[:], 0.0)); sync()
            for a in range(2):
                go(dve.tensor_copy(kpe[64 * a:64 * a + 64, a, :], cr[64 * a:64 * a + 64, 10, :]))
            sync()
            run("uv", lambda i, ps, _: dve.tensor_copy(at(v2f, i), ps))
            run("uk", lambda i, ps, _: dve.tensor_copy(at(kn, i), ps))
            for g in range(8):
                dve.wait_ge(S("v2_tp"), g + 1)
                dve.tensor_copy(vt2[:, g // 4, (g % 4) * 512:(g % 4 + 1) * 512], bank[5 + g % 2][:]
                                ).then_inc(S("v2_tok"), 1)
            run("uq", lambda i, ps, _: dve.tensor_copy(at(q2, i), ps))
            dve.wait_ge(tile_free["D"], TILES + PLAN["ao"].td)
            for j in range(8):
                rotate(q2[:, 16 + j, :], j + 2)

            def att_mask(hd):
                dve.wait_ge(S("att_s"), hd + 1)
                dve.scalar_tensor_tensor(flat(sm[hd % 2][:]), bank[hd % 2][:], SCALE, c2("causal"), ALU.mult, ALU.add
                                         ).then_inc(S("att_masked"), 1)
                dve.wait_ge(S("att_masked"), hd + 1)
                m = mx[:, 2 * (hd % 4):2 * (hd % 4) + 2]
                go(dve.tensor_reduce(m, sm[hd % 2][:], AX, ALU.max)); sync()
                go(dve.tensor_scalar(m, m, -1.0, None, ALU.mult))
                event("att_max")

            def att_norm(hd):
                dve.wait_ge(S("att_exp"), 2 * hd + 2)
                a = 2 * (hd % 4)
                go(dve.reciprocal(mx[:, 32 + a:34 + a], mx[:, 16 + a:18 + a])); sync()
                for t in range(2):
                    go(dve.tensor_scalar(sm[hd % 2][:, t, :], sm[hd % 2][:, t, :], mx[:, 32 + a + t:33 + a + t], None,
                                         ALU.mult))
                event("att_p")

            def att_turn(hd):
                dve.wait_ge(S("att_tp"), hd + 1)
                dve.tensor_copy(flat(ptt[hd % 2][:]), bank[2][:]).then_inc(S("att_pt"), 1)

            def att_out(hd):
                dve.wait_ge(S("o_hi"), hd + 1)
                dve.tensor_tensor(oh[1][:, hd, :], bank[5 + hd % 2][:, 0:T], oh[0][:, hd, :].bitcast(F32), ALU.subtract
                                  ).then_inc(S("o_ready"), 1)

            att_mask(0)
            for hd in range(HEADS):
                att_norm(hd)
                if hd + 1 < HEADS:
                    att_mask(hd + 1)
                att_turn(hd)
                if hd >= 1:
                    att_out(hd - 1)
            att_out(HEADS - 1)
            run("ao", lambda i, ps, _: dve.tensor_copy(at(ya, i), ps))

            s1, s2, s3 = (rw[:, 3, i * KC:(i + 1) * KC] for i in range(3))
            go(dve.scalar_tensor_tensor(lam_s[:], V("lam", 0, KC), -1.0, V("lam", 0, KC), ALU.mult, ALU.max))
            event("lam_abs")

            def conv4(i, ps, _):
                x = at(xcv, i)
                go(dve.tensor_scalar(x, ps, vcol("conv_w", 48 + i), vcol("conv_b", i), ALU.mult, ALU.add)); sync()
                for j in (2, 1, 0):
                    ins = dve.scalar_tensor_tensor(at(xcv, i, 3 - j, T), ps[:, 0:T - 3 + j], vcol("conv_w", 16 * j + i),
                                                   at(xcv, i, 3 - j, T), ALU.mult, ALU.add)
                    if j:
                        go(ins); sync()
                return ins
            run("xr", conv4, per=3 * 4)
            dve.wait_ge(S("lam_exp"), 1)
            log1p(lam_s[:], s1, s2, s3)
            go(dve.tensor_scalar(s1, V("lam", 0, KC), -1.0, 0.0, ALU.mult, ALU.max)); sync()
            go(dve.tensor_tensor(lam_s[:], s1, s3, ALU.add)); sync()
            go(dve.tensor_scalar(lam_s[:], lam_s[:], -8.0, None, ALU.mult)); sync()
            for c in range(KC):
                dve.wait_ge(S("rg_r"), c + 1)
                go(dve.tensor_scalar(la[:, c, :], xr[:, c, :], lam_s[:, c:c + 1], None, ALU.mult))
                dve.wait_ge(S("rg_used"), c + 1)
                dve.tensor_tensor(xcv[:, c, :], xcv[:, c, :], rw[:, c % 2, :], ALU.mult).then_inc(S("ix_used"), 1)
            event("la_ready")
            dve.wait_ge(S("a_ready"), 2)
            def ga_mult(a, b):
                for c in range(a, b):
                    dve.wait_ge(tile_free["A"], TILES + PLAN["ga"].ta + c + 1)
                    dve.tensor_tensor(ya[:, c, :], ya[:, c, :], yr[:, c, :], ALU.mult).then_inc(S("ga_used"), 1)

            for g in range(NG):
                go(dve.tensor_tensor(rw[:], group(xr, g), group(xr, g), ALU.mult)); sync()
                go(dve.scalar_tensor_tensor(group(la, g), rw[:], 1.0, group(la, g), ALU.add, ALU.mult)); sync()
            go(dve.tensor_scalar(flat(la[:]), flat(la[:]), -1.0, 1e-30, ALU.mult, ALU.max))
            event("m2_ready")
            ga_mult(0, 8)
            dve.wait_ge(S("mult_ready"), 1)
            go(dve.memset(la[:, :, 0:1], 1.0)); sync()
            dve.wait_ge(S("ix_used"), KC)
            go(dve.tensor_tensor(xcv[:], xcv[:], la[:], ALU.mult)); sync()
            for c in range(KC):
                go(dve.tensor_tensor_scan(la[:, c, :], xr[:, c, :], xcv[:, c, :], 0.0, ALU.mult, ALU.add))
            event("scanned")
            ga_mult(8, KC)
            dve.wait_ge(tile_free["A"], TILES + PLAN["gr"].ta)
            for g in range(NG):
                go(dve.tensor_tensor(group(yr, g), group(yr, g), group(la, g), ALU.mult))
                event("ry_t")
            lo_rest("ro")
            dve.wait_ge(tile_free["A"], TILES + PLAN["ro"].ta)

            def mix(i, ps, k):
                go(dve.tensor_tensor(rw[:, k % 2, :], ps, at(xr, i), ALU.mult)); sync()
                return dve.tensor_tensor(at(ya, i), at(ya, i), rw[:, k % 2, :], ALU.add)
            run("ro", mix, per=4)
            dve.wait_ge(tile_free["D"], TILES + PLAN["wo"].td)
            for g in range(NG):
                event("mix_t")
            lo_rest("wo")

            def add_h(i, ps, _):
                go(dve.tensor_tensor(at(h, i), ps, at(h, i), ALU.add))
                return add_square(at(h, i), PLAN["wo"], i)
            acc_start()
            run("wo", add_h, per=2 * 4)
            acc_done(PLAN["wo"])
            normed(2, "ffn_n", rt, "rms_t")
            lo_rest("pq")
            run("pq", lambda i, ps, _: dve.tensor_copy(at(pqq, i), ps))
            for g in range(8):
                if g < 7:
                    dve.wait_ge(S("s_done"), g + 1)
                else:
                    dve.wait_ge(plain_done, PLAN["sk"].p0 + 1)
                dve.tensor_copy(flat(ss[:, g // 4, 4 * (g % 4):4 * (g % 4) + 4, :]), bank[5 + g % 2][:]
                                ).then_inc(S("s_evac"), 1)
            dve.wait_ge(S("s_evac"), 8)

            def top16(rows, vals, idx):
                for r in range(2):
                    for x, v, _ in zip(rows, vals, idx):
                        go(dve.max(v[:, 8 * r:8 * r + 8], x))
                    sync()
                    for x, v, i in zip(rows, vals, idx):
                        go(dve.max_index(i[:, 8 * r:8 * r + 8], v[:, 8 * r:8 * r + 8], x))
                    sync()
                    if r == 0:
                        for x, v, _ in zip(rows, vals, idx):
                            go(dve.match_replace(x, v[:, 0:8], x, -BIG))
                        sync()
            pairs = [(t, c) for t in range(2) for c in range(16)]
            top16([ss[:, t, c, :] for t, c in pairs], [tv[:, t, c, :] for t, c in pairs],
                  [ti[:, t, c, :] for t, c in pairs])
            go(dve.tensor_copy(tf[:], ti[:])); sync()
            four = [P, 8, TOPK, TOPK]
            for t in range(2):
                v2 = tv[:, t, :, :].rearrange("p (h c) k -> p h c k", c=2)
                i2 = tf[:, t, :, :].rearrange("p (h c) k -> p h c k", c=2)
                go(dve.tensor_tensor(cand[:].rearrange("p h (a b) -> p h a b", a=TOPK),
                                     v2[:, :, 0, :].unsqueeze(3).to_broadcast(four),
                                     v2[:, :, 1, :].unsqueeze(2).to_broadcast(four), ALU.add)); sync()
                top16([cand[:, k, :] for k in range(8)], [bv[:, t, k, :] for k in range(8)],
                      [bi[:, t, k, :] for k in range(8)])
                dst = gg[:, t, 2, :, :]
                go(dve.tensor_copy(dst, bv[:, t, :, 0:1].to_broadcast([P, 8, TOPK]))); sync()
                go(dve.tensor_tensor(bv[:, t, :, :], bv[:, t, :, :], dst, ALU.subtract))
                for c in range(2):
                    if c == 0:
                        go(dve.tensor_scalar(bj[:, t, :, :], bi[:, t, :, :], 4, None, ALU.logical_shift_right))
                    else:
                        go(dve.tensor_scalar(bj[:, t, :, :], bi[:, t, :, :], 15, None, ALU.bitwise_and))
                    sync()
                    go(dve.tensor_copy(bf[:, t, :, :], bj[:, t, :, :])); sync()
                    e = ceq[:].rearrange("p h (k a) -> p h k a", k=TOPK)
                    for k in range(8):
                        go(dve.tensor_tensor(e[:, k], bf[:, t, k, :].unsqueeze(2).to_broadcast([P, TOPK, TOPK]),
                                             bc(C("iota", 0, TOPK), TOPK), ALU.is_equal))
                    sync()
                    go(dve.tensor_tensor(e, e, i2[:, :, c, :].unsqueeze(2).to_broadcast(four), ALU.mult)); sync()
                    go(dve.tensor_reduce(gg[:, t, c, :, :], e, AX, ALU.add)); sync()
            event("topk_done")
            dve.wait_ge(S("gate_e"), 1)
            for t in range(2):
                go(dve.tensor_reduce(gs[:, t, 0, :], bv[:, t, :, :], AX, ALU.add)); sync()
                go(dve.reciprocal(gs[:, t, 1, :], gs[:, t, 0, :])); sync()
                go(dve.tensor_tensor(gg[:, t, 2, :, :], bv[:, t, :, :],
                                     gs[:, t, 1, :].unsqueeze(2).to_broadcast([P, 8, TOPK]), ALU.mult))
                event("gates_tok")
            dve.wait_ge(S("gT_done"), 1)
            for t in range(2):
                dve.tensor_copy(gT[:, :, t * P:(t + 1) * P], bank[5 + t][:, 0:3 * P].rearrange("p (i t) -> p i t", i=3)
                                ).then_inc(S("gT_read"), 1)
            dve.wait_ge(S("gT_read"), 2)
            gate = gT[:, 2, :]
            go(dve.tensor_copy(gb[:, 0, :], gate)); sync()
            go(dve.tensor_tensor(gres[:], gate, gb[:, 0, :], ALU.subtract)); sync()
            go(dve.tensor_copy(gb[:, 1, :], gres[:]))
            go(dve.tensor_copy(gate, gb[:, 0, :])); sync()
            go(dve.tensor_tensor(gres[:], gres[:], gb[:, 1, :], ALU.subtract)); sync()
            go(dve.tensor_copy(gb[:, 2, :], gres[:]))
            event("gate_parts")
            groups = T // TG
            for r in range(2):
                def hot_2(i, k, r=r):
                    dve.tensor_tensor(oe[k][:], bc(C("iota", r * I2, (r + 1) * I2), TG),
                                      gT[:, 1, bass.ds(i * TG, TG)].unsqueeze(2).to_broadcast([P, TG, I2]),
                                      ALU.is_equal).then_inc(S("hot_2"), 1)

                def hot_1(i, k, r=r):
                    dve.wait_ge(S("g_done"), r * groups + 1 + i)
                    dve.tensor_tensor(oa[k][:], bc(C("iota"), TG), gT[:, 0, bass.ds(i * TG, TG)].unsqueeze(2)
                                      .to_broadcast([P, TG, NKEY]), ALU.is_equal).then_inc(S("hot_1"), 1)

                def gated(i, k, r=r):
                    dve.wait_ge(S("g_done"), r * groups + 3 + i)
                    w_ = W[:, :, bass.ds(i * TG, TG)]
                    dve.tensor_tensor(w_, w_, bank[5 + k][:, :].rearrange("p (t i) -> p i t", t=TG), ALU.mult
                                      ).then_inc(S("g_used"), 1)
                for k in range(2):
                    hot_2(k, k)
                    hot_1(k, k)
                dve.wait_ge(tile_free["A"], TILES + PLAN[f"peer_v{r}"].ta)

                def w_body(it, r=r):
                    for k in range(2):
                        i = it * 2 + k
                        dve.wait_ge(S("hot_g0"), r * groups + k + 1 + it * 2)
                        dve.wait_ge(S("hot_g12"), r * groups + k + 1 + it * 2)
                        hot_2(i + 2, k)
                        gated(i, k)
                        hot_1(i + 2, k)
                loop(groups // 2 - 1, 0, w_body)
                for k in range(2):
                    gated(groups - 2 + k, k)
                dve.wait_ge(S("g_used"), (r + 1) * groups + 2)

                def wl_body(it, r=r):
                    for j in range(4):
                        i = it * 4 + j
                        dve.wait_ge(S("wr_hi"), r * I2 + j + 1 + it * 4)
                        dve.tensor_tensor(wr[j % 2][:, 1, :], at(W, i), wr[j % 2][:, 0, :].bitcast(F32), ALU.subtract
                                          ).then_inc(S("wr_ready"), 1)
                loop(PLAN[f"peer_v{r}"].iters, 0, wl_body)
                s = PLAN[f"peer_v{r}"]
                dve.wait_ge(half_done, NBUF + 2 * (s.n0 + s.npi * s.iters))
                for b in range(8):
                    go(dve.tensor_tensor(flat(h[:, 2 * b:2 * b + 2, :]), flat(h[:, 2 * b:2 * b + 2, :]), bank[b][:],
                                         ALU.add))
                    if r == 1 and b % 2:
                        event("h_ready")
                    if r == 0 and b % 4 == 3:
                        event("acc_used")

            normed(3, "ple_n", rt, "rms_t")
            lo_rest("pg")
            acc_start()
            lo([pt_r[:, 0, :, :], pt_r[:, 1, :, :]], pt_x[:], "p_hi", 1, "p_ready")
            dve.wait_ge(tile_free["A"], TILES + PLAN["pp"].ta)

            def ple(i, ps, k):
                go(dve.tensor_tensor(ptile[:, k % 2, :], ps, at(sg, i), ALU.mult)); sync()
                go(dve.tensor_tensor(at(h, i), at(h, i), ptile[:, k % 2, :], ALU.add))
                return add_square(at(h, i), PLAN["pp"], i)
            run("pp", ple, per=3 * 16)
            acc_done(PLAN["pp"])
            normed(4, "fin_n", h, "final")


PER_TILE = {"uv": 4, "uk": 4, "uq": 6, "pp": 2}


def columns(v):
    return np.asarray(v).reshape(-1, P).T


def units(w, per=1):
    k, n = w.shape
    a = w.reshape(k // P, P, n // P // per, per, P).transpose(2, 1, 3, 0, 4)
    return a.reshape(n // P // per, P, -1)


def feature_major(x):
    return np.ascontiguousarray(np.asarray(x).reshape(x.shape[0], -1, P).transpose(2, 1, 0))


def constants():
    c = {"ident": np.eye(P), "ones": np.ones((P, P)), "tri_u": np.triu(np.ones((P, P))),
         "tri_l": np.tril(np.ones((P, P))), "iota": np.tile(np.arange(P), (P, 1))}
    pos = np.arange(ROW)
    inv = []
    for w in (2, 4, 8, 16):
        low, high = np.maximum(pos - w // 2, 0), np.minimum(pos + (w - 1 - w // 2), ROW - 1)
        inv.append(1.0 / (high - low + 1))
    c["invcnt"] = np.tile(np.concatenate(inv), (P, 1))
    inv_freq = (1.0 / (np.float32(10000.0) ** (np.arange(32, dtype=np.float32) / np.float32(32)))).astype(np.float32)
    ang = np.arange(T, dtype=np.float32)[None, :] * inv_freq[:, None]
    rot = np.zeros((P, P))
    for b in (0, 64):
        for i in range(32):
            rot[b + i + 32, b + i] = -1.0
            rot[b + i, b + i + 32] = 1.0
    q = np.arange(P)[:, None, None] + P * np.arange(2)[None, :, None]
    k = np.arange(T)[None, None, :]
    c2 = {"cos": np.tile(np.cos(ang), (4, 1)), "sin": np.tile(np.sin(ang), (4, 1)),
          "causal": np.where(k <= q, 0.0, -BIG).reshape(P, -1), "rot": rot}
    return (np.concatenate([c[n] for n, _ in CON], 1).astype(np.float32),
            np.concatenate([c2[n] for n, _ in CON2], 1).astype(np.float32))


def layout(a):
    f = np.float32
    w = np.zeros((N_UNITS, P, UNIT), f)

    def put(name, ns, ps=None):
        s = PLAN[name]
        if ns is not None:
            at = [s.u0 + it * len(s.pattern) + p for it in range(s.iters) for p in s.npos]
            w[at[:len(ns)], :, :ns.shape[2]] = ns
        if ps is not None:
            at = [s.u0 + it * len(s.pattern) + p for it in range(s.iters)
                  for p, kind in enumerate(s.pattern) if kind == "P"]
            w[at, :, :ps.shape[2]] = ps

    ada = a["ada_w"].reshape(2, KC, P, 3, D).transpose(0, 3, 1, 2, 4).reshape(6, KC, P, D)
    we = a["w_in_even"][0]
    m = D // 2
    put("ada_ss", None, ada[0:2].transpose(1, 0, 2, 3).reshape(2 * KC, P, D))
    ada = ada.reshape(6 * KC, P, D)
    g = np.zeros((D, P), f)
    gc = 5 * m
    for kind in range(2):
        for d in range(2):
            g[:, 64 * kind + 32 * d:64 * kind + 32 * d + 4] = we[:, gc + 8 * kind + 4 * d:gc + 8 * kind + 4 * d + 4]
    put("gates", units(g))
    left = 32
    cols = {"q": 0, "k": m, "v": 2 * m, "o": 3 * m, "zm": 4 * m, "up": gc + 16, "zp": gc + 16 + m}
    for name in ("v", "k", "q", "o", "zm", "up", "zp"):
        n = PLAN[name].ppi * PLAN[name].iters
        put(name, units(we[:, cols[name]:cols[name] + m]), ada[left:left + n] if n else None)
        left += n
    assert left == 80
    pw = a["pool_w"][0].reshape(4, 2, P, 2, P).transpose(2, 0, 1, 3, 4).reshape(1, P, -1)
    put("poolw", None, pw)
    put("out0", units(a["w_out_even"][0]), ada[left:])
    wo = a["w_in_odd"][0]
    put("u1", units(wo[:, 0:D]))
    put("v1", units(wo[:, D:2 * D]))
    put("z1", units(wo[:, 2 * D:]))
    sp = np.concatenate([a["w_sp"][0].transpose(2, 0, 1).reshape(P, -1),
                         np.broadcast_to(a["b_sp"][0].reshape(1, -1), (P, 8 * P))], 1)
    put("wsp", None, sp[None])
    put("out1", units(a["w_out_odd"][0]))
    wi = a["w_in_2"][0]
    kr = wi[:, 1280:1344]
    put("cc", units(np.concatenate([wi[:, 0:1280], kr, kr], 1)))
    o = 1344
    put("xr", units(wi[:, o:o + D]))
    put("yr", units(wi[:, o + D:o + 2 * D]))
    put("ga", units(wi[:, o + 2 * D:o + 3 * D]))
    put("gr", units(wi[:, o + 3 * D:o + 4 * D]))
    ukv = a["w_ukv_2"][0].reshape(512, HEADS, 2, P)
    put("uk", units(ukv[:, :, 0].reshape(512, D), 4))
    put("uv", units(ukv[:, :, 1].reshape(512, D), 4))
    uq = a["w_uq_2"][0].reshape(768, HEADS, 192)
    uq = np.concatenate([uq[:, :, 0:128].reshape(768, -1), uq[:, :, 128:].reshape(768, -1)], 1)
    put("uq", units(uq, 2))
    put("ao", units(a["w_attn_o_2"][0]))
    put("rg", None, np.stack([a["w_rg_a_2"][0].transpose(1, 0, 2).reshape(P, -1),
                              a["w_rg_x_2"][0].transpose(1, 0, 2).reshape(P, -1)]))
    put("ro", units(a["w_rnn_o_2"][0]))
    put("wo", units(a["w_out_2"][0]))
    put("pq", units(a["w_peer_q_2"][0]))
    put("sk", None, a["peer_subkeys_2"][0].reshape(16, NKEY, P).transpose(2, 0, 1).reshape(1, P, -1))
    pu = a["peer_u_2"][0].reshape(NKEY, NKEY, KC, P).transpose(1, 3, 2, 0).reshape(NKEY, P, -1)
    pv = a["peer_v_2"][0].reshape(NKEY, NKEY, D).transpose(1, 0, 2)
    for r in range(2):
        put(f"peer_u{r}", pu[r * I2:(r + 1) * I2])
        put(f"peer_v{r}", pv[r * I2:(r + 1) * I2])
    put("pg", units(a["w_ple_gate_2"][0]))
    put("pp", units(a["w_ple_proj_2"][0], 8))

    gb = np.zeros((2, P), f)
    for i, name in enumerate(("b_igate", "b_fgate")):
        for d in range(2):
            gb[i, 32 * d:32 * d + 4] = a[name][0, d]
    v = {"ada_b": a["ada_b"], "pln_g": a["post_ln_g"], "pln_b": a["post_ln_b"],
         "conv_q": a["conv_qk"][0][:, 0:m], "conv_k": a["conv_qk"][0][:, m:], "mh_g": a["mh_norm_g"],
         "pool_s": a["pool_scale"], "sgu_g": a["sgu_ln_g"], "sgu_b": a["sgu_ln_b"], "gate_b": gb,
         "attn_n": a["attn_norm_2"], "b_gate": a["b_gate_2"], "q_n": a["q_norm_2"], "kv_n": a["kv_norm_2"],
         "conv_w": a["conv_w_2"], "conv_b": a["conv_b_2"], "b_ra": a["b_rg_a_2"], "b_rx": a["b_rg_x_2"],
         "lam": a["lru_lambda_2"], "ffn_n": a["ffn_norm_2"], "ple_n": a["ple_norm_2"], "fin_n": a["final_norm_2"]}
    vecs = np.ascontiguousarray(np.concatenate([columns(np.ascontiguousarray(v[n])) for n, _ in VEC], 1))
    con, con2 = constants()
    cond = np.ascontiguousarray(np.stack([columns(a["c"][0]), columns(a["c_ctx"])], 2))
    return {"w": w, "vec": vecs, "con": con, "con2": con2, "cond": cond, "xT": feature_major(a["x"][0]),
            "ctxT": feature_major(a["ctx"][0]), "pT": feature_major(a["p_2"][0, 0])}


def kernel(**inputs):
    import concourse.bacc as bacc
    from concourse.bass_utils import run_bass_kernel_spmd

    arrays = layout({k: np.asarray(v) for k, v in inputs.items()})
    nc = bacc.Bacc("TRN2", target_bir_lowering=False, num_devices=1)
    aps = {k: nc.dram_tensor(f"in_{k}", v.shape, mybir.dt.from_np(v.dtype), kind="ExternalInput").ap()
           for k, v in arrays.items()}
    out = nc.dram_tensor("out_0", (P, KC, T), F32, kind="ExternalOutput").ap()
    program(nc, aps, out)
    r = run_bass_kernel_spmd(nc, [{f"in_{k}": v for k, v in arrays.items()}], core_ids=[0])
    y = r.results[0]["out_0"]
    return np.ascontiguousarray(y.transpose(2, 1, 0)).reshape(1, T, D)
```
